# Optimizing a Trainium2 kernel written in Bass

```python
import jax, jax.numpy as jnp
from jax import lax
import numpy as np

D_MODEL = 1024
BATCH = 1
SEQ = 128
DEPTH = 2
DEC_BATCH = 1
DEC_SEQ = 256
PAST_LEN = 128

GRID_W = 64
GROUP_W = D_MODEL // 4
HEAD_DIM = 64
MIX_W = 4 * GROUP_W
CONV_W = GROUP_W
MLA_HEADS = GROUP_W // HEAD_DIM
MLA_NOPE = HEAD_DIM
MLA_ROPE = HEAD_DIM // 2
MLA_V = HEAD_DIM
Q_LORA = D_MODEL // 4
KV_LORA = D_MODEL // 8
RET_HEADS = GROUP_W // HEAD_DIM
RET_DK = HEAD_DIM
RET_DV = HEAD_DIM
RET_CHUNK = 64
POOL_WINDOWS = (2, 4, 8, 16)
POOL_GROUPS = 4
POOL_CH = GROUP_W // POOL_GROUPS
PEER_HEADS = 8
PEER_N_KEYS = 128
PEER_EXPERTS = PEER_N_KEYS * PEER_N_KEYS
PEER_TOPK = 16
PEER_QDIM = 128
PEER_HALF = PEER_QDIM // 2
ROPE_BASE = 10000.0
AXIS_PAIRS = MLA_ROPE // 4
Q_BLOCK = 128
TOKEN_BLOCK = 128
EPS = 1e-6
OFF_MLA = 3 * CONV_W
OFF_RET = OFF_MLA + Q_LORA + KV_LORA + MLA_ROPE
OFF_POOL = OFF_RET + 4 * GROUP_W
IN_COLS = OFF_POOL + GROUP_W

kernel_name = 'hybrid_diffusion_prefix_step'

def rmsnorm(x, g):
    xf = x.astype(jnp.float32)
    y = xf * lax.rsqrt(jnp.mean(xf * xf, axis=-1, keepdims=True) + EPS)
    return (y * g.astype(jnp.float32)).astype(x.dtype)

def modulation(cvec, w, b):
    m = (jax.nn.silu(cvec) @ w + b)[..., None, :]
    return jnp.split(m, 6, axis=-1)

def rope_tables(L):
    rows = L // GRID_W
    row = jnp.repeat(jnp.arange(rows, dtype=jnp.float32), GRID_W)
    col = jnp.tile(jnp.arange(GRID_W, dtype=jnp.float32), rows)
    inv = ROPE_BASE ** (-jnp.arange(AXIS_PAIRS, dtype=jnp.float32) / AXIS_PAIRS)
    ang_r = row[:, None] * inv
    ang_c = col[:, None] * inv
    ang = jnp.concatenate([ang_r, ang_r, ang_c, ang_c], axis=-1)
    return jnp.cos(ang), jnp.sin(ang)

def axial_rotate(x, cos, sin):
    xa = x.reshape(x.shape[:-1] + (2, 2, AXIS_PAIRS))
    rot = jnp.stack([-xa[..., 1, :], xa[..., 0, :]], axis=-2).reshape(x.shape)
    return (x * cos + rot * sin).astype(x.dtype)

def short_conv(z, w):
    zp = jnp.pad(z, ((0, 0), (1, 1), (0, 0)))
    return zp[:, :-2] * w[0] + zp[:, 1:-1] * w[1] + zp[:, 2:] * w[2]

def multiscale_pool(z, w_pool, scale):
    B, L, C = z.shape
    zf = z.astype(jnp.float32)
    cs = jnp.pad(jnp.cumsum(zf, axis=1), ((0, 0), (1, 0), (0, 0))).reshape(B, L + 1, POOL_GROUPS, POOL_CH)
    t = jnp.arange(L)
    means = []
    for g, w in enumerate(POOL_WINDOWS):
        lo = jnp.clip(t - w // 2, 0, L)
        hi = jnp.clip(t + w // 2, 0, L)
        cg = cs[:, :, g]
        means.append((cg[:, hi] - cg[:, lo]) / (hi - lo).astype(jnp.float32)[None, :, None])
    pooled = jnp.stack(means, axis=2) - zf.reshape(B, L, POOL_GROUPS, POOL_CH)
    y = jnp.einsum('blgc,gcd->blgd', pooled.astype(z.dtype), w_pool).reshape(B, L, C)
    return y * scale

def mla_expand(ckv, w_uk, w_uv):
    k_nope = jnp.einsum('blr,rhd->blhd', ckv, w_uk)
    v = jnp.einsum('blr,rhd->blhd', ckv, w_uv)
    return k_nope, v

def mla_attend(q_nope, q_rope, k_nope, k_rope, v):
    B, Lq, H, N = q_nope.shape
    nblk = Lq // Q_BLOCK
    sm_scale = (MLA_NOPE + MLA_ROPE) ** -0.5

    def one_block(blk):
        qn, qr = blk
        s = jnp.einsum('bqhn,bkhn->bhqk', qn, k_nope) + jnp.einsum('bqhr,bkr->bhqk', qr, k_rope)
        p = jax.nn.softmax(s.astype(jnp.float32) * sm_scale, axis=-1)
        return jnp.einsum('bhqk,bkhv->bqhv', p.astype(v.dtype), v)

    qn_b = q_nope.reshape(B, nblk, Q_BLOCK, H, N).swapaxes(0, 1)
    qr_b = q_rope.reshape(B, nblk, Q_BLOCK, H, MLA_ROPE).swapaxes(0, 1)
    out = lax.map(one_block, (qn_b, qr_b))
    return out.swapaxes(0, 1).reshape(B, Lq, H * MLA_V)

def retention_chunks(q, k, v, log_gamma, s0):
    B, L, H, DK = q.shape
    DV = v.shape[-1]
    n = L // RET_CHUNK

    def chunked(a):
        return a.reshape(B, n, RET_CHUNK, H, a.shape[-1]).transpose(1, 0, 3, 2, 4)

    pos = jnp.arange(RET_CHUNK, dtype=jnp.float32)
    rel = pos[:, None] - pos[None, :]
    dmat = jnp.where(rel >= 0, jnp.exp(log_gamma[:, None, None] * jnp.maximum(rel, 0.0)), 0.0)
    dq = jnp.exp(log_gamma[:, None] * (pos + 1.0))[..., None]
    dk = jnp.exp(log_gamma[:, None] * (RET_CHUNK - 1.0 - pos))[..., None]
    dc = jnp.exp(log_gamma * RET_CHUNK)[:, None, None]

    def step(S, qkv):
        qi, ki, vi = qkv
        inner = jnp.einsum('bhqd,bhkd->bhqk', qi, ki) * dmat
        o = jnp.einsum('bhqk,bhkv->bhqv', inner, vi) + jnp.einsum('bhqd,bhdv->bhqv', qi, S) * dq
        S = S * dc + jnp.einsum('bhkd,bhkv->bhdv', ki * dk, vi)
        return S, o

    S, o = lax.scan(step, s0, (chunked(q), chunked(k), chunked(v)))
    return o.transpose(1, 0, 3, 2, 4).reshape(B, L, H, DV), S

def retention_bidir(q, k, v, lg_f, lg_b, s_f, s_b):
    flip = lambda a: jnp.flip(a, axis=1)
    o_f, S_f = retention_chunks(q, k, v, lg_f, s_f)
    o_b, S_b = retention_chunks(flip(q), flip(k), flip(v), lg_b, s_b)
    return o_f + flip(o_b), S_f, S_b

def head_groupnorm(o):
    mu = jnp.mean(o, axis=-1, keepdims=True)
    var = jnp.mean(jnp.square(o - mu), axis=-1, keepdims=True)
    return (o - mu) * lax.rsqrt(var + EPS)

def token_mix(h, P, l, ctx):
    B, L, _ = h.shape
    dt = h.dtype
    z = h @ P['w_in'][l]

    a_b, a_c, a_h = jnp.split(z[..., :OFF_MLA], 3, axis=-1)
    y_a = a_b * short_conv(a_c * a_h, P['conv_w'][l])

    zm = z[..., OFF_MLA:OFF_RET]
    q_lat = zm[..., :Q_LORA]
    ckv = rmsnorm(zm[..., Q_LORA:Q_LORA + KV_LORA], P['mla_kv_norm'][l])
    k_rope = zm[..., Q_LORA + KV_LORA:]
    q = jnp.einsum('blr,rhd->blhd', rmsnorm(q_lat, P['mla_q_norm'][l]), P['mla_w_uq'][l])
    q_nope, q_rope = q[..., :MLA_NOPE], q[..., MLA_NOPE:]
    k_nope, v = mla_expand(ckv, P['mla_w_uk'][l], P['mla_w_uv'][l])

    zr = z[..., OFF_RET:OFF_POOL].reshape(B, L, 4, RET_HEADS, RET_DK).astype(jnp.float32)
    rq, rk, rv, rg = zr[:, :, 0], zr[:, :, 1] * (RET_DK ** -0.5), zr[:, :, 2], zr[:, :, 3]
    lg = jax.nn.log_sigmoid(P['ret_decay_logit'][l].astype(jnp.float32))

    y_p = multiscale_pool(z[..., OFF_POOL:], P['pool_w'][l], P['pool_scale'][l])

    if ctx is None:
        y_m = mla_attend(q_nope, q_rope, k_nope, k_rope, v)
        zero = jnp.zeros((B, RET_HEADS, RET_DK, RET_DV), jnp.float32)
        o_r, S_f, S_b = retention_bidir(rq, rk, rv, lg[0], lg[1], zero, zero)
        new = (ckv, k_rope, jnp.stack([S_f, S_b], axis=1).astype(dt))
    else:
        ckv_c, krope_c, st_c = ctx
        cos, sin = rope_tables(L)
        q_rope = axial_rotate(q_rope, cos[:, None, :], sin[:, None, :])
        k_rope = axial_rotate(k_rope, cos, sin)
        kn_c, v_c = mla_expand(ckv_c, P['mla_w_uk'][l], P['mla_w_uv'][l])
        y_m = mla_attend(q_nope, q_rope,
                         jnp.concatenate([kn_c, k_nope], axis=1),
                         jnp.concatenate([krope_c, k_rope], axis=1),
                         jnp.concatenate([v_c, v], axis=1))
        st_c = st_c.astype(jnp.float32)
        o_r, _, _ = retention_bidir(rq, rk, rv, lg[0], lg[1], st_c[:, 0], st_c[:, 1])
        new = None
    y_r = (head_groupnorm(o_r) * jax.nn.silu(rg)).astype(dt).reshape(B, L, GROUP_W)

    y = jnp.concatenate([y_a, y_m.astype(dt), y_r, y_p], axis=-1)
    return y @ P['w_out'][l], new

def peer(h, w_q, subkeys, u_tab, v_tab):
    B, L, D = h.shape
    T = B * L
    xt = h.reshape(T, D)
    q = (xt @ w_q).reshape(T, PEER_HEADS, 2, PEER_HALF)
    s = jnp.einsum('thpd,hpnd->thpn', q, subkeys)
    s1, i1 = lax.top_k(s[:, :, 0], PEER_TOPK)
    s2, i2 = lax.top_k(s[:, :, 1], PEER_TOPK)
    cand = (s1[..., :, None] + s2[..., None, :]).reshape(T, PEER_HEADS, PEER_TOPK * PEER_TOPK)
    cidx = (i1[..., :, None] * PEER_N_KEYS + i2[..., None, :]).reshape(T, PEER_HEADS, PEER_TOPK * PEER_TOPK)
    top_s, sel = lax.top_k(cand, PEER_TOPK)
    eidx = jnp.take_along_axis(cidx, sel, axis=-1)
    gates = jax.nn.softmax(top_s.astype(jnp.float32), axis=-1)
    nb = T // TOKEN_BLOCK

    def block(args):
        xb, eb, gb = args
        a = jnp.einsum('td,thkd->thk', xb, u_tab[eb])
        coef = gb.astype(xb.dtype) * jax.nn.gelu(a)
        return jnp.einsum('thk,thkd->td', coef, v_tab[eb])

    y = lax.map(block, (xt.reshape(nb, TOKEN_BLOCK, D),
                        eidx.reshape(nb, TOKEN_BLOCK, PEER_HEADS, PEER_TOPK),
                        gates.reshape(nb, TOKEN_BLOCK, PEER_HEADS, PEER_TOPK)))
    return y.reshape(B, L, D)

def trunk_layer(x, mods, P, l, ctx):
    sh1, sc1, g1, sh2, sc2, g2 = mods
    h = rmsnorm(x, P['norm1'][l]) * (1 + sc1) + sh1
    mix, new = token_mix(h, P, l, ctx)
    x = x + g1 * mix
    h = rmsnorm(x, P['norm2'][l]) * (1 + sc2) + sh2
    x = x + g2 * peer(h, P['peer_w_q'][l], P['peer_subkeys'][l], P['peer_u'][l], P['peer_v'][l])
    return x, new

def setup_inputs(seed: int = 0) -> dict:
    key = jax.random.key(seed)
    keys = iter(jax.random.split(key, 40))
    f32 = jnp.float32

    def nrm(shape, scale):
        return jax.random.normal(next(keys), shape, f32) * scale

    gamma = 1.0 - 2.0 ** (-5.0 - jnp.arange(RET_HEADS, dtype=f32))
    base_logit = jnp.log(gamma) - jnp.log1p(-gamma)
    return {
        'x_prompt': nrm((BATCH, SEQ, D_MODEL), 1.0),
        'x_sample': nrm((DEC_BATCH, DEC_SEQ, D_MODEL), 1.0),
        'cache_mla_ckv': nrm((DEC_BATCH, DEPTH, PAST_LEN, KV_LORA), 1.0),
        'cache_mla_krope': nrm((DEC_BATCH, DEPTH, PAST_LEN, MLA_ROPE), 1.0),
        'state_ret': nrm((DEC_BATCH, DEPTH, 2, RET_HEADS, RET_DK, RET_DV), 0.5),
        'c': nrm((DEC_BATCH, D_MODEL), 1.0),
        'c_ctx': nrm((D_MODEL,), 1.0),
        'w_mod': nrm((DEPTH, D_MODEL, 6 * D_MODEL), 0.5 * D_MODEL ** -0.5),
        'b_mod': nrm((DEPTH, 6 * D_MODEL), 0.02),
        'norm1': 1.0 + nrm((DEPTH, D_MODEL), 0.1),
        'norm2': 1.0 + nrm((DEPTH, D_MODEL), 0.1),
        'w_in': nrm((DEPTH, D_MODEL, IN_COLS), D_MODEL ** -0.5),
        'conv_w': nrm((DEPTH, 3, CONV_W), 3 ** -0.5),
        'mla_q_norm': 1.0 + nrm((DEPTH, Q_LORA), 0.1),
        'mla_w_uq': nrm((DEPTH, Q_LORA, MLA_HEADS, MLA_NOPE + MLA_ROPE), Q_LORA ** -0.5),
        'mla_kv_norm': 1.0 + nrm((DEPTH, KV_LORA), 0.1),
        'mla_w_uk': nrm((DEPTH, KV_LORA, MLA_HEADS, MLA_NOPE), KV_LORA ** -0.5),
        'mla_w_uv': nrm((DEPTH, KV_LORA, MLA_HEADS, MLA_V), KV_LORA ** -0.5),
        'ret_decay_logit': base_logit + nrm((DEPTH, 2, RET_HEADS), 0.1),
        'pool_w': nrm((DEPTH, POOL_GROUPS, POOL_CH, POOL_CH), POOL_CH ** -0.5),
        'pool_scale': 1.0 + nrm((DEPTH, GROUP_W), 0.1),
        'w_out': nrm((DEPTH, MIX_W, D_MODEL), MIX_W ** -0.5),
        'peer_w_q': nrm((DEPTH, D_MODEL, PEER_HEADS * PEER_QDIM), D_MODEL ** -0.5),
        'peer_subkeys': nrm((DEPTH, PEER_HEADS, 2, PEER_N_KEYS, PEER_HALF), PEER_HALF ** -0.5),
        'peer_u': nrm((DEPTH, PEER_EXPERTS, D_MODEL), D_MODEL ** -0.5),
        'peer_v': nrm((DEPTH, PEER_EXPERTS, D_MODEL), PEER_HEADS ** -0.5),
        'norm_f': 1.0 + nrm((D_MODEL,), 0.1),
    }

def reference(x_prompt, x_sample, cache_mla_ckv, cache_mla_krope, state_ret, c, c_ctx,
              w_mod, b_mod, norm1, norm2, w_in, conv_w, mla_q_norm, mla_w_uq, mla_kv_norm,
              mla_w_uk, mla_w_uv, ret_decay_logit, pool_w, pool_scale, w_out, peer_w_q,
              peer_subkeys, peer_u, peer_v, norm_f):
    P = dict(norm1=norm1, norm2=norm2, w_in=w_in, conv_w=conv_w, mla_q_norm=mla_q_norm,
             mla_w_uq=mla_w_uq, mla_kv_norm=mla_kv_norm, mla_w_uk=mla_w_uk, mla_w_uv=mla_w_uv,
             ret_decay_logit=ret_decay_logit, pool_w=pool_w, pool_scale=pool_scale, w_out=w_out,
             peer_w_q=peer_w_q, peer_subkeys=peer_subkeys, peer_u=peer_u, peer_v=peer_v)

    xp = x_prompt
    ckv_list, krope_list, ret_list = [], [], []
    for l in range(DEPTH):
        mods = modulation(c_ctx, w_mod[l], b_mod[l])
        xp, (ckv_l, krope_l, ret_l) = trunk_layer(xp, mods, P, l, None)
        ckv_list.append(ckv_l)
        krope_list.append(krope_l)
        ret_list.append(ret_l)
    y_prompt = rmsnorm(xp, norm_f)
    new_mla_ckv = jnp.stack(ckv_list, axis=1)
    new_mla_krope = jnp.stack(krope_list, axis=1)
    new_state_ret = jnp.stack(ret_list, axis=1)

    xs = x_sample
    for l in range(DEPTH):
        mods = modulation(c, w_mod[l], b_mod[l])
        ctx = (cache_mla_ckv[:, l], cache_mla_krope[:, l], state_ret[:, l])
        xs, _ = trunk_layer(xs, mods, P, l, ctx)
    y_sample = rmsnorm(xs, norm_f)

    return (y_prompt, y_sample, new_mla_ckv, new_mla_krope, new_state_ret)


_drawn_inputs = setup_inputs


def setup_inputs(seed=0):
    import zlib

    import numpy as np

    out = dict(_drawn_inputs(seed))
    spreads = {}
    factors = {'cache_mla_ckv': 4.145, 'cache_mla_krope': 6.29, 'mla_q_norm': 8.0}
    for name, (base, spread) in spreads.items():
        noise = np.random.default_rng([zlib.crc32(name.encode()), seed]).standard_normal(out[name].shape)
        drawn = base * np.exp(spread * noise) if base else spread * noise
        out[name] = __import__('jax').numpy.asarray(drawn.astype(out[name].dtype))
    for name, factor in factors.items():
        out[name] = (out[name] * factor).astype(out[name].dtype)
    return out
```

```python
from contextlib import ExitStack

import numpy as np

import concourse.bass as bass
from concourse import mybir

F32 = mybir.dt.float32
U32 = mybir.dt.uint32
ALU = mybir.AluOpType
ACT = mybir.ActivationFunctionType
AX = mybir.AxisListType.X

P = 128
D = 1024
DC = D // P
DEPTH = 2
SEQ = 128
DEC = 256
PAST = 128
GROUP_W = D // 4
HD = 64
HEADS = GROUP_W // HD
ROPE = HD // 2
QK = HD + ROPE
Q_LORA = D // 4
KV_LORA = D // 8
GRID_W = 64
WINDOWS = (2, 4, 8, 16)
EPS = 1e-6
SM_SCALE = float(QK) ** -0.5
K_SCALE = float(HD) ** -0.5
OFF_MLA = 3 * GROUP_W
OFF_RET = OFF_MLA + Q_LORA + KV_LORA + ROPE
OFF_POOL = OFF_RET + 4 * GROUP_W
LAT = Q_LORA + KV_LORA + ROPE
PEER_H = 8
N_KEYS = 128
EXPERTS = N_KEYS * N_KEYS
TOPK = 16
PICKS = PEER_H * TOPK
LOWEST = -3.0e38

G = 4
SLOTS = G
NG = PICKS // G
DIAGS = 4

TILES = [[0], [1, 2], [3], [4, 5]]
STREAM = [0, 1, 0, 1]
LAYER = [0, 0, 1, 1]
M_OF = [0, 1, 1, 2, 3, 3]
XBUF = [0, 1, 2, 0, 1, 2]

SH1, SC1, G1, SH2, SC2, G2 = range(6)


def mix_stages(m):
    return ([("ln", 1, t) for t in TILES[m]] + [("in", m), ("mla", m), ("conv", m), ("ret", m), ("pool", m), ("out", m)]
            + [("ln", 2, t) for t in TILES[m]] + [("q", m)])


SCHEDULE = [("start", 0), ("mods", 0), ("keys", 0), ("decay", 0)]
SCHEDULE += mix_stages(0) + [("score", 0), ("topk", 0), ("peer", 0)]
SCHEDULE += mix_stages(1) + [("score", 1), ("topk", 1), ("peer", 1), ("score", 2), ("topk", 2), ("peer", 2)]
SCHEDULE += [("mods", 1), ("keys", 1), ("decay", 1)]
SCHEDULE += mix_stages(2) + [("score", 3), ("topk", 3), ("peer", 3)]
SCHEDULE += mix_stages(3) + [("score", 4), ("topk", 4), ("peer", 4), ("score", 5), ("topk", 5), ("peer", 5)]


def nk_of(m):
    return 1 if STREAM[m] == 0 else 3


def banks_used(stage):
    kind, *a = stage
    if kind == "start":
        yield ("vec",)
    elif kind == "mods":
        yield ("modrow", a[0], 0)
        for j in range(12):
            if j + 1 < 12:
                yield ("modrow", a[0], j + 1)
            yield ("modcol", a[0], j)
    elif kind == "keys":
        yield from (("sk", a[0], b) for b in range(2))
    elif kind == "ln":
        yield from (("xnT", a[0], a[1], b) for b in range(2))
        if a[0] == 2:
            yield from (("h2tok", a[1], b) for b in range(2))
    elif kind == "in":
        m = a[0]
        yield from (("zm", t) for t in TILES[m])
        yield from (("a", m, f) for f in range(6))
        yield from (("zp", t) for t in TILES[m])
        yield from (("rqk", m, f) for f in range(4))
        if STREAM[m] == 0:
            yield ("rk", m)
        yield from (("rvg", t) for t in TILES[m])
    elif kind == "mla":
        m = a[0]
        if STREAM[m] == 1:
            yield ("ctxT", m)
        for t in TILES[m]:
            yield ("latT", t)
            yield ("q", t)
            yield ("qT", t)
        yield from (("kT", m, h) for h in range(HEADS))
        yield from (("v", m, k) for k in range(nk_of(m)))
        for t in TILES[m]:
            yield from (("sc", t, h) for h in range(HEADS))
            for h in range(HEADS):
                yield ("pT", t, h)
                if h % 2:
                    yield ("o", t, h // 2)
    elif kind == "ret":
        m = a[0]
        nt = len(TILES[m])
        yield from (("inn", m, 0, i) for i in range(nt))
        for h in range(HEADS):
            if h + 1 < HEADS:
                yield from (("inn", m, h + 1, i) for i in range(nt))
            yield ("oh", m, h)
        if STREAM[m] == 0:
            yield ("st", m)
        yield from (("yrT", t) for t in TILES[m])
    elif kind == "pool":
        yield from (("pl", a[0], b) for b in range(2))
        yield from (("plo", a[0], b) for b in range(2))
    elif kind == "out":
        yield from (("gate", 1, a[0], b) for b in range(2))
        yield from (("mix", t, b) for b in range(2) for t in TILES[a[0]])
    elif kind == "q":
        yield from (("qp", a[0], h) for h in range(PEER_H))
    elif kind == "score":
        yield from (("s", a[0], b) for b in range(4))
    elif kind == "peer":
        yield from (("gate", 2, a[0], b) for b in range(2))


def weight_blocks(stage):
    kind, *a = stage
    if kind == "mods":
        for j in range(12):
            yield ("w_mod", a[0], [(512 * j, 512)], ("modrow", a[0], j))
    elif kind == "in":
        m = a[0]
        last = TILES[m][-1]
        yield ("w_in", LAYER[m], [(OFF_MLA, LAT)], ("zm", last))
        yield ("w_in", LAYER[m], [(0, 512)], ("a", m, 3))
        yield ("w_in", LAYER[m], [(512, GROUP_W), (OFF_POOL, GROUP_W)], ("zp", last))
        yield ("w_in", LAYER[m], [(OFF_RET, 512)], ("rk", m) if STREAM[m] == 0 else ("rqk", m, 3))
        yield ("w_in", LAYER[m], [(OFF_RET + 512, 512)], ("rvg", last))
    elif kind == "out":
        for b in range(2):
            yield ("w_out", LAYER[a[0]], [(512 * b, 512)], ("mix", TILES[a[0]][-1], b))
    elif kind == "q":
        for b in range(2):
            yield ("peer_w_q", LAYER[a[0]], [(512 * b, 512)], ("qp", a[0], 4 * b + 3))


def announced(stage):
    kind, *a = stage
    if kind == "start":
        yield from [("cond", 0), ("abs_logit", 0), ("log1p", 0), ("decay_log", 0)]
    elif kind == "mods":
        yield from (("mrow", (a[0], j)) for j in range(12))
        yield from (("modcol", (a[0], j)) for j in range(12))
        yield ("mods", a[0])
    elif kind == "keys":
        yield ("sk", a[0])
    elif kind == "decay":
        yield from (("decay_arg", (a[0], h)) for h in range(HEADS))
        yield from (("decay_exp", (a[0], h)) for h in range(HEADS))
        yield from (("decay_col", (a[0], i)) for i in range(2 * HEADS))
    elif kind == "ln":
        yield ("sumsq", ("ln", *a))
        yield ("std", ("ln", *a))
        yield ("xn", tuple(a))
        yield ("hT", tuple(a))
        if a[0] == 2:
            yield from (("h2", (a[1], b)) for b in range(2))
    elif kind == "in":
        m = a[0]
        yield ("za", m)
        yield ("rqk", m)
        for t in TILES[m]:
            yield ("zp", t)
            yield ("rvg", t)
    elif kind == "mla":
        m = a[0]
        if STREAM[m] == 1:
            yield ("ctxT", m)
        for t in TILES[m]:
            yield ("sumsq", ("mla", t))
            yield ("std", ("mla", t))
            yield ("lat", t)
            yield ("latT", t)
            yield ("qtok", t)
            yield ("qT", t)
            yield ("row_max", t)
            yield ("probs", t)
            yield from (("pT", (t, h)) for h in range(HEADS))
            yield from (("y_mla", (t, p)) for p in range(2))
        yield from (("kT", (m, h)) for h in range(HEADS))
        yield from (("v", (m, k)) for k in range(nk_of(m)))
    elif kind == "conv":
        yield ("y_conv", a[0])
    elif kind == "ret":
        m = a[0]
        if STREAM[m] == 0:
            yield ("k_decayed", m)
            yield ("state", m)
        for t in TILES[m]:
            yield ("sumsq", ("ret", t))
            yield ("std", ("ret", t))
            yield ("ret_out", t)
            yield ("y_ret", t)
    elif kind == "pool":
        for p in range(2):
            yield ("pooled", (a[0], p))
            yield ("y_pool", (a[0], p))
    elif kind == "out":
        yield from (("gate", (1, a[0], b)) for b in range(2))
        yield from (("mixed", t) for t in TILES[a[0]])
    elif kind == "q":
        yield from (("qp", (a[0], h)) for h in range(PEER_H))
    elif kind == "score":
        yield from (("scores", (a[0], b)) for b in range(4))
    elif kind == "topk":
        yield from [("gate_arg", a[0]), ("gate_exp", a[0]), ("picked", a[0])]
    elif kind == "peer":
        yield from (("gate", (2, a[0], b)) for b in range(2))
        yield ("updated", a[0])
        if a[0] >= 3:
            yield ("sumsq", ("final", a[0]))
            yield ("std", ("final", a[0]))
            yield ("final", a[0])


def plan():
    ring = 6
    bank, blocks, value, total = {}, [], {}, {}
    n = 0
    for stage in SCHEDULE:
        for key in banks_used(stage):
            bank[key] = (n % ring, n // ring)
            n += 1
        blocks += list(weight_blocks(stage))
        for name, key in announced(stage):
            total[name] = total.get(name, 0) + 1
            value[name, key] = total[name]
    return ring, bank, blocks, value, total


def hybrid_step(nc, a, c, outs):
    y_prompt, y_sample, new_ckv, new_krope, new_state = outs
    RING, BANK, BLOCKS, VALUE, TOTAL = plan()
    WSLOTS = 2
    block_at = {}
    for n, (what, layer, cols, last) in enumerate(BLOCKS):
        block_at[what, layer, last] = n
    landed_at, per_slot = [], [0] * WSLOTS
    for n, (_, _, cols, _) in enumerate(BLOCKS):
        per_slot[n % WSLOTS] += 16 * len(cols)
        landed_at.append(per_slot[n % WSLOTS])

    with ExitStack() as ctx:
        def sb(name, shape, dt=F32):
            return ctx.enter_context(nc.sbuf_tensor(name, shape, dt))

        def sem(name):
            return ctx.enter_context(nc.semaphore(name))

        ident = sb("ident", [P, P])
        iota16 = sb("iota16", [P, TOPK])
        rel = sb("rel", [P, 2, 3 * P])
        pos3 = sb("pos3", [P, 2, 3])
        cs = sb("cs", [P, 2, 2, ROPE])
        band = sb("band", [P, 3, 4, P])
        edge = sb("edge", [P, 2, 4, 8])
        VC = 68
        cols = sb("cols", [P, VC + 96])
        cond = sb("cond", [P, 2, DC])
        logit = sb("logit", [P, 4, 16])
        kvn = sb("kvn", [P, KV_LORA])
        w_uq = sb("w_uq", [P, 2, HEADS * QK])
        w_ukv = sb("w_ukv", [P, 2, GROUP_W])
        w_pool = sb("w_pool", [P, 2, HD])
        s0 = sb("s0", [P, 2, 2 * HD])
        ctx_ckv = sb("ctx_ckv", [P, KV_LORA])
        ctx_kr = sb("ctx_kr", [P, ROPE])
        normf = sb("normf", [P, D])
        skT = sb("skT", [P, PEER_H, N_KEYS])
        modc = sb("modc", [P, DEPTH, 48, 2])
        moda = sb("moda", [P, DEPTH, 2, 2, DC])
        decay = sb("decay", [P, HEADS, 3 * P])
        dcol = sb("dcol", [P, 2, HEADS, 3])
        x = sb("x", [P, 3, D])
        h2 = sb("h2", [P, 3, D])
        hT = sb("hT", [P, DC, DEC])
        yT = hT
        xn = sb("xn", [P, D])
        gate_row = sb("gate_row", [P, D])
        wring = sb("wring", [P, WSLOTS, DC, 512])
        mrow = sb("mrow", [2, 2, 512])
        za = sb("za", [P, 6, DEC])
        rqk = sb("rqk", [P, 4, DEC])
        zm = sb("zm", [P, 2, LAT])
        zp = sb("zp", [P, 2, GROUP_W])
        rv = sb("rv", [P, 2, 2, GROUP_W])
        scratch = sb("scratch", [P, 6144])
        at = [0]

        def part(n):
            at[0] += n
            return scratch[:, at[0] - n:at[0]]

        lat = part(2 * 384).rearrange("p (i n) -> p i n", i=2)
        q_tok = part(384)
        qlT = part(512).rearrange("p (k n) -> p k n", k=2)
        ckvT = part(384)
        qT = part(1024).rearrange("p (h n) -> p h n", h=4)
        kT = part(4 * 384).rearrange("p (h n) -> p h n", h=4)
        vtok = part(768).rearrange("p (k n) -> p k n", k=3)
        pooled = part(512).rearrange("p (b n) -> p b n", b=2)
        rk = part(256)
        assert at[0] <= 6144, at[0]
        at[0] = 0
        s_sb = part(2048)
        cand = part(2048)
        tv = part(256).rearrange("p (n k) -> p n k", k=TOPK)
        ti = part(256).bitcast(U32).rearrange("p (n k) -> p n k", k=TOPK)
        tif = part(256).rearrange("p (n k) -> p n k", k=TOPK)
        cv = part(128).rearrange("p (n k) -> p n k", k=TOPK)
        sel = part(128).bitcast(U32).rearrange("p (n k) -> p n k", k=TOPK)
        sel2 = part(256).bitcast(U32).rearrange("p (q n) -> p q n", q=2)
        self_ = part(256).rearrange("p (q n) -> p q n", q=2)
        e12 = part(256).rearrange("p (q n) -> p q n", q=2)
        assert at[0] <= 6144, at[0]
        vec_rows = scratch[0:96, 0:2 * P].rearrange("p (r n) -> p r n", r=2)
        qpT = sb("qpT", [P, PEER_H, DEC])
        shared = qpT[:, :, :].rearrange("p h n -> p (h n)")
        probs = shared[:, 0:4 * 384].rearrange("p (h n) -> p h n", h=4)
        pT = sb("pT", [P, 2, 384])
        krr = sb("krr", [P, 2, ROPE])
        stat = sb("stat", [P, 64])
        inn = sb("inn", [P, 2, 2, DEC])
        o_tok = sb("o_tok", [P, 2, GROUP_W])
        state_out = inn[0:HD, 0, :, :].rearrange("p i n -> p (i n)")
        eidx = sb("eidx", [P, 2, PICKS], U32)
        gates = sb("gates", [P, 2, PICKS])
        ubuf = sb("ubuf", [P, SLOTS, D])
        vbuf = sb("vbuf", [P, SLOTS, D])
        uidx = sb("uidx", [P, 2, G], U32)
        vidx = sb("vidx", [P, 2, G], U32)
        dot = sb("dot", [P, G])
        act_dot = sb("act_dot", [P, G])
        coef = sb("coef", [P, G])
        diag = sb("diag", [P, DIAGS, P])

        psum = [ctx.enter_context(nc.psum_tensor(f"bank{i}", [P, 512], F32)) for i in range(RING)]
        ysum = ctx.enter_context(nc.psum_tensor("ysum", [P, 2, 512], F32))

        bank_filled = [sem(f"bank_filled{i}") for i in range(RING)]
        bank_free = [sem(f"bank_free{i}") for i in range(RING)]
        cond_ready = sem("cond_ready")
        abs_logit_ready = sem("abs_logit_ready")
        log1p_ready = sem("log1p_ready")
        decay_log_ready = sem("decay_log_ready")
        mrow_ready = sem("mrow_ready")
        modcol_ready = sem("modcol_ready")
        mods_ready = sem("mods_ready")
        sk_ready = sem("sk_ready")
        decay_arg_ready = sem("decay_arg_ready")
        decay_exp_ready = sem("decay_exp_ready")
        decay_col_ready = sem("decay_col_ready")
        sumsq_ready = sem("sumsq_ready")
        std_ready = sem("std_ready")
        xn_ready = sem("xn_ready")
        hT_ready = sem("hT_ready")
        za_ready = sem("za_ready")
        rqk_ready = sem("rqk_ready")
        zp_ready = sem("zp_ready")
        rvg_ready = sem("rvg_ready")
        lat_ready = sem("lat_ready")
        latT_ready = sem("latT_ready")
        qtok_ready = sem("qtok_ready")
        qT_ready = sem("qT_ready")
        row_max_ready = sem("row_max_ready")
        probs_ready = sem("probs_ready")
        pT_ready = sem("pT_ready")
        y_mla_ready = sem("y_mla_ready")
        kT_ready = sem("kT_ready")
        v_ready = sem("v_ready")
        y_conv_ready = sem("y_conv_ready")
        k_decayed_ready = sem("k_decayed_ready")
        state_ready = sem("state_ready")
        ret_out_ready = sem("ret_out_ready")
        y_ret_ready = sem("y_ret_ready")
        pooled_ready = sem("pooled_ready")
        y_pool_ready = sem("y_pool_ready")
        gate_ready = sem("gate_ready")
        mixed_ready = sem("mixed_ready")
        h2_ready = sem("h2_ready")
        qp_ready = sem("qp_ready")
        scores_ready = sem("scores_ready")
        gate_arg_ready = sem("gate_arg_ready")
        gate_exp_ready = sem("gate_exp_ready")
        picked_ready = sem("picked_ready")
        updated_ready = sem("updated_ready")
        ctxT_ready = sem("ctxT_ready")
        final_ready = sem("final_ready")
        w_landed = [sem(f"w_landed{i}") for i in range(WSLOTS)]
        small_landed = sem("small_landed")
        x_landed = sem("x_landed")
        rows_landed = sem("rows_landed")
        keys_landed = sem("keys_landed")
        layer_landed = sem("layer_landed")
        cache_stored = sem("cache_stored")
        state_stored = sem("state_stored")
        y_stored = sem("y_stored")
        dve_done = sem("dve_done")
        act_done = sem("act_done")
        idx_staged = sem("idx_staged")
        pool_order = sem("pool_order")
        u_landed = [sem(f"u_landed{i}") for i in range(SLOTS)]
        v_landed = [sem(f"v_landed{i}") for i in range(SLOTS)]
        u_free = sem("u_free")
        v_free = sem("v_free")
        gelu_done = sem("gelu_done")
        coef_done = sem("coef_done")
        diag_built = sem("diag_built")

        kr_dram = a["cache_mla_krope"]
        u_rows = a["peer_u"].rearrange("l e d -> (l e) d")
        v_rows = a["peer_v"].rearrange("l e d -> (l e) d")

        def slot(*key):
            return BANK[key][0]

        def use(*key):
            return BANK[key][1] + 1

        def nth(name, key):
            return VALUE[name, key]

        def tok(m, t):
            i = TILES[m].index(t)
            return i, slice(P * i, P * i + P)

        SMALL = []
        SMALL.append((ident[:, :], c["ident"]))
        SMALL.append((iota16[:, :], c["iota16"].partition_broadcast(P)))
        SMALL.append((rel[:, :, :], c["rel"]))
        SMALL.append((pos3[:, :, :], c["pos3"]))
        SMALL.append((cs[:, :, :, :], c["rope"]))
        SMALL.append((band[:, :, :, :], c["band"]))
        SMALL.append((edge[:, :, :, :], c["edge"]))
        SMALL.append((logit[:, 0, :], a["ret_decay_logit"].rearrange("l r h -> (l r h)").partition_broadcast(P)))
        SMALL.append((normf[:, :], a["norm_f"].partition_broadcast(P)))
        N_SMALL = len(SMALL)

        def layer_loads(l):
            loads = [(kvn[:, :], a["mla_kv_norm"][l].partition_broadcast(P)),
                     (w_uq[:, :, :], a["mla_w_uq"][l].rearrange("(k p) h d -> p k (h d)", p=P)),
                     (w_ukv[:, 0, :], a["mla_w_uk"][l].rearrange("r h d -> r (h d)")),
                     (w_ukv[:, 1, :], a["mla_w_uv"][l].rearrange("r h d -> r (h d)")),
                     (ctx_ckv[:, :], a["cache_mla_ckv"][0, l]), (ctx_kr[:, :], kr_dram[0, l])]
            for g in range(2):
                half = slice(HD * g, HD * g + HD)
                loads.append((w_pool[half, :, :], a["pool_w"][l, g:4:2].rearrange("q i o -> i q o")))
                for r in range(2):
                    loads.append((s0[half, :, HD * r:HD * r + HD], a["state_ret"][0, l, r, g:4:2].rearrange("q k v -> k q v")))
            return loads

        N_LAYER = len(layer_loads(0))
        ROWS = [(0, 8, a["c_ctx"].rearrange("(k p) -> k p", p=P)), (8, 8, a["c"][0].rearrange("(k p) -> k p", p=P)),
                (16, 16, a["norm1"].rearrange("l (k p) -> (l k) p", p=P)),
                (32, 16, a["norm2"].rearrange("l (k p) -> (l k) p", p=P)),
                (48, 4, a["mla_q_norm"].rearrange("l (k p) -> (l k) p", p=P)),
                (52, 12, a["conv_w"].rearrange("l t (k p) -> (l t k) p", p=P)),
                (64, 4, a["pool_scale"].rearrange("l (k p) -> (l k) p", p=P))]
        NORM = {1: 16, 2: 32}
        QNORM, CONVW, POOLS, BMOD = 48, 52, 64, VC

        block = ctx.enter_context(nc.Block())

        @block.sync
        def _(sp):
            for r0, n, src in ROWS:
                sp.dma_start(vec_rows[r0:r0 + n, 0, :], src).then_inc(rows_landed, 16)
            sp.dma_start(vec_rows[0:96, 1, :], a["b_mod"].rearrange("l (k p) -> (l k) p", p=P)).then_inc(rows_landed, 16)

            def weight(n):
                what, layer, cc, last = BLOCKS[n]
                if n >= WSLOTS:
                    sp.wait_ge(bank_filled[slot(*BLOCKS[n - WSLOTS][3])], use(*BLOCKS[n - WSLOTS][3]))
                off = 0
                for c0, w in cc:
                    sp.dma_start(wring[:, n % WSLOTS, :, off:off + w],
                                 a[what][layer].rearrange("(k p) n -> p k n", p=P)[:, :, c0:c0 + w])\
                      .then_inc(w_landed[n % WSLOTS], 16)
                    off += w

            for dst, src in SMALL[:1]:
                sp.dma_start(dst, src).then_inc(small_landed, 16)
            for n in range(WSLOTS):
                weight(n)
            for dst, src in SMALL[1:]:
                sp.dma_start(dst, src).then_inc(small_landed, 16)
            sp.dma_start(x[:, 0, :], a["x_prompt"][0]).then_inc(x_landed, 16)
            for i in range(2):
                sp.dma_start(x[:, 1 + i, :], a["x_sample"][0, P * i:P * i + P, :]).then_inc(x_landed, 16)
            n = WSLOTS
            for stage in SCHEDULE:
                if stage[0] == "keys":
                    l = stage[1]
                    if l:
                        sp.wait_ge(picked_ready, nth("picked", 2))
                        sp.wait_ge(mixed_ready, nth("mixed", TILES[1][-1]))
                    for dst, src in layer_loads(l):
                        sp.dma_start(dst, src).then_inc(layer_landed, 16)
                    sp.dma_start(cand[:, 0:1024].rearrange("n (h d) -> n h d", h=2 * PEER_H),
                                 a["peer_subkeys"][l].rearrange("h q n d -> n (h q) d")).then_inc(keys_landed, 16)
                for b in weight_blocks(stage):
                    k = block_at[b[0], b[1], b[3]]
                    if k >= n:
                        weight(k)
                        n = k + 1

        @block.tensor
        def _(pe):
            def weights(what, layer, last):
                n = block_at[what, layer, last]
                pe.wait_ge(w_landed[n % WSLOTS], landed_at[n])
                return wring[:, n % WSLOTS, :, :]

            def start(_):
                pe.wait_ge(rows_landed, 16 * (len(ROWS) + 1))
                pe.wait_ge(small_landed, 16 * N_SMALL)
                pe.wait_ge(bank_free[slot("vec")], use("vec"))
                ps = psum[slot("vec")]
                pe.transpose(ps[:, 0:VC], vec_rows[0:VC, 0, :], ident[0:VC, 0:VC])
                pe.transpose(ps[:, VC:VC + 96], vec_rows[0:96, 1, :], ident[0:96, 0:96]).then_inc(bank_filled[slot("vec")], 1)
                pe.wait_ge(cond_ready, nth("cond", 0))

            def mods(l):
                def row(j):
                    key = ("modrow", l, j)
                    w = weights("w_mod", l, key)
                    pe.wait_ge(bank_free[slot(*key)], use(*key))
                    ps = psum[slot(*key)]
                    for k in range(DC):
                        mm = pe.matmul(ps[0:2, :], cond[:, :, k], w[:, k, :], start=(k == 0), stop=(k == DC - 1))
                    mm.then_inc(bank_filled[slot(*key)], 1)

                row(0)
                for j in range(12):
                    if j + 1 < 12:
                        row(j + 1)
                    key = ("modcol", l, j)
                    pe.wait_ge(mrow_ready, nth("mrow", (l, j)))
                    pe.wait_ge(bank_free[slot(*key)], use(*key))
                    ps = psum[slot(*key)]
                    for i in range(4):
                        mm = pe.transpose(ps[:, 2 * i:2 * i + 2], mrow[0:2, j % 2, P * i:P * i + P], ident[0:2, 0:2])
                    mm.then_inc(bank_filled[slot(*key)], 1)

            def keys(l):
                pe.wait_ge(layer_landed, 16 * N_LAYER * (l + 1))
                pe.wait_ge(keys_landed, 16 * (l + 1))
                for b in range(2):
                    pe.wait_ge(bank_free[slot("sk", l, b)], use("sk", l, b))
                    ps = psum[slot("sk", l, b)]
                    for i in range(4):
                        h = 4 * b + i
                        mm = pe.transpose(ps[:, P * i:P * i + P], cand[:, P * h:P * h + P], ident[:, :])
                    mm.then_inc(bank_filled[slot("sk", l, b)], 1)

            def ln(which, t):
                i, cc = tok(M_OF[t], t)
                pe.wait_ge(xn_ready, nth("xn", (which, t)))
                for b in range(2):
                    key = ("xnT", which, t, b)
                    pe.wait_ge(bank_free[slot(*key)], use(*key))
                    ps = psum[slot(*key)]
                    for k in range(4):
                        mm = pe.transpose(ps[:, P * k:P * k + P], xn[:, P * (4 * b + k):P * (4 * b + k) + P], ident[:, :])
                    mm.then_inc(bank_filled[slot(*key)], 1)
                if which == 2:
                    pe.wait_ge(hT_ready, nth("hT", (which, t)))
                    for b in range(2):
                        key = ("h2tok", t, b)
                        pe.wait_ge(bank_free[slot(*key)], use(*key))
                        ps = psum[slot(*key)]
                        for k in range(4):
                            mm = pe.transpose(ps[:, P * k:P * k + P], hT[:, 4 * b + k, cc], ident[:, :])
                        mm.then_inc(bank_filled[slot(*key)], 1)

            def project(m):
                T = P * len(TILES[m])
                l = LAYER[m]
                last = TILES[m][-1]

                def by_token(key, t, w, c0, n):
                    _, cc = tok(m, t)
                    pe.wait_ge(bank_free[slot(*key)], use(*key))
                    ps = psum[slot(*key)]
                    for k in range(DC):
                        mm = pe.matmul(ps[:, 0:n], hT[:, k, cc], w[:, k, c0:c0 + n], start=(k == 0), stop=(k == DC - 1))
                    mm.then_inc(bank_filled[slot(*key)], 1)

                def by_feature(key, w, c0):
                    pe.wait_ge(bank_free[slot(*key)], use(*key))
                    ps = psum[slot(*key)]
                    for k in range(DC):
                        mm = pe.matmul(ps[:, 0:T], w[:, k, c0:c0 + P], hT[:, k, 0:T], start=(k == 0), stop=(k == DC - 1))
                    mm.then_inc(bank_filled[slot(*key)], 1)

                for t in TILES[m]:
                    pe.wait_ge(hT_ready, nth("hT", (1, t)))
                w = weights("w_in", l, ("zm", last))
                for t in TILES[m]:
                    by_token(("zm", t), t, w, 0, LAT)
                w = weights("w_in", l, ("a", m, 3))
                for f in range(4):
                    by_feature(("a", m, f), w, P * f)
                w = weights("w_in", l, ("zp", last))
                for f in range(2):
                    by_feature(("a", m, 4 + f), w, P * f)
                for t in TILES[m]:
                    by_token(("zp", t), t, w, GROUP_W, GROUP_W)
                w = weights("w_in", l, ("rk", m) if STREAM[m] == 0 else ("rqk", m, 3))
                for f in range(4):
                    by_feature(("rqk", m, f), w, P * f)
                if STREAM[m] == 0:
                    by_token(("rk", m), TILES[m][0], w, GROUP_W, GROUP_W)
                w = weights("w_in", l, ("rvg", last))
                for t in TILES[m]:
                    by_token(("rvg", t), t, w, 0, 512)

            def mla(m):
                l, s, nk = LAYER[m], STREAM[m], nk_of(m)
                if s == 1:
                    pe.wait_ge(bank_free[slot("ctxT", m)], use("ctxT", m))
                    ps = psum[slot("ctxT", m)]
                    pe.transpose(ps[:, 0:P], ctx_ckv[:, :], ident[:, :]).then_inc(bank_filled[slot("ctxT", m)], 1)
                for t in TILES[m]:
                    i, cc = tok(m, t)
                    pe.wait_ge(lat_ready, nth("lat", t))
                    pe.wait_ge(bank_free[slot("latT", t)], use("latT", t))
                    ps = psum[slot("latT", t)]
                    for k in range(3):
                        mm = pe.transpose(ps[:, P * k:P * k + P], lat[:, i, P * k:P * k + P], ident[:, :])
                    mm.then_inc(bank_filled[slot("latT", t)], 1)
                    pe.wait_ge(latT_ready, nth("latT", t))
                    pe.wait_ge(bank_free[slot("q", t)], use("q", t))
                    ps = psum[slot("q", t)]
                    for k in range(2):
                        mm = pe.matmul(ps[:, 0:HEADS * QK], qlT[:, k, cc], w_uq[:, k, :], start=(k == 0), stop=(k == 1))
                    mm.then_inc(bank_filled[slot("q", t)], 1)
                    pe.wait_ge(qtok_ready, nth("qtok", t))
                    pe.wait_ge(bank_free[slot("qT", t)], use("qT", t))
                    ps = psum[slot("qT", t)]
                    for h in range(HEADS):
                        mm = pe.transpose(ps[0:QK, P * h:P * h + P], q_tok[:, QK * h:QK * h + QK], ident[:, :])
                    mm.then_inc(bank_filled[slot("qT", t)], 1)
                if s == 1:
                    pe.wait_ge(ctxT_ready, nth("ctxT", m))
                for h in range(HEADS):
                    pe.wait_ge(bank_free[slot("kT", m, h)], use("kT", m, h))
                    ps = psum[slot("kT", m, h)]
                    pe.matmul(ps[0:HD, 0:P * nk], w_ukv[:, 0, HD * h:HD * h + HD], ckvT[:, 0:P * nk], start=True, stop=True)
                    for k in range(nk):
                        if s == 0:
                            kr = zm[:, 0, Q_LORA + KV_LORA:LAT]
                        else:
                            kr = ctx_kr[:, :] if k == 0 else krr[:, k - 1, :]
                        mm = pe.matmul(ps[HD:QK, P * k:P * k + P], kr, ident[:, :], start=True, stop=True)
                    mm.then_inc(bank_filled[slot("kT", m, h)], 1)
                for k in range(nk):
                    pe.wait_ge(bank_free[slot("v", m, k)], use("v", m, k))
                    ps = psum[slot("v", m, k)]
                    pe.matmul(ps[:, 0:GROUP_W], ckvT[:, P * k:P * k + P], w_ukv[:, 1, :],
                                                 start=True, stop=True).then_inc(bank_filled[slot("v", m, k)], 1)
                pe.wait_ge(v_ready, nth("v", (m, nk - 1)))
                for t in TILES[m]:
                    _, cc = tok(m, t)
                    pe.wait_ge(qT_ready, nth("qT", t))
                    for h in range(HEADS):
                        pe.wait_ge(kT_ready, nth("kT", (m, h)))
                        pe.wait_ge(bank_free[slot("sc", t, h)], use("sc", t, h))
                        ps = psum[slot("sc", t, h)]
                        pe.matmul(ps[:, 0:P * nk], qT[0:QK, h, cc], kT[0:QK, h, 0:P * nk],
                                                      start=True, stop=True).then_inc(bank_filled[slot("sc", t, h)], 1)
                    pe.wait_ge(probs_ready, nth("probs", t))
                    for h in range(HEADS):
                        pe.wait_ge(bank_free[slot("pT", t, h)], use("pT", t, h))
                        ps = psum[slot("pT", t, h)]
                        for k in range(nk):
                            mm = pe.transpose(ps[:, P * k:P * k + P], probs[:, h, P * k:P * k + P], ident[:, :])
                        mm.then_inc(bank_filled[slot("pT", t, h)], 1)
                        if h % 2:
                            pe.wait_ge(bank_free[slot("o", t, h // 2)], use("o", t, h // 2))
                            ps = psum[slot("o", t, h // 2)]
                            for g in range(2):
                                pe.wait_ge(pT_ready, nth("pT", (t, h - 1 + g)))
                                for k in range(nk):
                                    mm = pe.matmul(ps[HD * g:HD * g + HD, 0:P], vtok[:, k, HD * (h - 1 + g):HD * (h + g)],
                                                   pT[:, g, P * k:P * k + P], start=(k == 0), stop=(k == nk - 1))
                            mm.then_inc(bank_filled[slot("o", t, h // 2)], 1)

            def ret(m):
                l, s, nt = LAYER[m], STREAM[m], len(TILES[m])
                T = P * nt
                pe.wait_ge(rqk_ready, nth("rqk", m))

                def inner(h):
                    q, g = h // 2, HD * (h % 2)
                    for i in range(nt):
                        pe.wait_ge(bank_free[slot("inn", m, h, i)], use("inn", m, h, i))
                        ps = psum[slot("inn", m, h, i)]
                        pe.matmul(ps[:, 0:T], rqk[g:g + HD, 2 + q, P * i:P * i + P],
                                                          rqk[g:g + HD, q, 0:T], start=True, stop=True).then_inc(bank_filled[slot("inn", m, h, i)], 1)

                inner(0)
                for h in range(HEADS):
                    q, g = h // 2, HD * (h % 2)
                    if h + 1 < HEADS:
                        inner(h + 1)
                    for i in range(nt):
                        pe.wait_ge(bank_free[slot("inn", m, h, i)], use("inn", m, h, i) + 1)
                        pe.wait_ge(rvg_ready, nth("rvg", TILES[m][i]))
                    pe.wait_ge(bank_free[slot("oh", m, h)], use("oh", m, h))
                    ps = psum[slot("oh", m, h)]
                    for j in range(nt):
                        for i in range(nt):
                            mm = pe.matmul(ps[:, 192 * j:192 * j + HD], inn[:, h % 2, i, P * j:P * j + P],
                                           rv[:, i, 0, HD * h:HD * h + HD], start=(i == 0), stop=(i == nt - 1))
                        if s == 1:
                            mm = pe.matmul(ps[:, 192 * j + HD:192 * j + 3 * HD], rqk[g:g + HD, q, P * j:P * j + P],
                                           s0[g:g + HD, q, :], start=True, stop=True)
                    mm.then_inc(bank_filled[slot("oh", m, h)], 1)
                if s == 0:
                    pe.wait_ge(k_decayed_ready, nth("k_decayed", m))
                    pe.wait_ge(bank_free[slot("st", m)], use("st", m))
                    ps = psum[slot("st", m)]
                    for r in range(2):
                        for h in range(HEADS):
                            o = HD * (HEADS * r + h)
                            mm = pe.matmul(ps[0:HD, o:o + HD], xn[:, 512 + o:512 + o + HD], rv[:, 0, 0, HD * h:HD * h + HD],
                                           start=True, stop=True)
                    mm.then_inc(bank_filled[slot("st", m)], 1)
                for t in TILES[m]:
                    i, _ = tok(m, t)
                    pe.wait_ge(ret_out_ready, nth("ret_out", t))
                    pe.wait_ge(bank_free[slot("yrT", t)], use("yrT", t))
                    ps = psum[slot("yrT", t)]
                    for k in range(2):
                        mm = pe.transpose(ps[:, P * k:P * k + P], o_tok[:, i, P * k:P * k + P], ident[:, :])
                    mm.then_inc(bank_filled[slot("yrT", t)], 1)

            def pool_(m):
                l, s, nt = LAYER[m], STREAM[m], len(TILES[m])
                T = P * nt
                for t in TILES[m]:
                    pe.wait_ge(zp_ready, nth("zp", t))
                for b in range(2):
                    pe.wait_ge(bank_free[slot("pl", m, b)], use("pl", m, b))
                    ps = psum[slot("pl", m, b)]
                    for g in range(2):
                        n = 2 * b + g
                        half = slice(HD * g, HD * g + HD)
                        for i in range(nt):
                            mm = pe.matmul(ps[half, P * i:P * i + P], zp[:, i, HD * n:HD * n + HD], band[:, s + i, n, :],
                                           start=True, stop=True)
                            if s == 1:
                                c0 = P - 8 if i == 0 else P
                                mm = pe.matmul(ps[half, c0:c0 + 8], zp[:, 1 - i, HD * n:HD * n + HD], edge[:, i, n, :],
                                               start=False, stop=True, skip_group_check=True)
                    mm.then_inc(bank_filled[slot("pl", m, b)], 1)
                for b in range(2):
                    pe.wait_ge(pooled_ready, nth("pooled", (m, b)))
                    pe.wait_ge(bank_free[slot("plo", m, b)], use("plo", m, b))
                    ps = psum[slot("plo", m, b)]
                    for g in range(2):
                        mm = pe.matmul(ps[HD * g:HD * g + HD, 0:T], w_pool[HD * g:HD * g + HD, b, :],
                                       pooled[HD * g:HD * g + HD, b, 0:T], start=True, stop=True)
                    mm.then_inc(bank_filled[slot("plo", m, b)], 1)

            def gate(which, n, l, s):
                for b in range(2):
                    pe.wait_ge(bank_free[slot("gate", which, n, b)], use("gate", which, n, b))
                    ps = psum[slot("gate", which, n, b)]
                    kind = G1 if which == 1 else G2
                    for k in range(4):
                        col = modc[:, l, 8 * kind + 4 * b + k, s:s + 1]
                        mm = pe.matmul(ps[:, P * k:P * k + P], col.to_broadcast([P, P]), ident[:, :], start=True, stop=True)
                    mm.then_inc(bank_filled[slot("gate", which, n, b)], 1)

            def out(m):
                pe.wait_ge(mods_ready, nth("mods", LAYER[m]))
                gate(1, m, LAYER[m], STREAM[m])
                pe.wait_ge(y_conv_ready, nth("y_conv", m))
                pe.wait_ge(y_pool_ready, nth("y_pool", (m, 1)))
                for b in range(2):
                    w = weights("w_out", LAYER[m], ("mix", TILES[m][-1], b))
                    for t in TILES[m]:
                        _, cc = tok(m, t)
                        pe.wait_ge(y_mla_ready, nth("y_mla", (t, 1)))
                        pe.wait_ge(y_ret_ready, nth("y_ret", t))
                        pe.wait_ge(bank_free[slot("mix", t, b)], use("mix", t, b))
                        ps = psum[slot("mix", t, b)]
                        for k in range(DC):
                            mm = pe.matmul(ps[:, :], yT[:, k, cc], w[:, k, :], start=(k == 0), stop=(k == DC - 1))
                        mm.then_inc(bank_filled[slot("mix", t, b)], 1)

            def query(m):
                T = P * len(TILES[m])
                for t in TILES[m]:
                    pe.wait_ge(hT_ready, nth("hT", (2, t)))
                for b in range(2):
                    w = weights("peer_w_q", LAYER[m], ("qp", m, 4 * b + 3))
                    for i in range(4):
                        key = ("qp", m, 4 * b + i)
                        pe.wait_ge(bank_free[slot(*key)], use(*key))
                        ps = psum[slot(*key)]
                        for k in range(DC):
                            mm = pe.matmul(ps[:, 0:T], w[:, k, P * i:P * i + P], hT[:, k, 0:T], start=(k == 0), stop=(k == DC - 1))
                        mm.then_inc(bank_filled[slot(*key)], 1)

            def score(t):
                m = M_OF[t]
                _, cc = tok(m, t)
                pe.wait_ge(sk_ready, nth("sk", LAYER[m]))
                for b in range(4):
                    pe.wait_ge(bank_free[slot("s", t, b)], use("s", t, b))
                    ps = psum[slot("s", t, b)]
                    for i in range(4):
                        h, g = 4 * (b % 2) + i, HD * (b // 2)
                        pe.wait_ge(qp_ready, nth("qp", (m, h)))
                        mm = pe.matmul(ps[:, P * i:P * i + P], qpT[g:g + HD, h, cc], skT[g:g + HD, h, :], start=True, stop=True)
                    mm.then_inc(bank_filled[slot("s", t, b)], 1)

            def peer(t):
                def step(r, k, it, first, last):
                    pe.wait_ge(v_landed[r], it)
                    pe.wait_ge(diag_built, k + 1)
                    for b in range(2):
                        mm = pe.matmul(ysum[:, b, :], diag[:, r % DIAGS, :], vbuf[:, r, 512 * b:512 * b + 512],
                                       start=first, stop=last, skip_group_check=True)
                    mm.then_inc(v_free, 1)

                if t == 0:
                    pe.sem_inc(v_free, SLOTS)
                else:
                    pe.wait_ge(updated_ready, nth("updated", t - 1))
                for r in range(G):
                    step(r, PICKS * t + r, 16 * (NG * t + 1), r == 0, False)
                with pe.Fori(1, NG - 1) as i:
                    for r in range(G):
                        step(r, i * G + (PICKS * t + r), i * 16 + 16 * (NG * t + 1), False, False)
                for r in range(G):
                    step(r, PICKS * t + G * (NG - 1) + r, 16 * (NG * t + NG), False, r == G - 1)
                gate(2, t, LAYER[M_OF[t]], STREAM[M_OF[t]])

            for kind, *n in SCHEDULE:
                if kind == "start":
                    start(*n)
                elif kind == "mods":
                    mods(*n)
                elif kind == "keys":
                    keys(*n)
                elif kind == "ln":
                    ln(*n)
                elif kind == "in":
                    project(*n)
                elif kind == "mla":
                    mla(*n)
                elif kind == "ret":
                    ret(*n)
                elif kind == "pool":
                    pool_(*n)
                elif kind == "out":
                    out(*n)
                elif kind == "q":
                    query(*n)
                elif kind == "score":
                    score(*n)
                elif kind == "peer":
                    peer(*n)

        @block.scalar
        def _(act):
            order = [0]

            def link(ins):
                order[0] += 1
                ins.then_inc(act_order, 1)
                act.wait_ge(act_order, order[0])

            def std(key, *parts):
                act.wait_ge(sumsq_ready, nth("sumsq", key))
                for dst, src, n in parts:
                    ins = act.activation(dst, src, ACT.Sqrt, scale=1.0 / n, bias=EPS)
                ins.then_inc(std_ready, 1)

            def start(_):
                act.wait_ge(small_landed, 16 * N_SMALL)
                act.wait_ge(bank_filled[slot("vec")], use("vec"))
                act.activation(cols[:, :], psum[slot("vec")][:, 0:VC + 96], ACT.Copy)\
                   .then_inc(bank_free[slot("vec")], 1)
                act.wait_ge(bank_free[slot("vec")], use("vec") + 1)
                act.activation(cond[:, :, :], cols[:, 0:16].rearrange("p (s k) -> p s k", s=2), ACT.Silu).then_inc(cond_ready, 1)
                act.wait_ge(cond_ready, nth("cond", 0))
                act.wait_ge(abs_logit_ready, nth("abs_logit", 0))
                act.activation(logit[:, 1, :], logit[:, 1, :], ACT.Exp, scale=-1.0).then_inc(act_done, 1)
                act.wait_ge(act_done, 1)
                act.activation(logit[:, 2, :], logit[:, 1, :], ACT.Ln, bias=1.0).then_inc(log1p_ready, 1)

            def mods(l):
                for j in range(12):
                    if (l, j) != (0, 0) and j >= 2:
                        act.wait_ge(bank_filled[slot("modcol", l, j - 2)], use("modcol", l, j - 2))
                    act.wait_ge(bank_filled[slot("modrow", l, j)], use("modrow", l, j))
                    act.activation(mrow[0:2, j % 2, :], psum[slot("modrow", l, j)][0:2, 0:512], ACT.Copy)\
                       .then_inc(bank_free[slot("modrow", l, j)], 1)
                    act.wait_ge(bank_free[slot("modrow", l, j)], use("modrow", l, j) + 1)
                    act.sem_inc(mrow_ready, 1)

            def keys(l):
                for b in range(2):
                    act.wait_ge(bank_filled[slot("sk", l, b)], use("sk", l, b))
                    act.activation(skT[:, 4 * b:4 * b + 4, :].rearrange("p h n -> p (h n)"), psum[slot("sk", l, b)][:, 0:512], ACT.Copy)\
                       .then_inc(bank_free[slot("sk", l, b)], 1)
                    act.wait_ge(bank_free[slot("sk", l, b)], use("sk", l, b) + 1)
                act.sem_inc(sk_ready, 1)

            def decay_(l):
                for h in range(HEADS):
                    act.wait_ge(decay_arg_ready, nth("decay_arg", (l, h)))
                    act.activation(decay[:, h, :], decay[:, h, :], ACT.Exp).then_inc(decay_exp_ready, 1)
                for r in range(2):
                    for h in range(HEADS):
                        k = 8 * l + 4 * r + h
                        act.activation(dcol[:, r, h, :], pos3[:, r, :], ACT.Exp, scale=logit[:, 3, k:k + 1]).then_inc(decay_col_ready, 1)

            def ln(which, t):
                m = M_OF[t]
                l, s = LAYER[m], STREAM[m]
                _, cc = tok(m, t)
                std(("ln", which, t), (stat[:, 1:2], stat[:, 0:1], D))
                act.wait_ge(mods_ready, nth("mods", l))
                for b in range(2):
                    key = ("xnT", which, t, b)
                    act.wait_ge(bank_filled[slot(*key)], use(*key))
                    ps = psum[slot(*key)]
                    for k in range(4):
                        f = 4 * b + k
                        ins = act.activation(hT[:, f, cc], ps[:, P * k:P * k + P], ACT.Identity,
                                             scale=moda[:, l, which - 1, s, f:f + 1],
                                             bias=modc[:, l, 8 * (SH1 if which == 1 else SH2) + f, s:s + 1])
                        if k == 3:
                            ins.then_inc(bank_free[slot(*key)], 1)
                    act.wait_ge(bank_free[slot(*key)], use(*key) + 1)
                act.sem_inc(hT_ready, 1)
                if which == 2:
                    for b in range(2):
                        act.wait_ge(bank_filled[slot("h2tok", t, b)], use("h2tok", t, b))
                        act.activation(h2[:, XBUF[t], 512 * b:512 * b + 512], psum[slot("h2tok", t, b)][:, 0:512], ACT.Copy)\
                           .then_inc(bank_free[slot("h2tok", t, b)], 1)
                        act.wait_ge(bank_free[slot("h2tok", t, b)], use("h2tok", t, b) + 1)
                        act.sem_inc(h2_ready, 1)

            def project(m):
                T = P * len(TILES[m])
                if m:
                    act.wait_ge(mixed_ready, nth("mixed", TILES[m - 1][-1]))
                for f in range(6):
                    act.wait_ge(bank_filled[slot("a", m, f)], use("a", m, f))
                    act.activation(za[:, f, 0:T], psum[slot("a", m, f)][:, 0:T], ACT.Copy)\
                       .then_inc(bank_free[slot("a", m, f)], 1)
                    act.wait_ge(bank_free[slot("a", m, f)], use("a", m, f) + 1)
                act.sem_inc(za_ready, 1)
                for t in TILES[m]:
                    i, _ = tok(m, t)
                    act.wait_ge(bank_filled[slot("zp", t)], use("zp", t))
                    act.activation(zp[:, i, :], psum[slot("zp", t)][:, 0:GROUP_W], ACT.Copy)\
                       .then_inc(bank_free[slot("zp", t)], 1)
                    act.wait_ge(bank_free[slot("zp", t)], use("zp", t) + 1)
                    act.sem_inc(zp_ready, 1)
                for f in range(4):
                    act.wait_ge(bank_filled[slot("rqk", m, f)], use("rqk", m, f))
                    act.activation(rqk[:, f, 0:T], psum[slot("rqk", m, f)][:, 0:T], ACT.Copy)\
                       .then_inc(bank_free[slot("rqk", m, f)], 1)
                    act.wait_ge(bank_free[slot("rqk", m, f)], use("rqk", m, f) + 1)
                act.sem_inc(rqk_ready, 1)
                for t in TILES[m]:
                    i, _ = tok(m, t)
                    act.wait_ge(bank_filled[slot("rvg", t)], use("rvg", t))
                    ps = psum[slot("rvg", t)]
                    act.activation(rv[:, i, 0, :], ps[:, 0:GROUP_W], ACT.Copy)
                    act.activation(rv[:, i, 1, :], ps[:, GROUP_W:512], ACT.Silu).then_inc(bank_free[slot("rvg", t)], 1)
                    act.wait_ge(bank_free[slot("rvg", t)], use("rvg", t) + 1)
                    act.sem_inc(rvg_ready, 1)

            def mla(m):
                l, s, nk = LAYER[m], STREAM[m], nk_of(m)
                act.wait_ge(bank_filled[slot("rvg", TILES[m][-1])], use("rvg", TILES[m][-1]))
                for t in TILES[m]:
                    std(("mla", t), (stat[:, 18:19], stat[:, 16:17], Q_LORA), (stat[:, 19:20], stat[:, 17:18], KV_LORA))
                if s == 1:
                    act.wait_ge(bank_filled[slot("ctxT", m)], use("ctxT", m))
                    act.activation(ckvT[:, 0:P], psum[slot("ctxT", m)][:, 0:P], ACT.Copy)\
                       .then_inc(bank_free[slot("ctxT", m)], 1)
                    act.wait_ge(bank_free[slot("ctxT", m)], use("ctxT", m) + 1)
                    act.sem_inc(ctxT_ready, 1)
                for t in TILES[m]:
                    i, cc = tok(m, t)
                    if s == 0:
                        act.wait_ge(lat_ready, nth("lat", t))
                        act.dma_start(new_ckv[0, l], lat[:, 0, Q_LORA:Q_LORA + KV_LORA]).then_inc(cache_stored, 16)
                        act.dma_start(new_krope[0, l], zm[:, 0, Q_LORA + KV_LORA:LAT]).then_inc(cache_stored, 16)
                    act.wait_ge(bank_filled[slot("latT", t)], use("latT", t))
                    ps = psum[slot("latT", t)]
                    for k in range(2):
                        act.activation(qlT[:, k, cc], ps[:, P * k:P * k + P], ACT.Identity,
                                       scale=cols[:, QNORM + 2 * l + k:QNORM + 2 * l + k + 1])
                    k0 = P * (i + nk - len(TILES[m]))
                    act.activation(ckvT[:, k0:k0 + P], ps[:, 2 * P:3 * P], ACT.Copy).then_inc(bank_free[slot("latT", t)], 1)
                    act.wait_ge(bank_free[slot("latT", t)], use("latT", t) + 1)
                    act.sem_inc(latT_ready, 1)
                    act.wait_ge(bank_filled[slot("qT", t)], use("qT", t))
                    act.activation(qT[0:QK, :, cc], psum[slot("qT", t)][0:QK, 0:512], ACT.Copy)\
                       .then_inc(bank_free[slot("qT", t)], 1)
                    act.wait_ge(bank_free[slot("qT", t)], use("qT", t) + 1)
                    act.sem_inc(qT_ready, 1)
                for h in range(HEADS):
                    act.wait_ge(bank_filled[slot("kT", m, h)], use("kT", m, h))
                    act.activation(kT[0:QK, h, 0:P * nk], psum[slot("kT", m, h)][0:QK, 0:P * nk], ACT.Copy)\
                       .then_inc(bank_free[slot("kT", m, h)], 1)
                    act.wait_ge(bank_free[slot("kT", m, h)], use("kT", m, h) + 1)
                    act.sem_inc(kT_ready, 1)
                for k in range(nk):
                    act.wait_ge(bank_filled[slot("v", m, k)], use("v", m, k))
                    act.activation(vtok[:, k, :], psum[slot("v", m, k)][:, 0:GROUP_W], ACT.Copy)\
                       .then_inc(bank_free[slot("v", m, k)], 1)
                    act.wait_ge(bank_free[slot("v", m, k)], use("v", m, k) + 1)
                    act.sem_inc(v_ready, 1)
                for t in TILES[m]:
                    _, cc = tok(m, t)
                    act.wait_ge(row_max_ready, nth("row_max", t))
                    for h in range(HEADS):
                        key = ("sc", t, h)
                        act.wait_ge(bank_filled[slot(*key)], use(*key))
                        ps = psum[slot(*key)]
                        act.activation(probs[:, h, 0:P * nk], ps[:, 0:P * nk], ACT.Exp, scale=SM_SCALE,
                                       bias=stat[:, 4 + h:5 + h], accum_out=stat[:, 8 + h:9 + h])\
                           .then_inc(bank_free[slot(*key)], 1)
                        act.wait_ge(bank_free[slot(*key)], use(*key) + 1)
                    for h in range(HEADS):
                        if h >= 2 and h % 2 == 0:
                            act.wait_ge(bank_filled[slot("o", t, h // 2 - 1)], use("o", t, h // 2 - 1))
                        act.wait_ge(bank_filled[slot("pT", t, h)], use("pT", t, h))
                        act.activation(pT[:, h % 2, 0:P * nk], psum[slot("pT", t, h)][:, 0:P * nk], ACT.Copy)\
                           .then_inc(bank_free[slot("pT", t, h)], 1)
                        act.wait_ge(bank_free[slot("pT", t, h)], use("pT", t, h) + 1)
                        act.sem_inc(pT_ready, 1)
                        if h % 2:
                            act.wait_ge(bank_filled[slot("o", t, h // 2)], use("o", t, h // 2))
                            act.activation(yT[:, 2 + h // 2, cc], psum[slot("o", t, h // 2)][:, 0:P], ACT.Copy)\
                               .then_inc(bank_free[slot("o", t, h // 2)], 1)
                            act.wait_ge(bank_free[slot("o", t, h // 2)], use("o", t, h // 2) + 1)
                            act.sem_inc(y_mla_ready, 1)

            def ret(m):
                if STREAM[m] == 0:
                    if m:
                        act.wait_ge(state_stored, 16)
                    act.wait_ge(bank_filled[slot("st", m)], use("st", m))
                    act.activation(state_out[:, :], psum[slot("st", m)][0:HD, 0:512], ACT.Copy)\
                       .then_inc(bank_free[slot("st", m)], 1)
                    act.wait_ge(bank_free[slot("st", m)], use("st", m) + 1)
                    act.sem_inc(state_ready, 1)
                    act.dma_start(new_state[0, LAYER[m]].rearrange("r h k v -> k (r h) v"),
                                  state_out[:, :].rearrange("k (n v) -> k n v", v=HD)).then_inc(state_stored, 16)
                for t in TILES[m]:
                    _, cc = tok(m, t)
                    std(("ret", t), (stat[:, 28:32], stat[:, 24:28], HD))
                    key = ("yrT", t)
                    act.wait_ge(bank_filled[slot(*key)], use(*key))
                    ps = psum[slot(*key)]
                    act.activation(yT[:, 4:6, cc], ps[:, 0:2 * P].rearrange("p (k n) -> p k n", k=2), ACT.Copy)\
                       .then_inc(bank_free[slot(*key)], 1)
                    act.wait_ge(bank_free[slot(*key)], use(*key) + 1)
                    act.sem_inc(y_ret_ready, 1)

            def pool_(m):
                T = P * len(TILES[m])
                l = LAYER[m]
                for b in range(2):
                    act.wait_ge(bank_filled[slot("pl", m, b)], use("pl", m, b))
                    act.activation(pooled[:, b, 0:T], psum[slot("pl", m, b)][:, 0:T], ACT.Copy)\
                       .then_inc(bank_free[slot("pl", m, b)], 1)
                    act.wait_ge(bank_free[slot("pl", m, b)], use("pl", m, b) + 1)
                    act.sem_inc(pooled_ready, 1)
                for b in range(2):
                    act.wait_ge(bank_filled[slot("plo", m, b)], use("plo", m, b))
                    act.activation(yT[:, 6 + b, 0:T], psum[slot("plo", m, b)][:, 0:T], ACT.Identity, scale=cols[:, POOLS + 2 * l + b:POOLS + 2 * l + b + 1])\
                       .then_inc(bank_free[slot("plo", m, b)], 1)
                    act.wait_ge(bank_free[slot("plo", m, b)], use("plo", m, b) + 1)
                    act.sem_inc(y_pool_ready, 1)

            def gate(which, n):
                for b in range(2):
                    act.wait_ge(bank_filled[slot("gate", which, n, b)], use("gate", which, n, b))
                    act.activation(gate_row[:, 512 * b:512 * b + 512], psum[slot("gate", which, n, b)][:, 0:512], ACT.Copy)\
                       .then_inc(bank_free[slot("gate", which, n, b)], 1)
                    act.wait_ge(bank_free[slot("gate", which, n, b)], use("gate", which, n, b) + 1)
                    act.sem_inc(gate_ready, 1)

            def out(m):
                if m:
                    act.wait_ge(updated_ready, nth("updated", TILES[m - 1][-1]))
                gate(1, m)

            def query(m):
                T = P * len(TILES[m])
                for h in range(PEER_H):
                    act.wait_ge(bank_filled[slot("qp", m, h)], use("qp", m, h))
                    act.activation(qpT[:, h, 0:T], psum[slot("qp", m, h)][:, 0:T], ACT.Copy)\
                       .then_inc(bank_free[slot("qp", m, h)], 1)
                    act.wait_ge(bank_free[slot("qp", m, h)], use("qp", m, h) + 1)
                    act.sem_inc(qp_ready, 1)

            def score(t):
                if t:
                    act.wait_ge(picked_ready, nth("picked", t - 1))
                if STREAM[M_OF[t]] == 0:
                    act.wait_ge(cache_stored, 32 * (LAYER[M_OF[t]] + 1))
                for b in range(4):
                    act.wait_ge(bank_filled[slot("s", t, b)], use("s", t, b))
                    act.activation(s_sb[:, 512 * b:512 * b + 512], psum[slot("s", t, b)][:, 0:512], ACT.Copy)\
                       .then_inc(bank_free[slot("s", t, b)], 1)
                    act.wait_ge(bank_free[slot("s", t, b)], use("s", t, b) + 1)
                    act.sem_inc(scores_ready, 1)

            def topk(t):
                act.wait_ge(gate_arg_ready, nth("gate_arg", t))
                act.activation(cv[:, :, :], cv[:, :, :], ACT.Exp).then_inc(gate_exp_ready, 1)

            def peer(t):
                with act.Fori(0, NG) as i:
                    act.wait_ge(u_free, i * G + (SLOTS + PICKS * t + G))
                    act.activation(act_dot[:, :], dot[:, :], ACT.Gelu_apprx_tanh).then_inc(gelu_done, 1)
                    for r in range(G):
                        if r == 0:
                            act.wait_ge(coef_done, i + (NG * t + 1))
                        act.wait_ge(v_free, i * G + (SLOTS + PICKS * t + r - DIAGS + 1))
                        act.activation(diag[:, r % DIAGS, :], ident[:, :], ACT.Copy, scale=coef[:, r:r + 1]).then_inc(diag_built, 1)
                act.wait_ge(mixed_ready, nth("mixed", TILES[M_OF[t]][-1]))
                if t:
                    act.wait_ge(updated_ready, nth("updated", t - 1))
                gate(2, t)
                if t >= 3:
                    std(("final", t), (stat[:, 1:2], stat[:, 0:1], D))
                    act.wait_ge(final_ready, nth("final", t))
                    dst = y_prompt[0] if t == 3 else y_sample[0, P * (t - 4):P * (t - 4) + P, :]
                    act.dma_start(dst, xn[:, :]).then_inc(y_stored, 16)

            for kind, *n in SCHEDULE:
                if kind == "start":
                    start(*n)
                elif kind == "mods":
                    mods(*n)
                elif kind == "keys":
                    keys(*n)
                elif kind == "decay":
                    decay_(*n)
                elif kind == "ln":
                    ln(*n)
                elif kind == "in":
                    project(*n)
                elif kind == "mla":
                    mla(*n)
                elif kind == "ret":
                    ret(*n)
                elif kind == "pool":
                    pool_(*n)
                elif kind == "out":
                    out(*n)
                elif kind == "q":
                    query(*n)
                elif kind == "score":
                    score(*n)
                elif kind == "topk":
                    topk(*n)
                elif kind == "peer":
                    peer(*n)
            act.wait_ge(cache_stored, 64)
            act.wait_ge(state_stored, 32)
            act.wait_ge(y_stored, 48)

        @block.vector
        def _(dve):
            steps = [0]

            def counted():
                steps[0] += 1
                return 1

            def rstd(dst, key):
                dve.sem_inc(sumsq_ready, 1)
                dve.wait_ge(std_ready, nth("std", key))
                dve.reciprocal(dst, dst).then_inc(dve_done, counted())
                dve.wait_ge(dve_done, steps[0])

            def start(_):
                for b in range(RING):
                    dve.sem_inc(bank_free[b], 1)
                dve.wait_ge(small_landed, 16 * N_SMALL)
                dve.wait_ge(x_landed, 48)
                dve.scalar_tensor_tensor(out=logit[:, 1, :], in0=logit[:, 0, :], scalar=-1.0, in1=logit[:, 0, :],
                                             op0=ALU.mult, op1=ALU.max).then_inc(abs_logit_ready, 1)
                dve.wait_ge(abs_logit_ready, nth("abs_logit", 0))
                dve.wait_ge(log1p_ready, nth("log1p", 0))
                dve.tensor_scalar(logit[:, 3, :], logit[:, 0, :], 0.0, None, ALU.min).then_inc(dve_done, counted())
                dve.wait_ge(dve_done, steps[0])
                dve.tensor_tensor(logit[:, 3, :], logit[:, 3, :], logit[:, 2, :], ALU.subtract).then_inc(decay_log_ready, 1)
                dve.wait_ge(decay_log_ready, nth("decay_log", 0))
                dve.wait_ge(cond_ready, nth("cond", 0))

            def mods(l):
                for j in range(12):
                    key = ("modcol", l, j)
                    dve.wait_ge(bank_filled[slot(*key)], use(*key))
                    ps = psum[slot(*key)]
                    bias = cols[:, BMOD + 48 * l + 4 * j:BMOD + 48 * l + 4 * j + 4]
                    dve.tensor_tensor(modc[:, l, 4 * j:4 * j + 4, :], ps[:, 0:8].rearrange("p (k s) -> p k s", s=2),
                                                    bias.unsqueeze(2).to_broadcast([P, 4, 2]), ALU.add).then_inc(bank_free[slot(*key)], 1)
                    dve.wait_ge(bank_free[slot(*key)], use(*key) + 1)
                for which in (1, 2):
                    kind = SC1 if which == 1 else SC2
                    for s in range(2):
                        ins = dve.scalar_tensor_tensor(out=moda[:, l, which - 1, s, :], in0=modc[:, l, 8 * kind:8 * kind + 8, s],
                                                       scalar=1.0, in1=cols[:, NORM[which] + 8 * l:NORM[which] + 8 * l + 8],
                                                       op0=ALU.add, op1=ALU.mult)
                        if (which, s) == (2, 1):
                            ins.then_inc(mods_ready, 1)
                            dve.wait_ge(mods_ready, nth("mods", l))

            def decay_(l):
                for h in range(HEADS):
                    f, b = 8 * l + h, 8 * l + 4 + h
                    dve.tensor_scalar(decay[:, h, :], rel[:, 1, :], logit[:, 3, b:b + 1], None, ALU.mult).then_inc(dve_done, counted())
                    dve.wait_ge(dve_done, steps[0])
                    dve.scalar_tensor_tensor(out=decay[:, h, :], in0=rel[:, 0, :], scalar=logit[:, 3, f:f + 1],
                                                 in1=decay[:, h, :], op0=ALU.mult, op1=ALU.add).then_inc(decay_arg_ready, 1)
                    dve.wait_ge(decay_arg_ready, nth("decay_arg", (l, h)))
                for h in range(HEADS):
                    dve.wait_ge(decay_exp_ready, nth("decay_exp", (l, h)))
                    dve.tensor_scalar(decay[:, h, :], decay[:, h, :], K_SCALE, None, ALU.mult).then_inc(dve_done, counted())
                    dve.wait_ge(dve_done, steps[0])
                    mid = decay[:, h, P:2 * P]
                    dve.scalar_tensor_tensor(out=mid, in0=ident[:, :], scalar=K_SCALE, in1=mid, op0=ALU.mult, op1=ALU.add).then_inc(dve_done, counted())
                    dve.wait_ge(dve_done, steps[0])
                dve.wait_ge(decay_col_ready, nth("decay_col", (l, 7)))

            def ln(which, t):
                xt = x[:, XBUF[t], :]
                if t >= 4 and which == 1:
                    dve.wait_ge(y_stored, 16)
                dve.tensor_tensor_reduce(xn[:, :], xt, xt, 1.0, 0.0, ALU.mult, ALU.add, stat[:, 0:1]).then_inc(dve_done, counted())
                dve.wait_ge(dve_done, steps[0])
                rstd(stat[:, 1:2], ("ln", which, t))
                dve.tensor_scalar(xn[:, :], xt, stat[:, 1:2], None, ALU.mult).then_inc(xn_ready, 1)
                dve.wait_ge(xn_ready, nth("xn", (which, t)))
                dve.wait_ge(bank_filled[slot("xnT", which, t, 1)], use("xnT", which, t, 1))

            def project(m):
                for t in TILES[m]:
                    i, _ = tok(m, t)
                    if m and i == 0:
                        dve.wait_ge(cache_stored, 32 * (LAYER[m - 1] + 1))
                    dve.wait_ge(bank_filled[slot("zm", t)], use("zm", t))
                    ps = psum[slot("zm", t)]
                    dve.tensor_copy(zm[:, i, :], ps[:, 0:LAT]).then_inc(bank_free[slot("zm", t)], 1)
                    dve.wait_ge(bank_free[slot("zm", t)], use("zm", t) + 1)
                if STREAM[m] == 0:
                    dve.wait_ge(bank_filled[slot("rk", m)], use("rk", m))
                    ps = psum[slot("rk", m)]
                    dve.tensor_copy(rk[:, :], ps[:, 0:GROUP_W]).then_inc(bank_free[slot("rk", m)], 1)
                    dve.wait_ge(bank_free[slot("rk", m)], use("rk", m) + 1)

            def rope(dst, src, i, heads, tmp):
                def table(k):
                    return cs[:, i, k, :].unsqueeze(1).to_broadcast([P, heads, ROPE])

                dve.tensor_tensor(tmp, src, table(0), ALU.mult).then_inc(dve_done, counted())
                dve.wait_ge(dve_done, steps[0])
                hs = tmp2[:, 0:heads * ROPE].rearrange("p (h a o e) -> p h a o e", h=heads, a=2, o=2)
                sv = src.rearrange("p h (a o e) -> p h a o e", a=2, o=2)
                sn = cs[:, i, 1, :].rearrange("p (a o e) -> p a o e", a=2, o=2)
                for o in range(2):
                    tab = sn[:, :, o, :].unsqueeze(1).to_broadcast([P, heads, 2, 8])
                    dve.tensor_tensor(hs[:, :, :, o, :], sv[:, :, :, 1 - o, :], tab, ALU.mult).then_inc(dve_done, counted())
                dve.wait_ge(dve_done, steps[0])
                return dve.tensor_tensor(dst, tmp, tmp2[:, 0:heads * ROPE].rearrange("p (h n) -> p h n", h=heads), ALU.add)

            tmp1, tmp2 = xn[:, 0:256], xn[:, 256:512]

            def mla(m):
                l, s, nk = LAYER[m], STREAM[m], nk_of(m)
                for t in TILES[m]:
                    i, _ = tok(m, t)
                    z = zm[:, i, :]
                    dve.tensor_tensor_reduce(tmp1, z[:, 0:Q_LORA], z[:, 0:Q_LORA], 1.0, 0.0, ALU.mult, ALU.add, stat[:, 16:17]).then_inc(dve_done, counted())
                    dve.wait_ge(dve_done, steps[0])
                    zc = z[:, Q_LORA:Q_LORA + KV_LORA]
                    dve.tensor_tensor_reduce(tmp1[:, 0:KV_LORA], zc, zc, 1.0, 0.0, ALU.mult, ALU.add, stat[:, 17:18]).then_inc(dve_done, counted())
                    dve.wait_ge(dve_done, steps[0])
                    rstd(stat[:, 18:20], ("mla", t))
                    dve.tensor_scalar(lat[:, i, 0:Q_LORA], z[:, 0:Q_LORA], stat[:, 18:19], None, ALU.mult).then_inc(dve_done, counted())
                    dve.wait_ge(dve_done, steps[0])
                    if s == 1:
                        rope(krr[:, i:i + 1, :], z[:, Q_LORA + KV_LORA:LAT].unsqueeze(1), i, 1,
                                  tmp1[:, 0:ROPE].unsqueeze(1)).then_inc(dve_done, counted())
                        dve.wait_ge(dve_done, steps[0])
                    dve.scalar_tensor_tensor(out=lat[:, i, Q_LORA:Q_LORA + KV_LORA], in0=zc, scalar=stat[:, 19:20],
                                                 in1=kvn[:, :], op0=ALU.mult, op1=ALU.mult).then_inc(lat_ready, 1)
                    dve.wait_ge(lat_ready, nth("lat", t))
                for t in TILES[m]:
                    i, _ = tok(m, t)
                    if i:
                        dve.wait_ge(bank_filled[slot("qT", t - 1)], use("qT", t - 1))
                    dve.wait_ge(bank_filled[slot("q", t)], use("q", t))
                    ps = psum[slot("q", t)]
                    dve.tensor_copy(q_tok[:, :], ps[:, 0:HEADS * QK]).then_inc(bank_free[slot("q", t)], 1)
                    dve.wait_ge(bank_free[slot("q", t)], use("q", t) + 1)
                    if s == 1:
                        qr = q_tok[:, :].rearrange("p (h n) -> p h n", h=HEADS)[:, :, HD:QK]
                        rope(qr, qr, i, HEADS, tmp1[:, 0:HEADS * ROPE].rearrange("p (h n) -> p h n", h=HEADS)).then_inc(dve_done, counted())
                        dve.wait_ge(dve_done, steps[0])
                    dve.sem_inc(qtok_ready, 1)
                for t in TILES[m]:
                    for h in range(HEADS):
                        dve.wait_ge(bank_filled[slot("sc", t, h)], use("sc", t, h))
                        ps = psum[slot("sc", t, h)]
                        dve.tensor_reduce(stat[:, h:h + 1], ps[:, 0:P * nk], AX, ALU.max).then_inc(dve_done, counted())
                    dve.wait_ge(dve_done, steps[0])
                    dve.tensor_scalar(stat[:, 4:8], stat[:, 0:4], -SM_SCALE, None, ALU.mult).then_inc(row_max_ready, 1)
                    dve.wait_ge(row_max_ready, nth("row_max", t))
                    dve.wait_ge(bank_free[slot("sc", t, HEADS - 1)], use("sc", t, HEADS - 1) + 1)
                    dve.reciprocal(stat[:, 12:16], stat[:, 8:12]).then_inc(dve_done, counted())
                    dve.wait_ge(dve_done, steps[0])
                    dve.tensor_tensor(probs[:, :, 0:P * nk], probs[:, :, 0:P * nk],
                                          stat[:, 12:16].unsqueeze(2).to_broadcast([P, HEADS, P * nk]), ALU.mult).then_inc(probs_ready, 1)
                    dve.wait_ge(probs_ready, nth("probs", t))

            def conv(m):
                T = P * len(TILES[m])
                l = LAYER[m]
                dve.wait_ge(za_ready, nth("za", m))
                dve.wait_ge(bank_filled[slot("rvg", TILES[m][-1])], use("rvg", TILES[m][-1]))
                u, acc = xn[:, 0:T], xn[:, 256:256 + T]
                for f in range(2):
                    def w(tap):
                        k = CONVW + 6 * l + 2 * tap + f
                        return cols[:, k:k + 1]

                    dve.tensor_tensor(u, za[:, 2 + f, 0:T], za[:, 4 + f, 0:T], ALU.mult).then_inc(dve_done, counted())
                    dve.wait_ge(dve_done, steps[0])
                    dve.tensor_scalar(acc, u, w(1), None, ALU.mult).then_inc(dve_done, counted())
                    dve.wait_ge(dve_done, steps[0])
                    dve.scalar_tensor_tensor(out=acc[:, 1:T], in0=u[:, 0:T - 1], scalar=w(0), in1=acc[:, 1:T],
                                                  op0=ALU.mult, op1=ALU.add).then_inc(dve_done, counted())
                    dve.wait_ge(dve_done, steps[0])
                    dve.scalar_tensor_tensor(out=acc[:, 0:T - 1], in0=u[:, 1:T], scalar=w(2), in1=acc[:, 0:T - 1],
                                                  op0=ALU.mult, op1=ALU.add).then_inc(dve_done, counted())
                    dve.wait_ge(dve_done, steps[0])
                    ins = dve.tensor_tensor(yT[:, f, 0:T], acc, za[:, f, 0:T], ALU.mult)
                    if f == 1:
                        ins.then_inc(y_conv_ready, 1)
                        dve.wait_ge(y_conv_ready, nth("y_conv", m))
                    else:
                        ins.then_inc(dve_done, counted())
                        dve.wait_ge(dve_done, steps[0])

            def ret(m):
                l, s, nt = LAYER[m], STREAM[m], len(TILES[m])
                T = P * nt

                def outer(h):
                    key = ("oh", m, h)
                    dve.wait_ge(bank_filled[slot(*key)], use(*key))
                    ps = psum[slot(*key)]
                    for j in range(nt):
                        o = o_tok[:, j, HD * h:HD * h + HD]
                        inner = ps[:, 192 * j:192 * j + HD]
                        if s == 1:
                            b = 192 * j + HD
                            dve.tensor_scalar(o, ps[:, b:b + HD], dcol[:, 0, h, j:j + 1], None, ALU.mult).then_inc(dve_done, counted())
                            dve.wait_ge(dve_done, steps[0])
                            dve.scalar_tensor_tensor(out=o, in0=ps[:, b + HD:b + 2 * HD], scalar=dcol[:, 1, h, j:j + 1],
                                                          in1=o, op0=ALU.mult, op1=ALU.add).then_inc(dve_done, counted())
                            dve.wait_ge(dve_done, steps[0])
                            ins = dve.tensor_tensor(o, inner, o, ALU.add)
                        else:
                            ins = dve.tensor_copy(o, inner)
                        if j == nt - 1:
                            ins.then_inc(bank_free[slot(*key)], 1)
                            dve.wait_ge(bank_free[slot(*key)], use(*key) + 1)
                        else:
                            ins.then_inc(dve_done, counted())
                            dve.wait_ge(dve_done, steps[0])

                if s == 1:
                    dve.wait_ge(state_stored, 16 * (l + 1))
                for h in range(HEADS):
                    for i in range(nt):
                        key = ("inn", m, h, i)
                        dve.wait_ge(bank_filled[slot(*key)], use(*key))
                        ps = psum[slot(*key)]
                        dve.tensor_tensor(inn[:, h % 2, i, 0:T], ps[:, 0:T],
                                                        decay[:, h, P - P * i:P - P * i + T], ALU.mult).then_inc(bank_free[slot(*key)], 1)
                        dve.wait_ge(bank_free[slot(*key)], use(*key) + 1)
                    if h:
                        outer(h - 1)
                outer(HEADS - 1)
                if s == 0:
                    for r in range(2):
                        ins = dve.scalar_tensor_tensor(out=xn[:, 512 + 256 * r:768 + 256 * r].rearrange("p (h n) -> p h n", h=HEADS),
                                                       in0=rk[:, :].rearrange("p (h n) -> p h n", h=HEADS), scalar=K_SCALE,
                                                       in1=dcol[:, r, :, 2:3].to_broadcast([P, HEADS, HD]),
                                                       op0=ALU.mult, op1=ALU.mult)
                        if r == 1:
                            ins.then_inc(k_decayed_ready, 1)
                            dve.wait_ge(k_decayed_ready, nth("k_decayed", m))
                    dve.wait_ge(bank_filled[slot("st", m)], use("st", m))
                for t in TILES[m]:
                    i, _ = tok(m, t)
                    o = o_tok[:, i, :].rearrange("p (h n) -> p h n", h=HEADS)
                    sq = xn[:, 512:768].rearrange("p (h n) -> p h n", h=HEADS)

                    def per_head(v):
                        return v.unsqueeze(2).to_broadcast([P, HEADS, HD])

                    dve.tensor_reduce(stat[:, 20:24], o, AX, ALU.add).then_inc(dve_done, counted())
                    dve.wait_ge(dve_done, steps[0])
                    dve.tensor_scalar(stat[:, 20:24], stat[:, 20:24], 1.0 / HD, None, ALU.mult).then_inc(dve_done, counted())
                    dve.wait_ge(dve_done, steps[0])
                    dve.tensor_tensor(o, o, per_head(stat[:, 20:24]), ALU.subtract).then_inc(dve_done, counted())
                    dve.wait_ge(dve_done, steps[0])
                    dve.tensor_tensor(sq, o, o, ALU.mult).then_inc(dve_done, counted())
                    dve.wait_ge(dve_done, steps[0])
                    dve.tensor_reduce(stat[:, 24:28], sq, AX, ALU.add).then_inc(dve_done, counted())
                    dve.wait_ge(dve_done, steps[0])
                    rstd(stat[:, 28:32], ("ret", t))
                    dve.tensor_tensor(o, o, per_head(stat[:, 28:32]), ALU.mult).then_inc(dve_done, counted())
                    dve.wait_ge(dve_done, steps[0])
                    dve.tensor_tensor(o_tok[:, i, :], o_tok[:, i, :], rv[:, i, 1, :], ALU.mult).then_inc(ret_out_ready, 1)
                    dve.wait_ge(ret_out_ready, nth("ret_out", t))

            def out(m):
                for b in range(2):
                    dve.wait_ge(gate_ready, nth("gate", (1, m, b)))
                    hb = slice(512 * b, 512 * b + 512)
                    for t in TILES[m]:
                        key = ("mix", t, b)
                        dve.wait_ge(bank_filled[slot(*key)], use(*key))
                        ps = psum[slot(*key)]
                        dve.tensor_tensor(xn[:, hb], ps[:, :], gate_row[:, hb], ALU.mult).then_inc(bank_free[slot(*key)], 1)
                        dve.wait_ge(bank_free[slot(*key)], use(*key) + 1)
                        ins = dve.tensor_tensor(x[:, XBUF[t], hb], x[:, XBUF[t], hb], xn[:, hb], ALU.add)
                        if b:
                            ins.then_inc(mixed_ready, 1)
                            dve.wait_ge(mixed_ready, nth("mixed", t))
                        else:
                            ins.then_inc(dve_done, counted())
                            dve.wait_ge(dve_done, steps[0])

            def best16(vals, idx, src):
                n = len(src)
                for k in range(n):
                    dve.max(vals[k][:, 0:8], src[k]).then_inc(dve_done, counted())
                dve.wait_ge(dve_done, steps[0])
                for k in range(n):
                    dve.max_index(idx[k][:, 0:8], vals[k][:, 0:8], src[k]).then_inc(dve_done, counted())
                dve.wait_ge(dve_done, steps[0])
                for k in range(n):
                    dve.match_replace(src[k], vals[k][:, 0:8], src[k], LOWEST).then_inc(dve_done, counted())
                dve.wait_ge(dve_done, steps[0])
                for k in range(n):
                    dve.max(vals[k][:, 8:16], src[k]).then_inc(dve_done, counted())
                dve.wait_ge(dve_done, steps[0])
                for k in range(n):
                    dve.max_index(idx[k][:, 8:16], vals[k][:, 8:16], src[k]).then_inc(dve_done, counted())
                dve.wait_ge(dve_done, steps[0])

            def topk(t):
                l = LAYER[M_OF[t]]
                for b in range(4):
                    dve.wait_ge(scores_ready, nth("scores", (t, b)))
                best16([tv[:, k, :] for k in range(16)], [ti[:, k, :] for k in range(16)],
                       [s_sb[:, N_KEYS * k:N_KEYS * k + N_KEYS] for k in range(16)])
                tvh = tv[:, :, :].rearrange("p (q h) k -> p h q k", q=2)
                dve.tensor_tensor(cand.rearrange("p (h i j) -> p h i j", h=PEER_H, i=TOPK),
                                       tvh[:, :, 0, :].unsqueeze(3).to_broadcast([P, PEER_H, TOPK, TOPK]),
                                       tvh[:, :, 1, :].unsqueeze(2).to_broadcast([P, PEER_H, TOPK, TOPK]), ALU.add).then_inc(dve_done, counted())
                dve.wait_ge(dve_done, steps[0])
                best16([cv[:, h, :] for h in range(PEER_H)], [sel[:, h, :] for h in range(PEER_H)],
                       [cand[:, 256 * h:256 * h + 256] for h in range(PEER_H)])
                dve.tensor_copy(stat[:, 32:40], cv[:, :, 0]).then_inc(dve_done, counted())
                dve.wait_ge(dve_done, steps[0])
                dve.tensor_tensor(cv[:, :, :], cv[:, :, :], stat[:, 32:40].unsqueeze(2).to_broadcast([P, PEER_H, TOPK]),
                                      ALU.subtract).then_inc(gate_arg_ready, 1)
                dve.wait_ge(gate_arg_ready, nth("gate_arg", t))
                dve.tensor_copy(tif[:, :, :], ti[:, :, :]).then_inc(dve_done, counted())
                sf = sel[:, :, :].rearrange("p h k -> p (h k)")
                dve.tensor_scalar(sel2[:, 0, :], sf, 4, None, ALU.logical_shift_right).then_inc(dve_done, counted())
                dve.tensor_scalar(sel2[:, 1, :], sf, 15, None, ALU.bitwise_and).then_inc(dve_done, counted())
                dve.wait_ge(dve_done, steps[0])
                dve.tensor_copy(self_[:, :, :], sel2[:, :, :]).then_inc(dve_done, counted())
                dve.wait_ge(dve_done, steps[0])
                tih = tif[:, :, :].rearrange("p (q h) k -> p h q k", q=2)
                hot = s_sb.rearrange("p (n j) -> p n j", j=TOPK)
                hot4 = s_sb.rearrange("p (h k j) -> p h k j", h=PEER_H, k=TOPK)
                for q in range(2):
                    dve.tensor_tensor(hot, self_[:, q, :].unsqueeze(2).to_broadcast([P, PICKS, TOPK]),
                                           iota16[:, :].unsqueeze(1).to_broadcast([P, PICKS, TOPK]), ALU.is_equal).then_inc(dve_done, counted())
                    dve.wait_ge(dve_done, steps[0])
                    dve.tensor_tensor(hot4, hot4, tih[:, :, q, :].unsqueeze(2).to_broadcast([P, PEER_H, TOPK, TOPK]), ALU.mult).then_inc(dve_done, counted())
                    dve.wait_ge(dve_done, steps[0])
                    dve.tensor_reduce(e12[:, q, :], hot, AX, ALU.add).then_inc(dve_done, counted())
                    dve.wait_ge(dve_done, steps[0])
                dve.tensor_scalar(e12[:, 0, :], e12[:, 0, :], float(N_KEYS), float(l * EXPERTS), ALU.mult, ALU.add).then_inc(dve_done, counted())
                dve.wait_ge(dve_done, steps[0])
                dve.tensor_tensor(eidx[:, t % 2, :], e12[:, 0, :], e12[:, 1, :], ALU.add).then_inc(dve_done, counted())
                dve.wait_ge(dve_done, steps[0])
                dve.wait_ge(gate_exp_ready, nth("gate_exp", t))
                dve.tensor_reduce(stat[:, 40:48], cv[:, :, :], AX, ALU.add).then_inc(dve_done, counted())
                dve.wait_ge(dve_done, steps[0])
                dve.reciprocal(stat[:, 40:48], stat[:, 40:48]).then_inc(dve_done, counted())
                dve.wait_ge(dve_done, steps[0])
                dve.tensor_tensor(gates[:, t % 2, :].rearrange("p (h k) -> p h k", h=PEER_H), cv[:, :, :],
                                      stat[:, 40:48].unsqueeze(2).to_broadcast([P, PEER_H, TOPK]), ALU.mult).then_inc(picked_ready, 1)
                dve.wait_ge(picked_ready, nth("picked", t))

            def peer(t):
                if t == 0:
                    dve.sem_inc(u_free, SLOTS)
                for b in range(2):
                    dve.wait_ge(h2_ready, nth("h2", (t, b)))
                with dve.Fori(0, NG) as i:
                    for r in range(G):
                        dve.wait_ge(u_landed[r], i * 16 + 16 * (NG * t + 1))
                        dve.tensor_tensor_reduce(ubuf[:, r, :], ubuf[:, r, :], h2[:, XBUF[t], :], 1.0, 0.0, ALU.mult, ALU.add,
                                                 dot[:, r:r + 1]).then_inc(u_free, 1)
                    dve.wait_ge(gelu_done, i + (NG * t + 1))
                    dve.tensor_tensor(coef[:, :], act_dot[:, :], gates[:, t % 2, bass.ts(i, G)], ALU.mult).then_inc(coef_done, 1)
                dve.wait_ge(v_free, SLOTS + PICKS * (t + 1))
                if t >= 4:
                    dve.wait_ge(y_stored, 16 * (t - 3))
                for b in range(2):
                    dve.wait_ge(gate_ready, nth("gate", (2, t, b)))
                    hb = slice(512 * b, 512 * b + 512)
                    dve.tensor_tensor(xn[:, hb], ysum[:, b, :], gate_row[:, hb], ALU.mult).then_inc(dve_done, counted())
                    dve.wait_ge(dve_done, steps[0])
                    ins = dve.tensor_tensor(x[:, XBUF[t], hb], x[:, XBUF[t], hb], xn[:, hb], ALU.add)
                    if b:
                        ins.then_inc(updated_ready, 1)
                        dve.wait_ge(updated_ready, nth("updated", t))
                    else:
                        ins.then_inc(dve_done, counted())
                        dve.wait_ge(dve_done, steps[0])
                if t >= 3:
                    xt = x[:, XBUF[t], :]
                    dve.tensor_tensor_reduce(xn[:, :], xt, xt, 1.0, 0.0, ALU.mult, ALU.add, stat[:, 0:1]).then_inc(dve_done, counted())
                    dve.wait_ge(dve_done, steps[0])
                    rstd(stat[:, 1:2], ("final", t))
                    dve.scalar_tensor_tensor(out=xn[:, :], in0=xt, scalar=stat[:, 1:2], in1=normf[:, :],
                                                 op0=ALU.mult, op1=ALU.mult).then_inc(final_ready, 1)
                    dve.wait_ge(final_ready, nth("final", t))

            for kind, *n in SCHEDULE:
                if kind == "start":
                    start(*n)
                elif kind == "mods":
                    mods(*n)
                elif kind == "decay":
                    decay_(*n)
                elif kind == "ln":
                    ln(*n)
                elif kind == "in":
                    project(*n)
                elif kind == "mla":
                    mla(*n)
                elif kind == "conv":
                    conv(*n)
                elif kind == "ret":
                    ret(*n)
                elif kind == "out":
                    out(*n)
                elif kind == "topk":
                    topk(*n)
                elif kind == "peer":
                    peer(*n)

        @block.gpsimd
        def _(pool):
            def peer(t):
                pool.wait_ge(picked_ready, nth("picked", t))
                picks = eidx[:, t % 2, :]

                def stage_idx(idx, g, n):
                    pool.tensor_copy(idx, picks[:, bass.ts(g, G)]).then_inc(idx_staged, 1)
                    pool.wait_ge(idx_staged, n)
                    pool.sem_inc(pool_order, 1)

                def gather(rows, buf, idx, landed, free, k, r):
                    pool.wait_ge(free, k)
                    pool.sem_inc(pool_order, 1)
                    pool.indirect_dma_start(buf[:, r, :], None, rows, bass.IndirectOffsetOnAxis(idx[:, r:r + 1], 0))\
                        .then_inc(landed[r], 16)

                K = PICKS * t
                N = 2 * NG * t

                def u_group(g, q):
                    for r in range(G):
                        gather(u_rows, ubuf, uidx[:, q, :], u_landed, u_free, g * G + (K + r + 1), r)

                def both(g, q):
                    stage_idx(uidx[:, q, :], g, g * 2 + N)
                    stage_idx(vidx[:, 1 - q, :], g - 1, g * 2 + (N + 1))
                    for r in range(G):
                        gather(u_rows, ubuf, uidx[:, q, :], u_landed, u_free, g * G + (K + r + 1), r)
                        gather(v_rows, vbuf, vidx[:, 1 - q, :], v_landed, v_free, g * G + (K - G + r + 1), r)

                stage_idx(uidx[:, 0, :], 0, N + 1)
                u_group(0, 0)
                with pool.Fori(0, NG // 2 - 1) as i:
                    both(i * 2 + 1, 1)
                    both(i * 2 + 2, 0)
                both(NG - 1, 1)
                stage_idx(vidx[:, 1, :], NG - 1, N + 2 * NG)
                for r in range(G):
                    gather(v_rows, vbuf, vidx[:, 1, :], v_landed, v_free, K + PICKS - G + r + 1, r)

            for kind, *args in SCHEDULE:
                if kind == "peer":
                    peer(*args)


def shape_constants():
    f = np.float32
    u = np.arange(3 * P)[None, :] - P - np.arange(P)[:, None]
    rel = np.stack([np.maximum(u, 0), np.maximum(-u, 0)], 1).astype(f)
    p = np.arange(P)
    fwd = np.stack([p + 1, p + P + 1, P - 1 - p], 1)
    bwd = np.stack([DEC - p, DEC - P - p, p], 1)
    pos3 = np.stack([fwd, bwd], 1).astype(f)
    pairs = ROPE // 4
    inv = (np.float32(10000.0) ** (-np.arange(pairs, dtype=f) / pairs)).astype(f)
    t = np.arange(DEC)
    ar = (t // GRID_W).astype(f)[:, None] * inv
    ac = (t % GRID_W).astype(f)[:, None] * inv
    ang = np.concatenate([ar, ar, ac, ac], -1)
    sign = np.repeat(np.array([-1, 1, -1, 1], f), pairs)
    rope = np.stack([np.cos(ang), np.sin(ang) * sign], 1).astype(f)
    rope = rope.reshape(2, P, 2, ROPE).transpose(1, 0, 2, 3)

    def window(L):
        out = np.zeros((L, 4, L), f)
        q = np.arange(L)
        for g, w in enumerate(WINDOWS):
            lo, hi = np.clip(q - w // 2, 0, L), np.clip(q + w // 2, 0, L)
            k = np.arange(L)[:, None]
            out[:, g, :] = ((k >= lo) & (k < hi)) / (hi - lo).astype(f) - (k == q)
        return out

    ws = window(DEC)
    band = np.stack([window(SEQ), ws[0:P, :, 0:P], ws[P:, :, P:]], 1)
    edge = np.stack([ws[P:, :, P - 8:P], ws[0:P, :, P:P + 8]], 1)
    return {"ident": np.eye(P, dtype=f), "iota16": np.arange(TOPK, dtype=f), "rel": rel, "pos3": pos3,
            "rope": np.ascontiguousarray(rope), "band": band, "edge": edge}


_OUTS = [((1, SEQ, D), "float32"), ((1, DEC, D), "float32"), ((1, DEPTH, SEQ, KV_LORA), "float32"),
         ((1, DEPTH, SEQ, ROPE), "float32"), ((1, DEPTH, 2, HEADS, HD, HD), "float32")]
_INS = ["x_prompt", "x_sample", "cache_mla_ckv", "cache_mla_krope", "state_ret", "c", "c_ctx", "w_mod", "b_mod", "norm1",
        "norm2", "w_in", "conv_w", "mla_q_norm", "mla_w_uq", "mla_kv_norm", "mla_w_uk", "mla_w_uv", "ret_decay_logit",
        "pool_w", "pool_scale", "w_out", "peer_w_q", "peer_subkeys", "peer_u", "peer_v", "norm_f"]


def kernel(**inputs):
    import concourse.bacc as _bacc
    from concourse.bass_utils import run_bass_kernel_spmd as _run

    nc = _bacc.Bacc("TRN2", target_bir_lowering=False, num_devices=1)
    arrays = {}

    def declare(prefix, named):
        aps = {}
        for name, v in named.items():
            v = np.ascontiguousarray(v)
            arrays[f"{prefix}_{name}_dram"] = v
            aps[name] = nc.dram_tensor(f"{prefix}_{name}_dram", v.shape, mybir.dt.from_np(v.dtype), kind="ExternalInput").ap()
        return aps

    ins = declare("in", {name: inputs[name] for name in _INS})
    consts = declare("shape", shape_constants())
    outs = [nc.dram_tensor(f"out_{i}_dram", shape, mybir.dt.from_np(np.dtype(dt)), kind="ExternalOutput").ap()
            for i, (shape, dt) in enumerate(_OUTS)]
    hybrid_step(nc, ins, consts, outs)
    r = _run(nc, [arrays], core_ids=[0])
    return tuple(r.results[0][f"out_{i}_dram"] for i in range(len(_OUTS)))
```

```python
from contextlib import ExitStack

import numpy as np

import concourse.bass as bass
from concourse import mybir

F32 = mybir.dt.float32
U32 = mybir.dt.uint32
ALU = mybir.AluOpType
ACT = mybir.ActivationFunctionType
AX = mybir.AxisListType.X

P = 128
D = 1024
DC = D // P
DEPTH = 2
SEQ = 128
DEC = 256
PAST = 128
GROUP_W = D // 4
HD = 64
HEADS = GROUP_W // HD
ROPE = HD // 2
QK = HD + ROPE
Q_LORA = D // 4
KV_LORA = D // 8
GRID_W = 64
WINDOWS = (2, 4, 8, 16)
EPS = 1e-6
SM_SCALE = float(QK) ** -0.5
K_SCALE = float(HD) ** -0.5
OFF_MLA = 3 * GROUP_W
OFF_RET = OFF_MLA + Q_LORA + KV_LORA + ROPE
OFF_POOL = OFF_RET + 4 * GROUP_W
LAT = Q_LORA + KV_LORA + ROPE
PEER_H = 8
N_KEYS = 128
EXPERTS = N_KEYS * N_KEYS
TOPK = 16
PICKS = PEER_H * TOPK
LOWEST = -3.0e38

G = 4
SLOTS = G
NG = PICKS // G
DIAGS = 4
GAP_US = 6

TILES = [[0], [1, 2], [3], [4, 5]]
STREAM = [0, 1, 0, 1]
LAYER = [0, 0, 1, 1]
M_OF = [0, 1, 1, 2, 3, 3]
XBUF = [0, 1, 2, 0, 1, 2]

SH1, SC1, G1, SH2, SC2, G2 = range(6)


def nk_of(m):
    return 1 if STREAM[m] == 0 else 3


def beats(stage):
    kind, *a = stage
    if kind == "start":
        return [(1, [("vec",)])]
    if kind == "modrow":
        return [(7, [("modrow", *a)])]
    if kind == "modcol":
        return [(1, [("modcol", *a)])]
    if kind == "modscale":
        return [(1, [])]
    if kind == "keys":
        return [(2, [("sk", a[0], b) for b in range(2)])]
    if kind == "decay":
        return [(6, [])]
    if kind == "ln":
        got = [(4, []), (3, [("xnT", *a, b) for b in range(2)])]
        return got + ([(3, [("h2tok", a[1], b) for b in range(2)])] if a[0] == 2 else [])
    if kind == "score":
        return [(4, [("s", a[0], b) for b in range(4)])]
    if kind == "topk":
        return [(1.5, [])] * 15
    if kind == "finish":
        return [(4, [("gate", 2, a[0], b) for b in range(2)])] + ([(4, [])] if a[0] >= 3 else [])
    m = a[0]
    ts, nt = TILES[m], len(TILES[m])
    if kind == "in":
        got = [(6, [("zm", t)]) for t in ts] + [(1.7 * nt, [("a", m, f)]) for f in range(6)]
        got += [(3.4, [("zp", t)]) for t in ts] + [(1.7 * nt, [("rqk", m, f)]) for f in range(4)]
        got += [(3.4, [("rk", m)])] if STREAM[m] == 0 else []
        return got + [(7, [("rvg", t)]) for t in ts]
    if kind == "mla":
        got = [(3, [])] * nt
        got += [(2, ([("ctxT", m)] if STREAM[m] and t == ts[0] else []) + [("latT", t)]) for t in ts]
        for t in ts:
            got += [(3, [("q", t)]), (2, [("qT", t)])]
        got += [(4, [("kT", m, h) for h in range(HEADS)]), (2, [("v", m, k) for k in range(nk_of(m))])]
        for t in ts:
            got += [(5, [("sc", t, h) for h in range(HEADS)]), (4, [])]
            got += [(2, [("pT", t, 2 * p), ("pT", t, 2 * p + 1), ("o", t, p)]) for p in range(2)]
        return got
    if kind == "conv":
        return [(4, [])]
    if kind == "ret":
        got = [(1, [("inn", m, 0, i) for i in range(nt)])]
        for h in range(HEADS):
            got.append((2, [("inn", m, h + 1, i) for i in range(nt) if h + 1 < HEADS] + [("oh", m, h)]))
        got += [(1, []), (2, [("st", m)])] if STREAM[m] == 0 else []
        for t in ts:
            got += [(2, []), (1, [("yrT", t)])]
        return got
    if kind == "pool":
        return [(3, [("pl", m, b) for b in range(2)]), (2, [("plo", m, b) for b in range(2)])]
    if kind == "out":
        return [(4, [("gate", 1, m, b) for b in range(2)])] + [(8, [("mix", t, b)]) for b in range(2) for t in ts]
    assert kind == "q"
    return [(1.7 * nt, [("qp", m, h)]) for h in range(PEER_H)]


def weight_blocks(stage):
    kind, *a = stage
    if kind == "modrow":
        yield ("w_mod", a[0], [(512 * a[1], 512)], ("modrow", *a))
    elif kind == "in":
        m = a[0]
        last = TILES[m][-1]
        yield ("w_in", LAYER[m], [(OFF_MLA, LAT)], ("zm", last))
        yield ("w_in", LAYER[m], [(0, 512)], ("a", m, 3))
        yield ("w_in", LAYER[m], [(512, GROUP_W), (OFF_POOL, GROUP_W)], ("zp", last))
        yield ("w_in", LAYER[m], [(OFF_RET, 512)], ("rk", m) if STREAM[m] == 0 else ("rqk", m, 3))
        yield ("w_in", LAYER[m], [(OFF_RET + 512, 512)], ("rvg", last))
    elif kind == "out":
        for b in range(2):
            yield ("w_out", LAYER[a[0]], [(512 * b, 512)], ("mix", TILES[a[0]][-1], b))
    elif kind == "q":
        for b in range(2):
            yield ("peer_w_q", LAYER[a[0]], [(512 * b, 512)], ("qp", a[0], 4 * b + 3))


def announced(stage):
    kind, *a = stage
    if kind == "start":
        yield from [("cond", 0), ("abs_logit", 0), ("log1p", 0), ("decay_log", 0)]
    elif kind == "modrow":
        yield ("mrow", tuple(a))
    elif kind == "modscale":
        yield ("mods", tuple(a))
    elif kind == "keys":
        yield ("sk", a[0])
    elif kind == "decay":
        yield from (("decay_arg", (a[0], h)) for h in range(HEADS))
        yield from (("decay_exp", (a[0], h)) for h in range(HEADS))
        yield from (("decay_col", (a[0], i)) for i in range(2 * HEADS))
    elif kind == "ln":
        yield ("sumsq", ("ln", *a))
        yield ("std", ("ln", *a))
        yield ("xn", tuple(a))
        yield ("hT", tuple(a))
        if a[0] == 2:
            yield from (("h2", (a[1], b)) for b in range(2))
    elif kind == "in":
        m = a[0]
        yield ("za", m)
        yield ("rqk", m)
        for t in TILES[m]:
            yield ("zp", t)
            yield ("rvg", t)
    elif kind == "mla":
        m = a[0]
        if STREAM[m] == 1:
            yield ("ctxT", m)
        for t in TILES[m]:
            yield ("sumsq", ("mla", t))
            yield ("std", ("mla", t))
            yield ("lat", t)
            yield ("latT", t)
            yield ("qtok", t)
            yield ("qT", t)
            yield ("row_max", t)
            yield ("probs", t)
            yield from (("pT", (t, h)) for h in range(HEADS))
            yield from (("y_mla", (t, p)) for p in range(2))
        yield from (("kT", (m, h)) for h in range(HEADS))
        yield from (("v", (m, k)) for k in range(nk_of(m)))
    elif kind == "conv":
        yield ("y_conv", a[0])
    elif kind == "ret":
        m = a[0]
        if STREAM[m] == 0:
            yield ("k_decayed", m)
            yield ("state", m)
        for t in TILES[m]:
            yield ("sumsq", ("ret", t))
            yield ("std", ("ret", t))
            yield ("ret_out", t)
            yield ("y_ret", t)
    elif kind == "pool":
        for p in range(2):
            yield ("pooled", (a[0], p))
            yield ("y_pool", (a[0], p))
    elif kind == "out":
        yield from (("gate", (1, a[0], b)) for b in range(2))
        yield from (("mixed", t) for t in TILES[a[0]])
    elif kind == "q":
        yield from (("qp", (a[0], h)) for h in range(PEER_H))
    elif kind == "score":
        yield from (("scores", (a[0], b)) for b in range(4))
    elif kind == "topk":
        yield from [("gate_arg", a[0]), ("gate_exp", a[0]), ("picked", a[0])]
    elif kind == "finish":
        yield from (("gate", (2, a[0], b)) for b in range(2))
        yield ("updated", a[0])
        if a[0] >= 3:
            yield ("sumsq", ("final", a[0]))
            yield ("std", ("final", a[0]))
            yield ("final", a[0])


def mod_stages(l, js):
    return [(kind, l, j) for j in js for kind in ("modrow", "modcol")]


def mixers(m):
    return [("mla", m), ("conv", m), ("ret", m), ("pool", m)]


def choose(t):
    return [("score", t), ("topk", t)]


def schedule():
    def beats_of(stages):
        return [(w, (stage, i)) for stage in stages for i, (w, _) in enumerate(beats(stage))]

    def side_by_side(stages, others):
        main, side = beats_of(stages), beats_of(others)
        total, n, at, got = sum(w for w, _ in main), len(side), 0, []
        for w, beat in main:
            got.append(beat)
            at += w
            while side and n - len(side) < n * at / total:
                got.append(side.pop(0)[1])
        return got + [beat for _, beat in side]

    def along(t, stages):
        work = beats_of(stages)
        total = sum(w for w, _ in work)
        gaps = 1
        while gaps < NG and total / gaps > GAP_US:
            gaps *= 2
        got, at, n = [], 0, NG // gaps
        for gap in range(gaps):
            while work and (at * gaps < total * (gap + 1) or gap == gaps - 1):
                at += work[0][0]
                got.append(work.pop(0)[1])
            got.append(("groups", t, gap * n, gap * n + n))
        return got

    order = [beat for _, beat in beats_of([("start", 0)] + mod_stages(0, range(4)) + [("modscale", 0, 1), ("ln", 1, 0)])]
    order += side_by_side([("in", 0)], [("decay", 0), ("keys", 0)])
    order += side_by_side(mixers(0), mod_stages(0, range(4, 10)) + [("modscale", 0, 2)])
    order += [beat for _, beat in beats_of([("out", 0), ("ln", 2, 0), ("q", 0)] + choose(0))]
    order += along(0, [("ln", 1, 1), ("ln", 1, 2), ("in", 1)] + mixers(1) + [("out", 1), ("ln", 2, 1), ("ln", 2, 2), ("q", 1)]
                   + choose(1) + mod_stages(0, range(10, 12)))
    order += along(1, [("finish", 0)] + choose(2) + mod_stages(1, range(12))
                   + [("modscale", 1, 1), ("modscale", 1, 2), ("keys", 1), ("decay", 1)])
    order += along(2, [("finish", 1), ("ln", 1, 3), ("in", 2)] + mixers(2) + [("out", 2), ("ln", 2, 3), ("q", 2)] + choose(3))
    order += along(3, [("finish", 2), ("ln", 1, 4), ("ln", 1, 5), ("in", 3)] + mixers(3)
                   + [("out", 3), ("ln", 2, 4), ("ln", 2, 5), ("q", 3)] + choose(4))
    order += along(4, [("finish", 3)] + choose(5))
    order += along(5, [("finish", 4)])
    order += [beat for _, beat in beats_of([("finish", 5)])]
    return order


def plan():
    ring = 6
    order = schedule()
    bank, blocks, value, total, before = {}, [], {}, {}, {}
    n, last_gate = 0, None
    for what, i, *_ in order:
        if what == "groups":
            continue
        for key in beats(what)[i][1]:
            bank[key] = (n % ring, n // ring)
            n += 1
        if i == 0:
            blocks += list(weight_blocks(what))
            for name, key in announced(what):
                total[name] = total.get(name, 0) + 1
                value[name, key] = total[name]
            if what[0] in ("out", "finish"):
                before[what] = last_gate
                last_gate = what
    blocks.sort(key=lambda b: bank[b[3]][1] * ring + bank[b[3]][0])
    return ring, order, bank, blocks, value, total, before


def hybrid_step(nc, a, c, outs):
    y_prompt, y_sample, new_ckv, new_krope, new_state = outs
    RING, ORDER, BANK, BLOCKS, VALUE, TOTAL, GATE_BEFORE = plan()
    WSLOTS = 2
    block_at = {}
    for n, (what, layer, cols, last) in enumerate(BLOCKS):
        block_at[what, layer, last] = n
    landed_at, per_slot = [], [0] * WSLOTS
    for n, (_, _, cols, _) in enumerate(BLOCKS):
        per_slot[n % WSLOTS] += 16 * len(cols)
        landed_at.append(per_slot[n % WSLOTS])

    with ExitStack() as ctx:
        def sb(name, shape, dt=F32):
            return ctx.enter_context(nc.sbuf_tensor(name, shape, dt))

        def sem(name):
            return ctx.enter_context(nc.semaphore(name))

        ident = sb("ident", [P, P])
        iota16 = sb("iota16", [P, TOPK])
        rel = sb("rel", [P, 2, 3 * P])
        pos3 = sb("pos3", [P, 2, 3])
        cs = sb("cs", [P, 2, 2, ROPE])
        band = sb("band", [P, 3, 4, P])
        edge = sb("edge", [P, 2, 4, 8])
        VC = 68
        cols = sb("cols", [P, VC + 96])
        cond = sb("cond", [P, 2, DC])
        logit = sb("logit", [P, 4, 16])
        kvn = sb("kvn", [P, KV_LORA])
        w_uq = sb("w_uq", [P, 2, HEADS * QK])
        w_ukv = sb("w_ukv", [P, 2, GROUP_W])
        w_pool = sb("w_pool", [P, 2, HD])
        s0 = sb("s0", [P, 2, 2 * HD])
        ctx_ckv = sb("ctx_ckv", [P, KV_LORA])
        ctx_kr = sb("ctx_kr", [P, ROPE])
        normf = sb("normf", [P, D])
        skT = sb("skT", [P, PEER_H, N_KEYS])
        modc = sb("modc", [P, DEPTH, 48, 2])
        moda = sb("moda", [P, DEPTH, 2, 2, DC])
        decay = sb("decay", [P, HEADS, 3 * P])
        dcol = sb("dcol", [P, 2, HEADS, 3])
        x = sb("x", [P, 3, D])
        h2 = sb("h2", [P, 3, D])
        hT = sb("hT", [P, DC, DEC])
        yT = hT
        xn = sb("xn", [P, D])
        gate_row = sb("gate_row", [P, D])
        wring = sb("wring", [P, WSLOTS, DC, 512])
        mrow = sb("mrow", [2, 2, 512])
        za = sb("za", [P, 6, DEC])
        rqk = sb("rqk", [P, 4, DEC])
        zm = sb("zm", [P, 2, LAT])
        zp = sb("zp", [P, 2, GROUP_W])
        rv = sb("rv", [P, 2, 2, GROUP_W])
        scratch = sb("scratch", [P, 6144])
        at = [0]

        def part(n):
            at[0] += n
            return scratch[:, at[0] - n:at[0]]

        lat = part(2 * 384).rearrange("p (i n) -> p i n", i=2)
        q_tok = part(384)
        qlT = part(512).rearrange("p (k n) -> p k n", k=2)
        ckvT = part(384)
        qT = part(1024).rearrange("p (h n) -> p h n", h=4)
        kT = part(4 * 384).rearrange("p (h n) -> p h n", h=4)
        vtok = part(768).rearrange("p (k n) -> p k n", k=3)
        pooled = part(512).rearrange("p (b n) -> p b n", b=2)
        rk = part(256)
        assert at[0] <= 6144, at[0]
        at[0] = 0
        s_sb = part(2048)
        cand = part(2048)
        tv = part(256).rearrange("p (n k) -> p n k", k=TOPK)
        ti = part(256).bitcast(U32).rearrange("p (n k) -> p n k", k=TOPK)
        tif = part(256).rearrange("p (n k) -> p n k", k=TOPK)
        cv = part(128).rearrange("p (n k) -> p n k", k=TOPK)
        sel = part(128).bitcast(U32).rearrange("p (n k) -> p n k", k=TOPK)
        sel2 = part(256).bitcast(U32).rearrange("p (q n) -> p q n", q=2)
        self_ = part(256).rearrange("p (q n) -> p q n", q=2)
        e12 = part(256).rearrange("p (q n) -> p q n", q=2)
        assert at[0] <= 6144, at[0]
        vec_rows = scratch[0:96, 0:2 * P].rearrange("p (r n) -> p r n", r=2)
        qpT = sb("qpT", [P, PEER_H, DEC])
        shared = qpT[:, :, :].rearrange("p h n -> p (h n)")
        probs = shared[:, 0:4 * 384].rearrange("p (h n) -> p h n", h=4)
        pT = sb("pT", [P, 2, 384])
        krr = sb("krr", [P, 2, ROPE])
        stat = sb("stat", [P, 64])
        inn = sb("inn", [P, 2, 2, DEC])
        o_tok = sb("o_tok", [P, 2, GROUP_W])
        state_out = inn[0:HD, 0, :, :].rearrange("p i n -> p (i n)")
        eidx = sb("eidx", [P, 2, PICKS], U32)
        gates = sb("gates", [P, 2, PICKS])
        ubuf = sb("ubuf", [P, SLOTS, D])
        vbuf = sb("vbuf", [P, SLOTS, D])
        uidx = sb("uidx", [P, 2, G], U32)
        vidx = sb("vidx", [P, 2, G], U32)
        dot = sb("dot", [P, G])
        act_dot = sb("act_dot", [P, G])
        coef = sb("coef", [P, G])
        diag = sb("diag", [P, DIAGS, P])

        psum = [ctx.enter_context(nc.psum_tensor(f"bank{i}", [P, 512], F32)) for i in range(RING)]
        ysum = ctx.enter_context(nc.psum_tensor("ysum", [P, 2, 512], F32))

        bank_filled = [sem(f"bank_filled{i}") for i in range(RING)]
        bank_free = [sem(f"bank_free{i}") for i in range(RING)]
        cond_ready = sem("cond_ready")
        abs_logit_ready = sem("abs_logit_ready")
        log1p_ready = sem("log1p_ready")
        decay_log_ready = sem("decay_log_ready")
        mrow_ready = sem("mrow_ready")
        mods_ready = sem("mods_ready")
        sk_ready = sem("sk_ready")
        decay_arg_ready = sem("decay_arg_ready")
        decay_exp_ready = sem("decay_exp_ready")
        decay_col_ready = sem("decay_col_ready")
        sumsq_ready = sem("sumsq_ready")
        std_ready = sem("std_ready")
        xn_ready = sem("xn_ready")
        hT_ready = sem("hT_ready")
        za_ready = sem("za_ready")
        rqk_ready = sem("rqk_ready")
        zp_ready = sem("zp_ready")
        rvg_ready = sem("rvg_ready")
        lat_ready = sem("lat_ready")
        latT_ready = sem("latT_ready")
        qtok_ready = sem("qtok_ready")
        qT_ready = sem("qT_ready")
        row_max_ready = sem("row_max_ready")
        probs_ready = sem("probs_ready")
        pT_ready = sem("pT_ready")
        y_mla_ready = sem("y_mla_ready")
        kT_ready = sem("kT_ready")
        v_ready = sem("v_ready")
        y_conv_ready = sem("y_conv_ready")
        k_decayed_ready = sem("k_decayed_ready")
        state_ready = sem("state_ready")
        ret_out_ready = sem("ret_out_ready")
        y_ret_ready = sem("y_ret_ready")
        pooled_ready = sem("pooled_ready")
        y_pool_ready = sem("y_pool_ready")
        gate_ready = sem("gate_ready")
        mixed_ready = sem("mixed_ready")
        h2_ready = sem("h2_ready")
        qp_ready = sem("qp_ready")
        scores_ready = sem("scores_ready")
        gate_arg_ready = sem("gate_arg_ready")
        gate_exp_ready = sem("gate_exp_ready")
        picked_ready = sem("picked_ready")
        updated_ready = sem("updated_ready")
        ctxT_ready = sem("ctxT_ready")
        final_ready = sem("final_ready")
        w_landed = [sem(f"w_landed{i}") for i in range(WSLOTS)]
        small_landed = sem("small_landed")
        x_landed = sem("x_landed")
        rows_landed = sem("rows_landed")
        keys_landed = sem("keys_landed")
        layer_landed = sem("layer_landed")
        cache_stored = sem("cache_stored")
        state_stored = sem("state_stored")
        y_stored = sem("y_stored")
        dve_done = sem("dve_done")
        act_done = sem("act_done")
        idx_staged = sem("idx_staged")
        pool_order = sem("pool_order")
        u_landed = [sem(f"u_landed{i}") for i in range(SLOTS)]
        v_landed = [sem(f"v_landed{i}") for i in range(SLOTS)]
        u_free = sem("u_free")
        v_free = sem("v_free")
        gelu_done = sem("gelu_done")
        coef_done = sem("coef_done")
        diag_built = sem("diag_built")

        kr_dram = a["cache_mla_krope"]
        u_rows = a["peer_u"].rearrange("l e d -> (l e) d")
        v_rows = a["peer_v"].rearrange("l e d -> (l e) d")

        def slot(*key):
            return BANK[key][0]

        def use(*key):
            return BANK[key][1] + 1

        def nth(name, key):
            return VALUE[name, key]

        def beat_of(i, stage, running, body, *args):
            if i == 0:
                running[stage] = body(*args)
            if running[stage] is None:
                assert len(beats(stage)) == 1, stage
            else:
                assert next(running[stage], "over") is None, stage
                if i == len(beats(stage)) - 1:
                    assert next(running[stage], "over") == "over", stage

        def tok(m, t):
            i = TILES[m].index(t)
            return i, slice(P * i, P * i + P)

        SMALL = []
        SMALL.append((ident[:, :], c["ident"]))
        SMALL.append((iota16[:, :], c["iota16"].partition_broadcast(P)))
        SMALL.append((rel[:, :, :], c["rel"]))
        SMALL.append((pos3[:, :, :], c["pos3"]))
        SMALL.append((cs[:, :, :, :], c["rope"]))
        SMALL.append((band[:, :, :, :], c["band"]))
        SMALL.append((edge[:, :, :, :], c["edge"]))
        SMALL.append((logit[:, 0, :], a["ret_decay_logit"].rearrange("l r h -> (l r h)").partition_broadcast(P)))
        SMALL.append((normf[:, :], a["norm_f"].partition_broadcast(P)))
        N_SMALL = len(SMALL)

        def layer_loads(l):
            loads = [(kvn[:, :], a["mla_kv_norm"][l].partition_broadcast(P)),
                     (w_uq[:, :, :], a["mla_w_uq"][l].rearrange("(k p) h d -> p k (h d)", p=P)),
                     (w_ukv[:, 0, :], a["mla_w_uk"][l].rearrange("r h d -> r (h d)")),
                     (w_ukv[:, 1, :], a["mla_w_uv"][l].rearrange("r h d -> r (h d)")),
                     (ctx_ckv[:, :], a["cache_mla_ckv"][0, l]), (ctx_kr[:, :], kr_dram[0, l])]
            for g in range(2):
                half = slice(HD * g, HD * g + HD)
                loads.append((w_pool[half, :, :], a["pool_w"][l, g:4:2].rearrange("q i o -> i q o")))
                for r in range(2):
                    loads.append((s0[half, :, HD * r:HD * r + HD], a["state_ret"][0, l, r, g:4:2].rearrange("q k v -> k q v")))
            return loads

        N_LAYER = len(layer_loads(0))
        ROWS = [(0, 8, a["c_ctx"].rearrange("(k p) -> k p", p=P)), (8, 8, a["c"][0].rearrange("(k p) -> k p", p=P)),
                (16, 16, a["norm1"].rearrange("l (k p) -> (l k) p", p=P)),
                (32, 16, a["norm2"].rearrange("l (k p) -> (l k) p", p=P)),
                (48, 4, a["mla_q_norm"].rearrange("l (k p) -> (l k) p", p=P)),
                (52, 12, a["conv_w"].rearrange("l t (k p) -> (l t k) p", p=P)),
                (64, 4, a["pool_scale"].rearrange("l (k p) -> (l k) p", p=P))]
        NORM = {1: 16, 2: 32}
        QNORM, CONVW, POOLS, BMOD = 48, 52, 64, VC

        block = ctx.enter_context(nc.Block())

        @block.sync
        def _(sp):
            for r0, n, src in ROWS:
                sp.dma_start(vec_rows[r0:r0 + n, 0, :], src).then_inc(rows_landed, 16)
            sp.dma_start(vec_rows[0:96, 1, :], a["b_mod"].rearrange("l (k p) -> (l k) p", p=P)).then_inc(rows_landed, 16)

            def weight(n):
                what, layer, cc, last = BLOCKS[n]
                if n >= WSLOTS:
                    sp.wait_ge(bank_filled[slot(*BLOCKS[n - WSLOTS][3])], use(*BLOCKS[n - WSLOTS][3]))
                off = 0
                for c0, w in cc:
                    sp.dma_start(wring[:, n % WSLOTS, :, off:off + w],
                                 a[what][layer].rearrange("(k p) n -> p k n", p=P)[:, :, c0:c0 + w])\
                      .then_inc(w_landed[n % WSLOTS], 16)
                    off += w

            for dst, src in SMALL[:1]:
                sp.dma_start(dst, src).then_inc(small_landed, 16)
            for n in range(WSLOTS):
                weight(n)
            for dst, src in SMALL[1:]:
                sp.dma_start(dst, src).then_inc(small_landed, 16)
            sp.dma_start(x[:, 0, :], a["x_prompt"][0]).then_inc(x_landed, 16)
            for i in range(2):
                sp.dma_start(x[:, 1 + i, :], a["x_sample"][0, P * i:P * i + P, :]).then_inc(x_landed, 16)
            n = WSLOTS
            for stage, i, *_ in ORDER:
                if stage == "groups" or i:
                    continue
                if stage[0] == "keys":
                    l = stage[1]
                    if l:
                        sp.wait_ge(picked_ready, nth("picked", 2))
                        sp.wait_ge(mixed_ready, nth("mixed", TILES[1][-1]))
                    for dst, src in layer_loads(l):
                        sp.dma_start(dst, src).then_inc(layer_landed, 16)
                    sp.dma_start(cand[:, 0:1024].rearrange("n (h d) -> n h d", h=2 * PEER_H),
                                 a["peer_subkeys"][l].rearrange("h q n d -> n (h q) d")).then_inc(keys_landed, 16)
                for what, layer, _, last in weight_blocks(stage):
                    while n <= block_at[what, layer, last]:
                        weight(n)
                        n += 1

        @block.tensor
        def _(pe):
            def weights(what, layer, last):
                n = block_at[what, layer, last]
                pe.wait_ge(w_landed[n % WSLOTS], landed_at[n])
                return wring[:, n % WSLOTS, :, :]

            def start(_):
                pe.wait_ge(rows_landed, 16 * (len(ROWS) + 1))
                pe.wait_ge(small_landed, 16 * N_SMALL)
                pe.wait_ge(bank_free[slot("vec")], use("vec"))
                ps = psum[slot("vec")]
                pe.transpose(ps[:, 0:VC], vec_rows[0:VC, 0, :], ident[0:VC, 0:VC])
                pe.transpose(ps[:, VC:VC + 96], vec_rows[0:96, 1, :], ident[0:96, 0:96]).then_inc(bank_filled[slot("vec")], 1)
                pe.wait_ge(cond_ready, nth("cond", 0))

            def modrow(l, j):
                key = ("modrow", l, j)
                w = weights("w_mod", l, key)
                pe.wait_ge(bank_free[slot(*key)], use(*key))
                ps = psum[slot(*key)]
                for k in range(DC):
                    mm = pe.matmul(ps[0:2, :], cond[:, :, k], w[:, k, :], start=(k == 0), stop=(k == DC - 1))
                mm.then_inc(bank_filled[slot(*key)], 1)

            def modcol(l, j):
                key = ("modcol", l, j)
                pe.wait_ge(mrow_ready, nth("mrow", (l, j)))
                pe.wait_ge(bank_free[slot(*key)], use(*key))
                ps = psum[slot(*key)]
                for i in range(4):
                    mm = pe.transpose(ps[:, 2 * i:2 * i + 2], mrow[0:2, j % 2, P * i:P * i + P], ident[0:2, 0:2])
                mm.then_inc(bank_filled[slot(*key)], 1)

            def keys(l):
                pe.wait_ge(layer_landed, 16 * N_LAYER * (l + 1))
                pe.wait_ge(keys_landed, 16 * (l + 1))
                for b in range(2):
                    pe.wait_ge(bank_free[slot("sk", l, b)], use("sk", l, b))
                    ps = psum[slot("sk", l, b)]
                    for i in range(4):
                        h = 4 * b + i
                        mm = pe.transpose(ps[:, P * i:P * i + P], cand[:, P * h:P * h + P], ident[:, :])
                    mm.then_inc(bank_filled[slot("sk", l, b)], 1)

            def ln(which, t):
                i, cc = tok(M_OF[t], t)
                yield
                pe.wait_ge(xn_ready, nth("xn", (which, t)))
                for b in range(2):
                    key = ("xnT", which, t, b)
                    pe.wait_ge(bank_free[slot(*key)], use(*key))
                    ps = psum[slot(*key)]
                    for k in range(4):
                        mm = pe.transpose(ps[:, P * k:P * k + P], xn[:, P * (4 * b + k):P * (4 * b + k) + P], ident[:, :])
                    mm.then_inc(bank_filled[slot(*key)], 1)
                yield
                if which == 2:
                    pe.wait_ge(hT_ready, nth("hT", (which, t)))
                    for b in range(2):
                        key = ("h2tok", t, b)
                        pe.wait_ge(bank_free[slot(*key)], use(*key))
                        ps = psum[slot(*key)]
                        for k in range(4):
                            mm = pe.transpose(ps[:, P * k:P * k + P], hT[:, 4 * b + k, cc], ident[:, :])
                        mm.then_inc(bank_filled[slot(*key)], 1)
                    yield

            def project(m):
                T = P * len(TILES[m])
                l = LAYER[m]
                last = TILES[m][-1]

                def by_token(key, t, w, c0, n):
                    _, cc = tok(m, t)
                    pe.wait_ge(bank_free[slot(*key)], use(*key))
                    ps = psum[slot(*key)]
                    for k in range(DC):
                        mm = pe.matmul(ps[:, 0:n], hT[:, k, cc], w[:, k, c0:c0 + n], start=(k == 0), stop=(k == DC - 1))
                    mm.then_inc(bank_filled[slot(*key)], 1)

                def by_feature(key, w, c0):
                    pe.wait_ge(bank_free[slot(*key)], use(*key))
                    ps = psum[slot(*key)]
                    for k in range(DC):
                        mm = pe.matmul(ps[:, 0:T], w[:, k, c0:c0 + P], hT[:, k, 0:T], start=(k == 0), stop=(k == DC - 1))
                    mm.then_inc(bank_filled[slot(*key)], 1)

                for t in TILES[m]:
                    pe.wait_ge(hT_ready, nth("hT", (1, t)))
                w = weights("w_in", l, ("zm", last))
                for t in TILES[m]:
                    by_token(("zm", t), t, w, 0, LAT)
                    yield
                w = weights("w_in", l, ("a", m, 3))
                for f in range(4):
                    by_feature(("a", m, f), w, P * f)
                    yield
                w = weights("w_in", l, ("zp", last))
                for f in range(2):
                    by_feature(("a", m, 4 + f), w, P * f)
                    yield
                for t in TILES[m]:
                    by_token(("zp", t), t, w, GROUP_W, GROUP_W)
                    yield
                w = weights("w_in", l, ("rk", m) if STREAM[m] == 0 else ("rqk", m, 3))
                for f in range(4):
                    by_feature(("rqk", m, f), w, P * f)
                    yield
                if STREAM[m] == 0:
                    by_token(("rk", m), TILES[m][0], w, GROUP_W, GROUP_W)
                    yield
                w = weights("w_in", l, ("rvg", last))
                for t in TILES[m]:
                    by_token(("rvg", t), t, w, 0, 512)
                    yield

            def mla(m):
                l, s, nk = LAYER[m], STREAM[m], nk_of(m)
                for t in TILES[m]:
                    yield
                for t in TILES[m]:
                    i, cc = tok(m, t)
                    if s == 1 and i == 0:
                        pe.wait_ge(bank_free[slot("ctxT", m)], use("ctxT", m))
                        ps = psum[slot("ctxT", m)]
                        pe.transpose(ps[:, 0:P], ctx_ckv[:, :], ident[:, :]).then_inc(bank_filled[slot("ctxT", m)], 1)
                    pe.wait_ge(lat_ready, nth("lat", t))
                    pe.wait_ge(bank_free[slot("latT", t)], use("latT", t))
                    ps = psum[slot("latT", t)]
                    for k in range(3):
                        mm = pe.transpose(ps[:, P * k:P * k + P], lat[:, i, P * k:P * k + P], ident[:, :])
                    mm.then_inc(bank_filled[slot("latT", t)], 1)
                    yield
                for t in TILES[m]:
                    i, cc = tok(m, t)
                    pe.wait_ge(latT_ready, nth("latT", t))
                    pe.wait_ge(bank_free[slot("q", t)], use("q", t))
                    ps = psum[slot("q", t)]
                    for k in range(2):
                        mm = pe.matmul(ps[:, 0:HEADS * QK], qlT[:, k, cc], w_uq[:, k, :], start=(k == 0), stop=(k == 1))
                    mm.then_inc(bank_filled[slot("q", t)], 1)
                    yield
                    pe.wait_ge(qtok_ready, nth("qtok", t))
                    pe.wait_ge(bank_free[slot("qT", t)], use("qT", t))
                    ps = psum[slot("qT", t)]
                    for h in range(HEADS):
                        mm = pe.transpose(ps[0:QK, P * h:P * h + P], q_tok[:, QK * h:QK * h + QK], ident[:, :])
                    mm.then_inc(bank_filled[slot("qT", t)], 1)
                    yield
                if s == 1:
                    pe.wait_ge(ctxT_ready, nth("ctxT", m))
                for h in range(HEADS):
                    pe.wait_ge(bank_free[slot("kT", m, h)], use("kT", m, h))
                    ps = psum[slot("kT", m, h)]
                    pe.matmul(ps[0:HD, 0:P * nk], w_ukv[:, 0, HD * h:HD * h + HD], ckvT[:, 0:P * nk], start=True, stop=True)
                    for k in range(nk):
                        if s == 0:
                            kr = zm[:, 0, Q_LORA + KV_LORA:LAT]
                        else:
                            kr = ctx_kr[:, :] if k == 0 else krr[:, k - 1, :]
                        mm = pe.matmul(ps[HD:QK, P * k:P * k + P], kr, ident[:, :], start=True, stop=True)
                    mm.then_inc(bank_filled[slot("kT", m, h)], 1)
                yield
                for k in range(nk):
                    pe.wait_ge(bank_free[slot("v", m, k)], use("v", m, k))
                    ps = psum[slot("v", m, k)]
                    pe.matmul(ps[:, 0:GROUP_W], ckvT[:, P * k:P * k + P], w_ukv[:, 1, :],
                                                 start=True, stop=True).then_inc(bank_filled[slot("v", m, k)], 1)
                yield
                pe.wait_ge(v_ready, nth("v", (m, nk - 1)))
                for t in TILES[m]:
                    _, cc = tok(m, t)
                    pe.wait_ge(qT_ready, nth("qT", t))
                    for h in range(HEADS):
                        pe.wait_ge(kT_ready, nth("kT", (m, h)))
                        pe.wait_ge(bank_free[slot("sc", t, h)], use("sc", t, h))
                        ps = psum[slot("sc", t, h)]
                        pe.matmul(ps[:, 0:P * nk], qT[0:QK, h, cc], kT[0:QK, h, 0:P * nk],
                                                      start=True, stop=True).then_inc(bank_filled[slot("sc", t, h)], 1)
                    yield
                    yield
                    pe.wait_ge(probs_ready, nth("probs", t))
                    for h in range(HEADS):
                        pe.wait_ge(bank_free[slot("pT", t, h)], use("pT", t, h))
                        ps = psum[slot("pT", t, h)]
                        for k in range(nk):
                            mm = pe.transpose(ps[:, P * k:P * k + P], probs[:, h, P * k:P * k + P], ident[:, :])
                        mm.then_inc(bank_filled[slot("pT", t, h)], 1)
                        if h % 2:
                            pe.wait_ge(bank_free[slot("o", t, h // 2)], use("o", t, h // 2))
                            ps = psum[slot("o", t, h // 2)]
                            for g in range(2):
                                pe.wait_ge(pT_ready, nth("pT", (t, h - 1 + g)))
                                for k in range(nk):
                                    mm = pe.matmul(ps[HD * g:HD * g + HD, 0:P], vtok[:, k, HD * (h - 1 + g):HD * (h + g)],
                                                   pT[:, g, P * k:P * k + P], start=(k == 0), stop=(k == nk - 1))
                            mm.then_inc(bank_filled[slot("o", t, h // 2)], 1)
                            yield

            def ret(m):
                l, s, nt = LAYER[m], STREAM[m], len(TILES[m])
                T = P * nt
                pe.wait_ge(rqk_ready, nth("rqk", m))

                def inner(h):
                    q, g = h // 2, HD * (h % 2)
                    for i in range(nt):
                        pe.wait_ge(bank_free[slot("inn", m, h, i)], use("inn", m, h, i))
                        ps = psum[slot("inn", m, h, i)]
                        pe.matmul(ps[:, 0:T], rqk[g:g + HD, 2 + q, P * i:P * i + P],
                                                          rqk[g:g + HD, q, 0:T], start=True, stop=True).then_inc(bank_filled[slot("inn", m, h, i)], 1)

                inner(0)
                yield
                for h in range(HEADS):
                    q, g = h // 2, HD * (h % 2)
                    if h + 1 < HEADS:
                        inner(h + 1)
                    for i in range(nt):
                        pe.wait_ge(bank_free[slot("inn", m, h, i)], use("inn", m, h, i) + 1)
                        pe.wait_ge(rvg_ready, nth("rvg", TILES[m][i]))
                    pe.wait_ge(bank_free[slot("oh", m, h)], use("oh", m, h))
                    ps = psum[slot("oh", m, h)]
                    for j in range(nt):
                        for i in range(nt):
                            mm = pe.matmul(ps[:, 192 * j:192 * j + HD], inn[:, h % 2, i, P * j:P * j + P],
                                           rv[:, i, 0, HD * h:HD * h + HD], start=(i == 0), stop=(i == nt - 1))
                        if s == 1:
                            mm = pe.matmul(ps[:, 192 * j + HD:192 * j + 3 * HD], rqk[g:g + HD, q, P * j:P * j + P],
                                           s0[g:g + HD, q, :], start=True, stop=True)
                    mm.then_inc(bank_filled[slot("oh", m, h)], 1)
                    yield
                if s == 0:
                    yield
                    pe.wait_ge(k_decayed_ready, nth("k_decayed", m))
                    pe.wait_ge(bank_free[slot("st", m)], use("st", m))
                    ps = psum[slot("st", m)]
                    for r in range(2):
                        for h in range(HEADS):
                            o = HD * (HEADS * r + h)
                            mm = pe.matmul(ps[0:HD, o:o + HD], xn[:, 512 + o:512 + o + HD], rv[:, 0, 0, HD * h:HD * h + HD],
                                           start=True, stop=True)
                    mm.then_inc(bank_filled[slot("st", m)], 1)
                    yield
                for t in TILES[m]:
                    i, _ = tok(m, t)
                    yield
                    pe.wait_ge(ret_out_ready, nth("ret_out", t))
                    pe.wait_ge(bank_free[slot("yrT", t)], use("yrT", t))
                    ps = psum[slot("yrT", t)]
                    for k in range(2):
                        mm = pe.transpose(ps[:, P * k:P * k + P], o_tok[:, i, P * k:P * k + P], ident[:, :])
                    mm.then_inc(bank_filled[slot("yrT", t)], 1)
                    yield

            def pool_(m):
                l, s, nt = LAYER[m], STREAM[m], len(TILES[m])
                T = P * nt
                for t in TILES[m]:
                    pe.wait_ge(zp_ready, nth("zp", t))
                for b in range(2):
                    pe.wait_ge(bank_free[slot("pl", m, b)], use("pl", m, b))
                    ps = psum[slot("pl", m, b)]
                    for g in range(2):
                        n = 2 * b + g
                        half = slice(HD * g, HD * g + HD)
                        for i in range(nt):
                            mm = pe.matmul(ps[half, P * i:P * i + P], zp[:, i, HD * n:HD * n + HD], band[:, s + i, n, :],
                                           start=True, stop=True)
                            if s == 1:
                                c0 = P - 8 if i == 0 else P
                                mm = pe.matmul(ps[half, c0:c0 + 8], zp[:, 1 - i, HD * n:HD * n + HD], edge[:, i, n, :],
                                               start=False, stop=True, skip_group_check=True)
                    mm.then_inc(bank_filled[slot("pl", m, b)], 1)
                yield
                for b in range(2):
                    pe.wait_ge(pooled_ready, nth("pooled", (m, b)))
                    pe.wait_ge(bank_free[slot("plo", m, b)], use("plo", m, b))
                    ps = psum[slot("plo", m, b)]
                    for g in range(2):
                        mm = pe.matmul(ps[HD * g:HD * g + HD, 0:T], w_pool[HD * g:HD * g + HD, b, :],
                                       pooled[HD * g:HD * g + HD, b, 0:T], start=True, stop=True)
                    mm.then_inc(bank_filled[slot("plo", m, b)], 1)
                yield

            def gate(which, n, l, s):
                pe.wait_ge(bank_free[slot("modcol", l, 5 if which == 1 else 11)], use("modcol", l, 5 if which == 1 else 11) + 1)
                for b in range(2):
                    pe.wait_ge(bank_free[slot("gate", which, n, b)], use("gate", which, n, b))
                    ps = psum[slot("gate", which, n, b)]
                    kind = G1 if which == 1 else G2
                    for k in range(4):
                        col = modc[:, l, 8 * kind + 4 * b + k, s:s + 1]
                        mm = pe.matmul(ps[:, P * k:P * k + P], col.to_broadcast([P, P]), ident[:, :], start=True, stop=True)
                    mm.then_inc(bank_filled[slot("gate", which, n, b)], 1)

            def out(m):
                gate(1, m, LAYER[m], STREAM[m])
                yield
                pe.wait_ge(y_conv_ready, nth("y_conv", m))
                pe.wait_ge(y_pool_ready, nth("y_pool", (m, 1)))
                for b in range(2):
                    w = weights("w_out", LAYER[m], ("mix", TILES[m][-1], b))
                    for t in TILES[m]:
                        _, cc = tok(m, t)
                        pe.wait_ge(y_mla_ready, nth("y_mla", (t, 1)))
                        pe.wait_ge(y_ret_ready, nth("y_ret", t))
                        pe.wait_ge(bank_free[slot("mix", t, b)], use("mix", t, b))
                        ps = psum[slot("mix", t, b)]
                        for k in range(DC):
                            mm = pe.matmul(ps[:, :], yT[:, k, cc], w[:, k, :], start=(k == 0), stop=(k == DC - 1))
                        mm.then_inc(bank_filled[slot("mix", t, b)], 1)
                        yield

            def query(m):
                T = P * len(TILES[m])
                for t in TILES[m]:
                    pe.wait_ge(hT_ready, nth("hT", (2, t)))
                for b in range(2):
                    w = weights("peer_w_q", LAYER[m], ("qp", m, 4 * b + 3))
                    for i in range(4):
                        key = ("qp", m, 4 * b + i)
                        pe.wait_ge(bank_free[slot(*key)], use(*key))
                        ps = psum[slot(*key)]
                        for k in range(DC):
                            mm = pe.matmul(ps[:, 0:T], w[:, k, P * i:P * i + P], hT[:, k, 0:T], start=(k == 0), stop=(k == DC - 1))
                        mm.then_inc(bank_filled[slot(*key)], 1)
                        yield

            def score(t):
                m = M_OF[t]
                _, cc = tok(m, t)
                pe.wait_ge(sk_ready, nth("sk", LAYER[m]))
                for b in range(4):
                    pe.wait_ge(bank_free[slot("s", t, b)], use("s", t, b))
                    ps = psum[slot("s", t, b)]
                    for i in range(4):
                        h, g = 4 * (b % 2) + i, HD * (b // 2)
                        pe.wait_ge(qp_ready, nth("qp", (m, h)))
                        mm = pe.matmul(ps[:, P * i:P * i + P], qpT[g:g + HD, h, cc], skT[g:g + HD, h, :], start=True, stop=True)
                    mm.then_inc(bank_filled[slot("s", t, b)], 1)

            def finish(t):
                gate(2, t, LAYER[M_OF[t]], STREAM[M_OF[t]])
                yield
                if t >= 3:
                    yield

            def groups(t, lo, hi):
                def group(i, first, last):
                    for r in range(G):
                        pe.wait_ge(v_landed[r], i * 16 + 16 * (NG * t + 1))
                        pe.wait_ge(diag_built, i * G + (PICKS * t + r + 1))
                        for b in range(2):
                            mm = pe.matmul(ysum[:, b, :], diag[:, r % DIAGS, :], vbuf[:, r, 512 * b:512 * b + 512],
                                           start=first and r == 0, stop=last and r == G - 1, skip_group_check=True)
                        mm.then_inc(v_free, 1)

                if lo == 0 and t == 0:
                    pe.sem_inc(v_free, SLOTS)
                if lo <= 1 < hi:
                    if t:
                        pe.wait_ge(updated_ready, nth("updated", t - 1))
                    group(0, True, False)
                a, b = max(lo - 1, 1), hi - 1
                if b - a > 1:
                    with pe.Fori(a, b) as i:
                        group(i, False, False)
                elif b > a:
                    group(a, False, False)
                if hi == NG:
                    group(NG - 1, False, True)

            running = {}
            for stage, i, *more in ORDER:
                if stage == "groups":
                    groups(i, *more)
                    continue
                kind, *n = stage
                if kind == "start":
                    beat_of(i, stage, running, start, *n)
                elif kind == "modrow":
                    beat_of(i, stage, running, modrow, *n)
                elif kind == "modcol":
                    beat_of(i, stage, running, modcol, *n)
                elif kind == "keys":
                    beat_of(i, stage, running, keys, *n)
                elif kind == "ln":
                    beat_of(i, stage, running, ln, *n)
                elif kind == "in":
                    beat_of(i, stage, running, project, *n)
                elif kind == "mla":
                    beat_of(i, stage, running, mla, *n)
                elif kind == "ret":
                    beat_of(i, stage, running, ret, *n)
                elif kind == "pool":
                    beat_of(i, stage, running, pool_, *n)
                elif kind == "out":
                    beat_of(i, stage, running, out, *n)
                elif kind == "q":
                    beat_of(i, stage, running, query, *n)
                elif kind == "score":
                    beat_of(i, stage, running, score, *n)
                elif kind == "finish":
                    beat_of(i, stage, running, finish, *n)

        @block.scalar
        def _(act):
            def std(key, *parts):
                act.wait_ge(sumsq_ready, nth("sumsq", key))
                for dst, src, n in parts:
                    ins = act.activation(dst, src, ACT.Sqrt, scale=1.0 / n, bias=EPS)
                ins.then_inc(std_ready, 1)

            def start(_):
                act.wait_ge(small_landed, 16 * N_SMALL)
                act.wait_ge(bank_filled[slot("vec")], use("vec"))
                act.activation(cols[:, :], psum[slot("vec")][:, 0:VC + 96], ACT.Copy)\
                   .then_inc(bank_free[slot("vec")], 1)
                act.wait_ge(bank_free[slot("vec")], use("vec") + 1)
                act.activation(cond[:, :, :], cols[:, 0:16].rearrange("p (s k) -> p s k", s=2), ACT.Silu).then_inc(cond_ready, 1)
                act.wait_ge(cond_ready, nth("cond", 0))
                act.wait_ge(abs_logit_ready, nth("abs_logit", 0))
                act.activation(logit[:, 1, :], logit[:, 1, :], ACT.Exp, scale=-1.0).then_inc(act_done, 1)
                act.wait_ge(act_done, 1)
                act.activation(logit[:, 2, :], logit[:, 1, :], ACT.Ln, bias=1.0).then_inc(log1p_ready, 1)

            def modrow(l, j):
                n = 12 * l + j
                if n >= 2:
                    key = ("modcol", (n - 2) // 12, (n - 2) % 12)
                    act.wait_ge(bank_filled[slot(*key)], use(*key))
                act.wait_ge(bank_filled[slot("modrow", l, j)], use("modrow", l, j))
                act.activation(mrow[0:2, j % 2, :], psum[slot("modrow", l, j)][0:2, :], ACT.Copy)\
                   .then_inc(bank_free[slot("modrow", l, j)], 1)
                act.wait_ge(bank_free[slot("modrow", l, j)], use("modrow", l, j) + 1)
                act.sem_inc(mrow_ready, 1)

            def keys(l):
                for b in range(2):
                    act.wait_ge(bank_filled[slot("sk", l, b)], use("sk", l, b))
                    act.activation(skT[:, 4 * b:4 * b + 4, :].rearrange("p h n -> p (h n)"), psum[slot("sk", l, b)][:, 0:512], ACT.Copy)\
                       .then_inc(bank_free[slot("sk", l, b)], 1)
                    act.wait_ge(bank_free[slot("sk", l, b)], use("sk", l, b) + 1)
                act.sem_inc(sk_ready, 1)

            def decay_(l):
                for h in range(HEADS):
                    act.wait_ge(decay_arg_ready, nth("decay_arg", (l, h)))
                    act.activation(decay[:, h, :], decay[:, h, :], ACT.Exp).then_inc(decay_exp_ready, 1)
                for r in range(2):
                    for h in range(HEADS):
                        k = 8 * l + 4 * r + h
                        act.activation(dcol[:, r, h, :], pos3[:, r, :], ACT.Exp, scale=logit[:, 3, k:k + 1]).then_inc(decay_col_ready, 1)

            def ln(which, t):
                m = M_OF[t]
                l, s = LAYER[m], STREAM[m]
                _, cc = tok(m, t)
                std(("ln", which, t), (stat[:, 1:2], stat[:, 0:1], D))
                yield
                act.wait_ge(mods_ready, nth("mods", (l, which)))
                for b in range(2):
                    key = ("xnT", which, t, b)
                    act.wait_ge(bank_filled[slot(*key)], use(*key))
                    ps = psum[slot(*key)]
                    for k in range(4):
                        f = 4 * b + k
                        ins = act.activation(hT[:, f, cc], ps[:, P * k:P * k + P], ACT.Identity,
                                             scale=moda[:, l, which - 1, s, f:f + 1],
                                             bias=modc[:, l, 8 * (SH1 if which == 1 else SH2) + f, s:s + 1])
                        if k == 3:
                            ins.then_inc(bank_free[slot(*key)], 1)
                    act.wait_ge(bank_free[slot(*key)], use(*key) + 1)
                act.sem_inc(hT_ready, 1)
                yield
                if which == 2:
                    for b in range(2):
                        act.wait_ge(bank_filled[slot("h2tok", t, b)], use("h2tok", t, b))
                        act.activation(h2[:, XBUF[t], 512 * b:512 * b + 512], psum[slot("h2tok", t, b)][:, 0:512], ACT.Copy)\
                           .then_inc(bank_free[slot("h2tok", t, b)], 1)
                        act.wait_ge(bank_free[slot("h2tok", t, b)], use("h2tok", t, b) + 1)
                        act.sem_inc(h2_ready, 1)
                    yield

            def project(m):
                T = P * len(TILES[m])
                if m:
                    act.wait_ge(mixed_ready, nth("mixed", TILES[m - 1][-1]))
                for t in TILES[m]:
                    yield
                for f in range(6):
                    act.wait_ge(bank_filled[slot("a", m, f)], use("a", m, f))
                    act.activation(za[:, f, 0:T], psum[slot("a", m, f)][:, 0:T], ACT.Copy)\
                       .then_inc(bank_free[slot("a", m, f)], 1)
                    act.wait_ge(bank_free[slot("a", m, f)], use("a", m, f) + 1)
                    if f == 5:
                        act.sem_inc(za_ready, 1)
                    yield
                for t in TILES[m]:
                    i, _ = tok(m, t)
                    act.wait_ge(bank_filled[slot("zp", t)], use("zp", t))
                    act.activation(zp[:, i, :], psum[slot("zp", t)][:, 0:GROUP_W], ACT.Copy)\
                       .then_inc(bank_free[slot("zp", t)], 1)
                    act.wait_ge(bank_free[slot("zp", t)], use("zp", t) + 1)
                    act.sem_inc(zp_ready, 1)
                    yield
                for f in range(4):
                    act.wait_ge(bank_filled[slot("rqk", m, f)], use("rqk", m, f))
                    act.activation(rqk[:, f, 0:T], psum[slot("rqk", m, f)][:, 0:T], ACT.Copy)\
                       .then_inc(bank_free[slot("rqk", m, f)], 1)
                    act.wait_ge(bank_free[slot("rqk", m, f)], use("rqk", m, f) + 1)
                    if f == 3:
                        act.sem_inc(rqk_ready, 1)
                    yield
                if STREAM[m] == 0:
                    yield
                for t in TILES[m]:
                    i, _ = tok(m, t)
                    act.wait_ge(bank_filled[slot("rvg", t)], use("rvg", t))
                    ps = psum[slot("rvg", t)]
                    act.activation(rv[:, i, 0, :], ps[:, 0:GROUP_W], ACT.Copy)
                    act.activation(rv[:, i, 1, :], ps[:, GROUP_W:512], ACT.Silu).then_inc(bank_free[slot("rvg", t)], 1)
                    act.wait_ge(bank_free[slot("rvg", t)], use("rvg", t) + 1)
                    act.sem_inc(rvg_ready, 1)
                    yield

            def mla(m):
                l, s, nk = LAYER[m], STREAM[m], nk_of(m)
                act.wait_ge(bank_filled[slot("rvg", TILES[m][-1])], use("rvg", TILES[m][-1]))
                for t in TILES[m]:
                    std(("mla", t), (stat[:, 18:19], stat[:, 16:17], Q_LORA), (stat[:, 19:20], stat[:, 17:18], KV_LORA))
                    yield
                if s == 1:
                    act.wait_ge(bank_filled[slot("ctxT", m)], use("ctxT", m))
                    act.activation(ckvT[:, 0:P], psum[slot("ctxT", m)][:, 0:P], ACT.Copy)\
                       .then_inc(bank_free[slot("ctxT", m)], 1)
                    act.wait_ge(bank_free[slot("ctxT", m)], use("ctxT", m) + 1)
                    act.sem_inc(ctxT_ready, 1)
                for t in TILES[m]:
                    i, cc = tok(m, t)
                    if s == 0:
                        act.wait_ge(lat_ready, nth("lat", t))
                        act.dma_start(new_ckv[0, l], lat[:, 0, Q_LORA:Q_LORA + KV_LORA]).then_inc(cache_stored, 16)
                        act.dma_start(new_krope[0, l], zm[:, 0, Q_LORA + KV_LORA:LAT]).then_inc(cache_stored, 16)
                    act.wait_ge(bank_filled[slot("latT", t)], use("latT", t))
                    ps = psum[slot("latT", t)]
                    for k in range(2):
                        act.activation(qlT[:, k, cc], ps[:, P * k:P * k + P], ACT.Identity,
                                       scale=cols[:, QNORM + 2 * l + k:QNORM + 2 * l + k + 1])
                    k0 = P * (i + nk - len(TILES[m]))
                    act.activation(ckvT[:, k0:k0 + P], ps[:, 2 * P:3 * P], ACT.Copy).then_inc(bank_free[slot("latT", t)], 1)
                    act.wait_ge(bank_free[slot("latT", t)], use("latT", t) + 1)
                    act.sem_inc(latT_ready, 1)
                    yield
                for t in TILES[m]:
                    _, cc = tok(m, t)
                    yield
                    act.wait_ge(bank_filled[slot("qT", t)], use("qT", t))
                    act.activation(qT[0:QK, :, cc], psum[slot("qT", t)][0:QK, 0:512], ACT.Copy)\
                       .then_inc(bank_free[slot("qT", t)], 1)
                    act.wait_ge(bank_free[slot("qT", t)], use("qT", t) + 1)
                    act.sem_inc(qT_ready, 1)
                    yield
                for h in range(HEADS):
                    act.wait_ge(bank_filled[slot("kT", m, h)], use("kT", m, h))
                    act.activation(kT[0:QK, h, 0:P * nk], psum[slot("kT", m, h)][0:QK, 0:P * nk], ACT.Copy)\
                       .then_inc(bank_free[slot("kT", m, h)], 1)
                    act.wait_ge(bank_free[slot("kT", m, h)], use("kT", m, h) + 1)
                    act.sem_inc(kT_ready, 1)
                yield
                for k in range(nk):
                    act.wait_ge(bank_filled[slot("v", m, k)], use("v", m, k))
                    act.activation(vtok[:, k, :], psum[slot("v", m, k)][:, 0:GROUP_W], ACT.Copy)\
                       .then_inc(bank_free[slot("v", m, k)], 1)
                    act.wait_ge(bank_free[slot("v", m, k)], use("v", m, k) + 1)
                    act.sem_inc(v_ready, 1)
                yield
                for t in TILES[m]:
                    _, cc = tok(m, t)
                    yield
                    act.wait_ge(row_max_ready, nth("row_max", t))
                    for h in range(HEADS):
                        key = ("sc", t, h)
                        act.wait_ge(bank_filled[slot(*key)], use(*key))
                        ps = psum[slot(*key)]
                        act.activation(probs[:, h, 0:P * nk], ps[:, 0:P * nk], ACT.Exp, scale=SM_SCALE,
                                       bias=stat[:, 4 + h:5 + h], accum_out=stat[:, 8 + h:9 + h])\
                           .then_inc(bank_free[slot(*key)], 1)
                        act.wait_ge(bank_free[slot(*key)], use(*key) + 1)
                    yield
                    for h in range(HEADS):
                        if h >= 2 and h % 2 == 0:
                            act.wait_ge(bank_filled[slot("o", t, h // 2 - 1)], use("o", t, h // 2 - 1))
                        act.wait_ge(bank_filled[slot("pT", t, h)], use("pT", t, h))
                        act.activation(pT[:, h % 2, 0:P * nk], psum[slot("pT", t, h)][:, 0:P * nk], ACT.Copy)\
                           .then_inc(bank_free[slot("pT", t, h)], 1)
                        act.wait_ge(bank_free[slot("pT", t, h)], use("pT", t, h) + 1)
                        act.sem_inc(pT_ready, 1)
                        if h % 2:
                            act.wait_ge(bank_filled[slot("o", t, h // 2)], use("o", t, h // 2))
                            act.activation(yT[:, 2 + h // 2, cc], psum[slot("o", t, h // 2)][:, 0:P], ACT.Copy)\
                               .then_inc(bank_free[slot("o", t, h // 2)], 1)
                            act.wait_ge(bank_free[slot("o", t, h // 2)], use("o", t, h // 2) + 1)
                            act.sem_inc(y_mla_ready, 1)
                            yield

            def ret(m):
                for h in range(HEADS + 1):
                    yield
                if STREAM[m] == 0:
                    yield
                    if m:
                        act.wait_ge(state_stored, 16)
                    act.wait_ge(bank_filled[slot("st", m)], use("st", m))
                    act.activation(state_out[:, :], psum[slot("st", m)][0:HD, 0:512], ACT.Copy)\
                       .then_inc(bank_free[slot("st", m)], 1)
                    act.wait_ge(bank_free[slot("st", m)], use("st", m) + 1)
                    act.sem_inc(state_ready, 1)
                    act.dma_start(new_state[0, LAYER[m]].rearrange("r h k v -> k (r h) v"),
                                  state_out[:, :].rearrange("k (n v) -> k n v", v=HD)).then_inc(state_stored, 16)
                    yield
                for t in TILES[m]:
                    _, cc = tok(m, t)
                    std(("ret", t), (stat[:, 28:32], stat[:, 24:28], HD))
                    yield
                    key = ("yrT", t)
                    act.wait_ge(bank_filled[slot(*key)], use(*key))
                    ps = psum[slot(*key)]
                    act.activation(yT[:, 4:6, cc], ps[:, 0:2 * P].rearrange("p (k n) -> p k n", k=2), ACT.Copy)\
                       .then_inc(bank_free[slot(*key)], 1)
                    act.wait_ge(bank_free[slot(*key)], use(*key) + 1)
                    act.sem_inc(y_ret_ready, 1)
                    yield

            def pool_(m):
                T = P * len(TILES[m])
                l = LAYER[m]
                for b in range(2):
                    act.wait_ge(bank_filled[slot("pl", m, b)], use("pl", m, b))
                    act.activation(pooled[:, b, 0:T], psum[slot("pl", m, b)][:, 0:T], ACT.Copy)\
                       .then_inc(bank_free[slot("pl", m, b)], 1)
                    act.wait_ge(bank_free[slot("pl", m, b)], use("pl", m, b) + 1)
                    act.sem_inc(pooled_ready, 1)
                yield
                for b in range(2):
                    act.wait_ge(bank_filled[slot("plo", m, b)], use("plo", m, b))
                    act.activation(yT[:, 6 + b, 0:T], psum[slot("plo", m, b)][:, 0:T], ACT.Identity, scale=cols[:, POOLS + 2 * l + b:POOLS + 2 * l + b + 1])\
                       .then_inc(bank_free[slot("plo", m, b)], 1)
                    act.wait_ge(bank_free[slot("plo", m, b)], use("plo", m, b) + 1)
                    act.sem_inc(y_pool_ready, 1)
                yield

            def gate(which, n):
                kind, last = GATE_BEFORE["out" if which == 1 else "finish", n] or (None, None)
                if kind == "out":
                    act.wait_ge(mixed_ready, nth("mixed", TILES[last][-1]))
                elif kind == "finish":
                    act.wait_ge(updated_ready, nth("updated", last))
                for b in range(2):
                    act.wait_ge(bank_filled[slot("gate", which, n, b)], use("gate", which, n, b))
                    act.activation(gate_row[:, 512 * b:512 * b + 512], psum[slot("gate", which, n, b)][:, 0:512], ACT.Copy)\
                       .then_inc(bank_free[slot("gate", which, n, b)], 1)
                    act.wait_ge(bank_free[slot("gate", which, n, b)], use("gate", which, n, b) + 1)
                    act.sem_inc(gate_ready, 1)

            def out(m):
                gate(1, m)
                yield
                for t in TILES[m]:
                    yield
                    yield

            def query(m):
                T = P * len(TILES[m])
                for h in range(PEER_H):
                    act.wait_ge(bank_filled[slot("qp", m, h)], use("qp", m, h))
                    act.activation(qpT[:, h, 0:T], psum[slot("qp", m, h)][:, 0:T], ACT.Copy)\
                       .then_inc(bank_free[slot("qp", m, h)], 1)
                    act.wait_ge(bank_free[slot("qp", m, h)], use("qp", m, h) + 1)
                    act.sem_inc(qp_ready, 1)
                    yield

            def score(t):
                if t:
                    act.wait_ge(picked_ready, nth("picked", t - 1))
                if STREAM[M_OF[t]] == 0:
                    act.wait_ge(cache_stored, 32 * (LAYER[M_OF[t]] + 1))
                for b in range(4):
                    act.wait_ge(bank_filled[slot("s", t, b)], use("s", t, b))
                    act.activation(s_sb[:, 512 * b:512 * b + 512], psum[slot("s", t, b)][:, 0:512], ACT.Copy)\
                       .then_inc(bank_free[slot("s", t, b)], 1)
                    act.wait_ge(bank_free[slot("s", t, b)], use("s", t, b) + 1)
                    act.sem_inc(scores_ready, 1)

            def topk(t):
                for _ in range(12):
                    yield
                act.wait_ge(gate_arg_ready, nth("gate_arg", t))
                act.activation(cv[:, :, :], cv[:, :, :], ACT.Exp).then_inc(gate_exp_ready, 1)
                for _ in range(3):
                    yield

            def finish(t):
                gate(2, t)
                yield
                if t >= 3:
                    std(("final", t), (stat[:, 1:2], stat[:, 0:1], D))
                    act.wait_ge(final_ready, nth("final", t))
                    dst = y_prompt[0] if t == 3 else y_sample[0, P * (t - 4):P * (t - 4) + P, :]
                    act.dma_start(dst, xn[:, :]).then_inc(y_stored, 16)
                    yield

            def groups(t, lo, hi):
                def group(i):
                    act.wait_ge(u_free, i * G + (SLOTS + PICKS * t + G))
                    act.activation(act_dot[:, :], dot[:, :], ACT.Gelu_apprx_tanh).then_inc(gelu_done, 1)
                    for r in range(G):
                        if r == 0:
                            act.wait_ge(coef_done, i + (NG * t + 1))
                        act.wait_ge(v_free, i * G + (SLOTS + PICKS * t + r - DIAGS + 1))
                        act.activation(diag[:, r % DIAGS, :], ident[:, :], ACT.Copy, scale=coef[:, r:r + 1]).then_inc(diag_built, 1)

                if hi - lo > 1:
                    with act.Fori(lo, hi) as i:
                        group(i)
                else:
                    group(lo)

            running = {}
            for stage, i, *more in ORDER:
                if stage == "groups":
                    groups(i, *more)
                    continue
                kind, *n = stage
                if kind == "start":
                    beat_of(i, stage, running, start, *n)
                elif kind == "modrow":
                    beat_of(i, stage, running, modrow, *n)
                elif kind == "keys":
                    beat_of(i, stage, running, keys, *n)
                elif kind == "decay":
                    beat_of(i, stage, running, decay_, *n)
                elif kind == "ln":
                    beat_of(i, stage, running, ln, *n)
                elif kind == "in":
                    beat_of(i, stage, running, project, *n)
                elif kind == "mla":
                    beat_of(i, stage, running, mla, *n)
                elif kind == "ret":
                    beat_of(i, stage, running, ret, *n)
                elif kind == "pool":
                    beat_of(i, stage, running, pool_, *n)
                elif kind == "out":
                    beat_of(i, stage, running, out, *n)
                elif kind == "q":
                    beat_of(i, stage, running, query, *n)
                elif kind == "score":
                    beat_of(i, stage, running, score, *n)
                elif kind == "topk":
                    beat_of(i, stage, running, topk, *n)
                elif kind == "finish":
                    beat_of(i, stage, running, finish, *n)
            act.wait_ge(cache_stored, 64)
            act.wait_ge(state_stored, 32)
            act.wait_ge(y_stored, 48)

        @block.vector
        def _(dve):
            steps = [0]

            def counted():
                steps[0] += 1
                return 1

            def rstd(dst, key):
                dve.sem_inc(sumsq_ready, 1)
                dve.wait_ge(std_ready, nth("std", key))
                dve.reciprocal(dst, dst).then_inc(dve_done, counted())
                dve.wait_ge(dve_done, steps[0])

            def start(_):
                for b in range(RING):
                    dve.sem_inc(bank_free[b], 1)
                dve.wait_ge(small_landed, 16 * N_SMALL)
                dve.wait_ge(x_landed, 48)
                dve.scalar_tensor_tensor(out=logit[:, 1, :], in0=logit[:, 0, :], scalar=-1.0, in1=logit[:, 0, :],
                                             op0=ALU.mult, op1=ALU.max).then_inc(abs_logit_ready, 1)
                dve.wait_ge(abs_logit_ready, nth("abs_logit", 0))
                dve.wait_ge(log1p_ready, nth("log1p", 0))
                dve.tensor_scalar(logit[:, 3, :], logit[:, 0, :], 0.0, None, ALU.min).then_inc(dve_done, counted())
                dve.wait_ge(dve_done, steps[0])
                dve.tensor_tensor(logit[:, 3, :], logit[:, 3, :], logit[:, 2, :], ALU.subtract).then_inc(decay_log_ready, 1)
                dve.wait_ge(decay_log_ready, nth("decay_log", 0))
                dve.wait_ge(cond_ready, nth("cond", 0))

            def modcol(l, j):
                key = ("modcol", l, j)
                dve.wait_ge(bank_filled[slot(*key)], use(*key))
                ps = psum[slot(*key)]
                bias = cols[:, BMOD + 48 * l + 4 * j:BMOD + 48 * l + 4 * j + 4]
                dve.tensor_tensor(modc[:, l, 4 * j:4 * j + 4, :], ps[:, 0:8].rearrange("p (k s) -> p k s", s=2),
                                  bias.unsqueeze(2).to_broadcast([P, 4, 2]), ALU.add).then_inc(bank_free[slot(*key)], 1)
                dve.wait_ge(bank_free[slot(*key)], use(*key) + 1)

            def modscale(l, which):
                kind = SC1 if which == 1 else SC2
                for s in range(2):
                    ins = dve.scalar_tensor_tensor(out=moda[:, l, which - 1, s, :], in0=modc[:, l, 8 * kind:8 * kind + 8, s],
                                                   scalar=1.0, in1=cols[:, NORM[which] + 8 * l:NORM[which] + 8 * l + 8],
                                                   op0=ALU.add, op1=ALU.mult)
                ins.then_inc(mods_ready, 1)
                dve.wait_ge(mods_ready, nth("mods", (l, which)))

            def decay_(l):
                for h in range(HEADS):
                    f, b = 8 * l + h, 8 * l + 4 + h
                    dve.tensor_scalar(decay[:, h, :], rel[:, 1, :], logit[:, 3, b:b + 1], None, ALU.mult).then_inc(dve_done, counted())
                    dve.wait_ge(dve_done, steps[0])
                    dve.scalar_tensor_tensor(out=decay[:, h, :], in0=rel[:, 0, :], scalar=logit[:, 3, f:f + 1],
                                                 in1=decay[:, h, :], op0=ALU.mult, op1=ALU.add).then_inc(decay_arg_ready, 1)
                    dve.wait_ge(decay_arg_ready, nth("decay_arg", (l, h)))
                for h in range(HEADS):
                    dve.wait_ge(decay_exp_ready, nth("decay_exp", (l, h)))
                    dve.tensor_scalar(decay[:, h, :], decay[:, h, :], K_SCALE, None, ALU.mult).then_inc(dve_done, counted())
                    dve.wait_ge(dve_done, steps[0])
                    mid = decay[:, h, P:2 * P]
                    dve.scalar_tensor_tensor(out=mid, in0=ident[:, :], scalar=K_SCALE, in1=mid, op0=ALU.mult, op1=ALU.add).then_inc(dve_done, counted())
                    dve.wait_ge(dve_done, steps[0])
                dve.wait_ge(decay_col_ready, nth("decay_col", (l, 7)))

            def ln(which, t):
                xt = x[:, XBUF[t], :]
                dve.tensor_tensor_reduce(xn[:, :], xt, xt, 1.0, 0.0, ALU.mult, ALU.add, stat[:, 0:1]).then_inc(dve_done, counted())
                dve.wait_ge(dve_done, steps[0])
                rstd(stat[:, 1:2], ("ln", which, t))
                dve.tensor_scalar(xn[:, :], xt, stat[:, 1:2], None, ALU.mult).then_inc(xn_ready, 1)
                dve.wait_ge(xn_ready, nth("xn", (which, t)))
                yield
                dve.wait_ge(bank_filled[slot("xnT", which, t, 1)], use("xnT", which, t, 1))
                yield
                if which == 2:
                    yield

            def project(m):
                for t in TILES[m]:
                    i, _ = tok(m, t)
                    if m and i == 0:
                        dve.wait_ge(cache_stored, 32 * (LAYER[m - 1] + 1))
                    dve.wait_ge(bank_filled[slot("zm", t)], use("zm", t))
                    ps = psum[slot("zm", t)]
                    dve.tensor_copy(zm[:, i, :], ps[:, 0:LAT]).then_inc(bank_free[slot("zm", t)], 1)
                    dve.wait_ge(bank_free[slot("zm", t)], use("zm", t) + 1)
                    yield
                for _ in range(6 + len(TILES[m]) + 4):
                    yield
                if STREAM[m] == 0:
                    dve.wait_ge(bank_filled[slot("rk", m)], use("rk", m))
                    ps = psum[slot("rk", m)]
                    dve.tensor_copy(rk[:, :], ps[:, 0:GROUP_W]).then_inc(bank_free[slot("rk", m)], 1)
                    dve.wait_ge(bank_free[slot("rk", m)], use("rk", m) + 1)
                    yield
                for t in TILES[m]:
                    yield

            def rope(dst, src, i, heads, tmp):
                def table(k):
                    return cs[:, i, k, :].unsqueeze(1).to_broadcast([P, heads, ROPE])

                dve.tensor_tensor(tmp, src, table(0), ALU.mult).then_inc(dve_done, counted())
                dve.wait_ge(dve_done, steps[0])
                hs = tmp2[:, 0:heads * ROPE].rearrange("p (h a o e) -> p h a o e", h=heads, a=2, o=2)
                sv = src.rearrange("p h (a o e) -> p h a o e", a=2, o=2)
                sn = cs[:, i, 1, :].rearrange("p (a o e) -> p a o e", a=2, o=2)
                for o in range(2):
                    tab = sn[:, :, o, :].unsqueeze(1).to_broadcast([P, heads, 2, 8])
                    dve.tensor_tensor(hs[:, :, :, o, :], sv[:, :, :, 1 - o, :], tab, ALU.mult).then_inc(dve_done, counted())
                dve.wait_ge(dve_done, steps[0])
                return dve.tensor_tensor(dst, tmp, tmp2[:, 0:heads * ROPE].rearrange("p (h n) -> p h n", h=heads), ALU.add)

            tmp1, tmp2 = xn[:, 0:256], xn[:, 256:512]

            def mla(m):
                l, s, nk = LAYER[m], STREAM[m], nk_of(m)
                for t in TILES[m]:
                    i, _ = tok(m, t)
                    z = zm[:, i, :]
                    dve.tensor_tensor_reduce(tmp1, z[:, 0:Q_LORA], z[:, 0:Q_LORA], 1.0, 0.0, ALU.mult, ALU.add, stat[:, 16:17]).then_inc(dve_done, counted())
                    dve.wait_ge(dve_done, steps[0])
                    zc = z[:, Q_LORA:Q_LORA + KV_LORA]
                    dve.tensor_tensor_reduce(tmp1[:, 0:KV_LORA], zc, zc, 1.0, 0.0, ALU.mult, ALU.add, stat[:, 17:18]).then_inc(dve_done, counted())
                    dve.wait_ge(dve_done, steps[0])
                    rstd(stat[:, 18:20], ("mla", t))
                    dve.tensor_scalar(lat[:, i, 0:Q_LORA], z[:, 0:Q_LORA], stat[:, 18:19], None, ALU.mult).then_inc(dve_done, counted())
                    dve.wait_ge(dve_done, steps[0])
                    if s == 1:
                        rope(krr[:, i:i + 1, :], z[:, Q_LORA + KV_LORA:LAT].unsqueeze(1), i, 1,
                                  tmp1[:, 0:ROPE].unsqueeze(1)).then_inc(dve_done, counted())
                        dve.wait_ge(dve_done, steps[0])
                    dve.scalar_tensor_tensor(out=lat[:, i, Q_LORA:Q_LORA + KV_LORA], in0=zc, scalar=stat[:, 19:20],
                                                 in1=kvn[:, :], op0=ALU.mult, op1=ALU.mult).then_inc(lat_ready, 1)
                    dve.wait_ge(lat_ready, nth("lat", t))
                    yield
                for t in TILES[m]:
                    yield
                for t in TILES[m]:
                    i, _ = tok(m, t)
                    if i:
                        dve.wait_ge(bank_filled[slot("qT", t - 1)], use("qT", t - 1))
                    dve.wait_ge(bank_filled[slot("q", t)], use("q", t))
                    ps = psum[slot("q", t)]
                    dve.tensor_copy(q_tok[:, :], ps[:, 0:HEADS * QK]).then_inc(bank_free[slot("q", t)], 1)
                    dve.wait_ge(bank_free[slot("q", t)], use("q", t) + 1)
                    if s == 1:
                        qr = q_tok[:, :].rearrange("p (h n) -> p h n", h=HEADS)[:, :, HD:QK]
                        rope(qr, qr, i, HEADS, tmp1[:, 0:HEADS * ROPE].rearrange("p (h n) -> p h n", h=HEADS)).then_inc(dve_done, counted())
                        dve.wait_ge(dve_done, steps[0])
                    dve.sem_inc(qtok_ready, 1)
                    yield
                    yield
                yield
                yield
                for t in TILES[m]:
                    for h in range(HEADS):
                        dve.wait_ge(bank_filled[slot("sc", t, h)], use("sc", t, h))
                        ps = psum[slot("sc", t, h)]
                        dve.tensor_reduce(stat[:, h:h + 1], ps[:, 0:P * nk], AX, ALU.max).then_inc(dve_done, counted())
                    dve.wait_ge(dve_done, steps[0])
                    dve.tensor_scalar(stat[:, 4:8], stat[:, 0:4], -SM_SCALE, None, ALU.mult).then_inc(row_max_ready, 1)
                    dve.wait_ge(row_max_ready, nth("row_max", t))
                    yield
                    dve.wait_ge(bank_free[slot("sc", t, HEADS - 1)], use("sc", t, HEADS - 1) + 1)
                    dve.reciprocal(stat[:, 12:16], stat[:, 8:12]).then_inc(dve_done, counted())
                    dve.wait_ge(dve_done, steps[0])
                    dve.tensor_tensor(probs[:, :, 0:P * nk], probs[:, :, 0:P * nk],
                                          stat[:, 12:16].unsqueeze(2).to_broadcast([P, HEADS, P * nk]), ALU.mult).then_inc(probs_ready, 1)
                    dve.wait_ge(probs_ready, nth("probs", t))
                    yield
                    yield
                    yield

            def conv(m):
                T = P * len(TILES[m])
                l = LAYER[m]
                dve.wait_ge(za_ready, nth("za", m))
                dve.wait_ge(bank_filled[slot("rvg", TILES[m][-1])], use("rvg", TILES[m][-1]))
                u, acc = xn[:, 0:T], xn[:, 256:256 + T]
                for f in range(2):
                    def w(tap):
                        k = CONVW + 6 * l + 2 * tap + f
                        return cols[:, k:k + 1]

                    dve.tensor_tensor(u, za[:, 2 + f, 0:T], za[:, 4 + f, 0:T], ALU.mult).then_inc(dve_done, counted())
                    dve.wait_ge(dve_done, steps[0])
                    dve.tensor_scalar(acc, u, w(1), None, ALU.mult).then_inc(dve_done, counted())
                    dve.wait_ge(dve_done, steps[0])
                    dve.scalar_tensor_tensor(out=acc[:, 1:T], in0=u[:, 0:T - 1], scalar=w(0), in1=acc[:, 1:T],
                                                  op0=ALU.mult, op1=ALU.add).then_inc(dve_done, counted())
                    dve.wait_ge(dve_done, steps[0])
                    dve.scalar_tensor_tensor(out=acc[:, 0:T - 1], in0=u[:, 1:T], scalar=w(2), in1=acc[:, 0:T - 1],
                                                  op0=ALU.mult, op1=ALU.add).then_inc(dve_done, counted())
                    dve.wait_ge(dve_done, steps[0])
                    ins = dve.tensor_tensor(yT[:, f, 0:T], acc, za[:, f, 0:T], ALU.mult)
                    if f == 1:
                        ins.then_inc(y_conv_ready, 1)
                        dve.wait_ge(y_conv_ready, nth("y_conv", m))
                    else:
                        ins.then_inc(dve_done, counted())
                        dve.wait_ge(dve_done, steps[0])

            def ret(m):
                l, s, nt = LAYER[m], STREAM[m], len(TILES[m])
                T = P * nt

                def outer(h):
                    key = ("oh", m, h)
                    dve.wait_ge(bank_filled[slot(*key)], use(*key))
                    ps = psum[slot(*key)]
                    for j in range(nt):
                        o = o_tok[:, j, HD * h:HD * h + HD]
                        inner = ps[:, 192 * j:192 * j + HD]
                        if s == 1:
                            b = 192 * j + HD
                            dve.tensor_scalar(o, ps[:, b:b + HD], dcol[:, 0, h, j:j + 1], None, ALU.mult).then_inc(dve_done, counted())
                            dve.wait_ge(dve_done, steps[0])
                            dve.scalar_tensor_tensor(out=o, in0=ps[:, b + HD:b + 2 * HD], scalar=dcol[:, 1, h, j:j + 1],
                                                          in1=o, op0=ALU.mult, op1=ALU.add).then_inc(dve_done, counted())
                            dve.wait_ge(dve_done, steps[0])
                            ins = dve.tensor_tensor(o, inner, o, ALU.add)
                        else:
                            ins = dve.tensor_copy(o, inner)
                        if j == nt - 1:
                            ins.then_inc(bank_free[slot(*key)], 1)
                            dve.wait_ge(bank_free[slot(*key)], use(*key) + 1)
                        else:
                            ins.then_inc(dve_done, counted())
                            dve.wait_ge(dve_done, steps[0])

                if s == 1:
                    dve.wait_ge(state_stored, 16 * (l + 1))
                for h in range(HEADS):
                    for i in range(nt):
                        key = ("inn", m, h, i)
                        dve.wait_ge(bank_filled[slot(*key)], use(*key))
                        ps = psum[slot(*key)]
                        dve.tensor_tensor(inn[:, h % 2, i, 0:T], ps[:, 0:T],
                                                        decay[:, h, P - P * i:P - P * i + T], ALU.mult).then_inc(bank_free[slot(*key)], 1)
                        dve.wait_ge(bank_free[slot(*key)], use(*key) + 1)
                    if h:
                        outer(h - 1)
                    yield
                outer(HEADS - 1)
                yield
                if s == 0:
                    for r in range(2):
                        ins = dve.scalar_tensor_tensor(out=xn[:, 512 + 256 * r:768 + 256 * r].rearrange("p (h n) -> p h n", h=HEADS),
                                                       in0=rk[:, :].rearrange("p (h n) -> p h n", h=HEADS), scalar=K_SCALE,
                                                       in1=dcol[:, r, :, 2:3].to_broadcast([P, HEADS, HD]),
                                                       op0=ALU.mult, op1=ALU.mult)
                        if r == 1:
                            ins.then_inc(k_decayed_ready, 1)
                            dve.wait_ge(k_decayed_ready, nth("k_decayed", m))
                    yield
                    dve.wait_ge(bank_filled[slot("st", m)], use("st", m))
                    yield
                for t in TILES[m]:
                    i, _ = tok(m, t)
                    o = o_tok[:, i, :].rearrange("p (h n) -> p h n", h=HEADS)
                    sq = xn[:, 512:768].rearrange("p (h n) -> p h n", h=HEADS)

                    def per_head(v):
                        return v.unsqueeze(2).to_broadcast([P, HEADS, HD])

                    dve.tensor_reduce(stat[:, 20:24], o, AX, ALU.add).then_inc(dve_done, counted())
                    dve.wait_ge(dve_done, steps[0])
                    dve.tensor_scalar(stat[:, 20:24], stat[:, 20:24], 1.0 / HD, None, ALU.mult).then_inc(dve_done, counted())
                    dve.wait_ge(dve_done, steps[0])
                    dve.tensor_tensor(o, o, per_head(stat[:, 20:24]), ALU.subtract).then_inc(dve_done, counted())
                    dve.wait_ge(dve_done, steps[0])
                    dve.tensor_tensor(sq, o, o, ALU.mult).then_inc(dve_done, counted())
                    dve.wait_ge(dve_done, steps[0])
                    dve.tensor_reduce(stat[:, 24:28], sq, AX, ALU.add).then_inc(dve_done, counted())
                    dve.wait_ge(dve_done, steps[0])
                    rstd(stat[:, 28:32], ("ret", t))
                    dve.tensor_tensor(o, o, per_head(stat[:, 28:32]), ALU.mult).then_inc(dve_done, counted())
                    dve.wait_ge(dve_done, steps[0])
                    dve.tensor_tensor(o_tok[:, i, :], o_tok[:, i, :], rv[:, i, 1, :], ALU.mult).then_inc(ret_out_ready, 1)
                    dve.wait_ge(ret_out_ready, nth("ret_out", t))
                    yield
                    yield

            def out(m):
                yield
                for b in range(2):
                    dve.wait_ge(gate_ready, nth("gate", (1, m, b)))
                    hb = slice(512 * b, 512 * b + 512)
                    for t in TILES[m]:
                        key = ("mix", t, b)
                        dve.wait_ge(bank_filled[slot(*key)], use(*key))
                        ps = psum[slot(*key)]
                        dve.tensor_tensor(xn[:, hb], ps[:, :], gate_row[:, hb], ALU.mult).then_inc(bank_free[slot(*key)], 1)
                        dve.wait_ge(bank_free[slot(*key)], use(*key) + 1)
                        ins = dve.tensor_tensor(x[:, XBUF[t], hb], x[:, XBUF[t], hb], xn[:, hb], ALU.add)
                        if b:
                            ins.then_inc(mixed_ready, 1)
                            dve.wait_ge(mixed_ready, nth("mixed", t))
                        else:
                            ins.then_inc(dve_done, counted())
                            dve.wait_ge(dve_done, steps[0])
                        yield

            def best16(vals, idx, src):
                n = len(src)
                for k in range(n):
                    dve.max(vals[k][:, 0:8], src[k]).then_inc(dve_done, counted())
                dve.wait_ge(dve_done, steps[0])
                yield
                for k in range(n):
                    dve.max_index(idx[k][:, 0:8], vals[k][:, 0:8], src[k]).then_inc(dve_done, counted())
                dve.wait_ge(dve_done, steps[0])
                yield
                for k in range(n):
                    dve.match_replace(src[k], vals[k][:, 0:8], src[k], LOWEST).then_inc(dve_done, counted())
                dve.wait_ge(dve_done, steps[0])
                yield
                for k in range(n):
                    dve.max(vals[k][:, 8:16], src[k]).then_inc(dve_done, counted())
                dve.wait_ge(dve_done, steps[0])
                yield
                for k in range(n):
                    dve.max_index(idx[k][:, 8:16], vals[k][:, 8:16], src[k]).then_inc(dve_done, counted())
                dve.wait_ge(dve_done, steps[0])
                yield

            def topk(t):
                l = LAYER[M_OF[t]]
                for b in range(4):
                    dve.wait_ge(scores_ready, nth("scores", (t, b)))
                yield from best16([tv[:, k, :] for k in range(16)], [ti[:, k, :] for k in range(16)],
                       [s_sb[:, N_KEYS * k:N_KEYS * k + N_KEYS] for k in range(16)])
                tvh = tv[:, :, :].rearrange("p (q h) k -> p h q k", q=2)
                dve.tensor_tensor(cand.rearrange("p (h i j) -> p h i j", h=PEER_H, i=TOPK),
                                       tvh[:, :, 0, :].unsqueeze(3).to_broadcast([P, PEER_H, TOPK, TOPK]),
                                       tvh[:, :, 1, :].unsqueeze(2).to_broadcast([P, PEER_H, TOPK, TOPK]), ALU.add).then_inc(dve_done, counted())
                dve.wait_ge(dve_done, steps[0])
                yield
                yield from best16([cv[:, h, :] for h in range(PEER_H)], [sel[:, h, :] for h in range(PEER_H)],
                       [cand[:, 256 * h:256 * h + 256] for h in range(PEER_H)])
                dve.tensor_copy(stat[:, 32:40], cv[:, :, 0]).then_inc(dve_done, counted())
                dve.wait_ge(dve_done, steps[0])
                dve.tensor_tensor(cv[:, :, :], cv[:, :, :], stat[:, 32:40].unsqueeze(2).to_broadcast([P, PEER_H, TOPK]),
                                      ALU.subtract).then_inc(gate_arg_ready, 1)
                dve.wait_ge(gate_arg_ready, nth("gate_arg", t))
                dve.tensor_copy(tif[:, :, :], ti[:, :, :]).then_inc(dve_done, counted())
                sf = sel[:, :, :].rearrange("p h k -> p (h k)")
                dve.tensor_scalar(sel2[:, 0, :], sf, 4, None, ALU.logical_shift_right).then_inc(dve_done, counted())
                dve.tensor_scalar(sel2[:, 1, :], sf, 15, None, ALU.bitwise_and).then_inc(dve_done, counted())
                dve.wait_ge(dve_done, steps[0])
                dve.tensor_copy(self_[:, :, :], sel2[:, :, :]).then_inc(dve_done, counted())
                dve.wait_ge(dve_done, steps[0])
                yield
                tih = tif[:, :, :].rearrange("p (q h) k -> p h q k", q=2)
                hot = s_sb.rearrange("p (n j) -> p n j", j=TOPK)
                hot4 = s_sb.rearrange("p (h k j) -> p h k j", h=PEER_H, k=TOPK)
                for q in range(2):
                    dve.tensor_tensor(hot, self_[:, q, :].unsqueeze(2).to_broadcast([P, PICKS, TOPK]),
                                           iota16[:, :].unsqueeze(1).to_broadcast([P, PICKS, TOPK]), ALU.is_equal).then_inc(dve_done, counted())
                    dve.wait_ge(dve_done, steps[0])
                    dve.tensor_tensor(hot4, hot4, tih[:, :, q, :].unsqueeze(2).to_broadcast([P, PEER_H, TOPK, TOPK]), ALU.mult).then_inc(dve_done, counted())
                    dve.wait_ge(dve_done, steps[0])
                    dve.tensor_reduce(e12[:, q, :], hot, AX, ALU.add).then_inc(dve_done, counted())
                    dve.wait_ge(dve_done, steps[0])
                    yield
                dve.tensor_scalar(e12[:, 0, :], e12[:, 0, :], float(N_KEYS), float(l * EXPERTS), ALU.mult, ALU.add).then_inc(dve_done, counted())
                dve.wait_ge(dve_done, steps[0])
                dve.tensor_tensor(eidx[:, t % 2, :], e12[:, 0, :], e12[:, 1, :], ALU.add).then_inc(dve_done, counted())
                dve.wait_ge(dve_done, steps[0])
                dve.wait_ge(gate_exp_ready, nth("gate_exp", t))
                dve.tensor_reduce(stat[:, 40:48], cv[:, :, :], AX, ALU.add).then_inc(dve_done, counted())
                dve.wait_ge(dve_done, steps[0])
                dve.reciprocal(stat[:, 40:48], stat[:, 40:48]).then_inc(dve_done, counted())
                dve.wait_ge(dve_done, steps[0])
                dve.tensor_tensor(gates[:, t % 2, :].rearrange("p (h k) -> p h k", h=PEER_H), cv[:, :, :],
                                      stat[:, 40:48].unsqueeze(2).to_broadcast([P, PEER_H, TOPK]), ALU.mult).then_inc(picked_ready, 1)
                dve.wait_ge(picked_ready, nth("picked", t))
                yield

            def finish(t):
                dve.wait_ge(v_free, SLOTS + PICKS * (t + 1))
                if t >= 4:
                    dve.wait_ge(y_stored, 16 * (t - 3))
                for b in range(2):
                    dve.wait_ge(gate_ready, nth("gate", (2, t, b)))
                    hb = slice(512 * b, 512 * b + 512)
                    dve.tensor_tensor(xn[:, hb], ysum[:, b, :], gate_row[:, hb], ALU.mult).then_inc(dve_done, counted())
                    dve.wait_ge(dve_done, steps[0])
                    ins = dve.tensor_tensor(x[:, XBUF[t], hb], x[:, XBUF[t], hb], xn[:, hb], ALU.add)
                    if b:
                        ins.then_inc(updated_ready, 1)
                        dve.wait_ge(updated_ready, nth("updated", t))
                    else:
                        ins.then_inc(dve_done, counted())
                        dve.wait_ge(dve_done, steps[0])
                yield
                if t >= 3:
                    xt = x[:, XBUF[t], :]
                    dve.tensor_tensor_reduce(xn[:, :], xt, xt, 1.0, 0.0, ALU.mult, ALU.add, stat[:, 0:1]).then_inc(dve_done, counted())
                    dve.wait_ge(dve_done, steps[0])
                    rstd(stat[:, 1:2], ("final", t))
                    dve.scalar_tensor_tensor(out=xn[:, :], in0=xt, scalar=stat[:, 1:2], in1=normf[:, :],
                                                 op0=ALU.mult, op1=ALU.mult).then_inc(final_ready, 1)
                    dve.wait_ge(final_ready, nth("final", t))
                    yield

            def groups(t, lo, hi):
                def group(i, gate_cols):
                    for r in range(G):
                        dve.wait_ge(u_landed[r], i * 16 + 16 * (NG * t + 1))
                        dve.tensor_tensor_reduce(ubuf[:, r, :], ubuf[:, r, :], h2[:, XBUF[t], :], 1.0, 0.0, ALU.mult, ALU.add,
                                                 dot[:, r:r + 1]).then_inc(u_free, 1)
                    dve.wait_ge(gelu_done, i + (NG * t + 1))
                    dve.tensor_tensor(coef[:, :], act_dot[:, :], gates[:, t % 2, gate_cols], ALU.mult).then_inc(coef_done, 1)

                if lo == 0:
                    if t == 0:
                        dve.sem_inc(u_free, SLOTS)
                    for b in range(2):
                        dve.wait_ge(h2_ready, nth("h2", (t, b)))
                if hi - lo > 1:
                    with dve.Fori(lo, hi) as i:
                        group(i, bass.ts(i, G))
                else:
                    group(lo, slice(G * lo, G * lo + G))

            running = {}
            for stage, i, *more in ORDER:
                if stage == "groups":
                    groups(i, *more)
                    continue
                kind, *n = stage
                if kind == "start":
                    beat_of(i, stage, running, start, *n)
                elif kind == "modcol":
                    beat_of(i, stage, running, modcol, *n)
                elif kind == "modscale":
                    beat_of(i, stage, running, modscale, *n)
                elif kind == "decay":
                    beat_of(i, stage, running, decay_, *n)
                elif kind == "ln":
                    beat_of(i, stage, running, ln, *n)
                elif kind == "in":
                    beat_of(i, stage, running, project, *n)
                elif kind == "mla":
                    beat_of(i, stage, running, mla, *n)
                elif kind == "conv":
                    beat_of(i, stage, running, conv, *n)
                elif kind == "ret":
                    beat_of(i, stage, running, ret, *n)
                elif kind == "out":
                    beat_of(i, stage, running, out, *n)
                elif kind == "topk":
                    beat_of(i, stage, running, topk, *n)
                elif kind == "finish":
                    beat_of(i, stage, running, finish, *n)

        @block.gpsimd
        def _(pool):
            def peer(t):
                pool.wait_ge(picked_ready, nth("picked", t))
                picks = eidx[:, t % 2, :]

                def stage_idx(idx, g, n):
                    pool.tensor_copy(idx, picks[:, bass.ts(g, G)]).then_inc(idx_staged, 1)
                    pool.wait_ge(idx_staged, n)
                    pool.sem_inc(pool_order, 1)

                def gather(rows, buf, idx, landed, free, k, r):
                    pool.wait_ge(free, k)
                    pool.sem_inc(pool_order, 1)
                    pool.indirect_dma_start(buf[:, r, :], None, rows, bass.IndirectOffsetOnAxis(idx[:, r:r + 1], 0))\
                        .then_inc(landed[r], 16)

                K = PICKS * t
                N = 2 * NG * t

                def u_group(g, q):
                    for r in range(G):
                        gather(u_rows, ubuf, uidx[:, q, :], u_landed, u_free, g * G + (K + r + 1), r)

                def both(g, q):
                    stage_idx(uidx[:, q, :], g, g * 2 + N)
                    stage_idx(vidx[:, 1 - q, :], g - 1, g * 2 + (N + 1))
                    for r in range(G):
                        gather(u_rows, ubuf, uidx[:, q, :], u_landed, u_free, g * G + (K + r + 1), r)
                        gather(v_rows, vbuf, vidx[:, 1 - q, :], v_landed, v_free, g * G + (K - G + r + 1), r)

                stage_idx(uidx[:, 0, :], 0, N + 1)
                u_group(0, 0)
                with pool.Fori(0, NG // 2 - 1) as i:
                    both(i * 2 + 1, 1)
                    both(i * 2 + 2, 0)
                both(NG - 1, 1)
                stage_idx(vidx[:, 1, :], NG - 1, N + 2 * NG)
                for r in range(G):
                    gather(v_rows, vbuf, vidx[:, 1, :], v_landed, v_free, K + PICKS - G + r + 1, r)

            for t in range(len(M_OF)):
                peer(t)



def shape_constants():
    f = np.float32
    u = np.arange(3 * P)[None, :] - P - np.arange(P)[:, None]
    rel = np.stack([np.maximum(u, 0), np.maximum(-u, 0)], 1).astype(f)
    p = np.arange(P)
    fwd = np.stack([p + 1, p + P + 1, P - 1 - p], 1)
    bwd = np.stack([DEC - p, DEC - P - p, p], 1)
    pos3 = np.stack([fwd, bwd], 1).astype(f)
    pairs = ROPE // 4
    inv = (np.float32(10000.0) ** (-np.arange(pairs, dtype=f) / pairs)).astype(f)
    t = np.arange(DEC)
    ar = (t // GRID_W).astype(f)[:, None] * inv
    ac = (t % GRID_W).astype(f)[:, None] * inv
    ang = np.concatenate([ar, ar, ac, ac], -1)
    sign = np.repeat(np.array([-1, 1, -1, 1], f), pairs)
    rope = np.stack([np.cos(ang), np.sin(ang) * sign], 1).astype(f)
    rope = rope.reshape(2, P, 2, ROPE).transpose(1, 0, 2, 3)

    def window(L):
        out = np.zeros((L, 4, L), f)
        q = np.arange(L)
        for g, w in enumerate(WINDOWS):
            lo, hi = np.clip(q - w // 2, 0, L), np.clip(q + w // 2, 0, L)
            k = np.arange(L)[:, None]
            out[:, g, :] = ((k >= lo) & (k < hi)) / (hi - lo).astype(f) - (k == q)
        return out

    ws = window(DEC)
    band = np.stack([window(SEQ), ws[0:P, :, 0:P], ws[P:, :, P:]], 1)
    edge = np.stack([ws[P:, :, P - 8:P], ws[0:P, :, P:P + 8]], 1)
    return {"ident": np.eye(P, dtype=f), "iota16": np.arange(TOPK, dtype=f), "rel": rel, "pos3": pos3,
            "rope": np.ascontiguousarray(rope), "band": band, "edge": edge}


_OUTS = [((1, SEQ, D), "float32"), ((1, DEC, D), "float32"), ((1, DEPTH, SEQ, KV_LORA), "float32"),
         ((1, DEPTH, SEQ, ROPE), "float32"), ((1, DEPTH, 2, HEADS, HD, HD), "float32")]
_INS = ["x_prompt", "x_sample", "cache_mla_ckv", "cache_mla_krope", "state_ret", "c", "c_ctx", "w_mod", "b_mod", "norm1",
        "norm2", "w_in", "conv_w", "mla_q_norm", "mla_w_uq", "mla_kv_norm", "mla_w_uk", "mla_w_uv", "ret_decay_logit",
        "pool_w", "pool_scale", "w_out", "peer_w_q", "peer_subkeys", "peer_u", "peer_v", "norm_f"]


def kernel(**inputs):
    import concourse.bacc as _bacc
    from concourse.bass_utils import run_bass_kernel_spmd as _run

    nc = _bacc.Bacc("TRN2", target_bir_lowering=False, num_devices=1)
    arrays = {}

    def declare(prefix, named):
        aps = {}
        for name, v in named.items():
            v = np.ascontiguousarray(v)
            arrays[f"{prefix}_{name}_dram"] = v
            aps[name] = nc.dram_tensor(f"{prefix}_{name}_dram", v.shape, mybir.dt.from_np(v.dtype), kind="ExternalInput").ap()
        return aps

    ins = declare("in", {name: inputs[name] for name in _INS})
    consts = declare("shape", shape_constants())
    outs = [nc.dram_tensor(f"out_{i}_dram", shape, mybir.dt.from_np(np.dtype(dt)), kind="ExternalOutput").ap()
            for i, (shape, dt) in enumerate(_OUTS)]
    hybrid_step(nc, ins, consts, outs)
    r = _run(nc, [arrays], core_ids=[0])
    return tuple(r.results[0][f"out_{i}_dram"] for i in range(len(_OUTS)))
```
